# Optimizing a Trainium2 kernel written in Bass

```python
import jax, jax.numpy as jnp
from jax import lax
import numpy as np

D_MODEL = 1024
BATCH = 1
SEQ = 128
DEPTH = 2
DEC_BATCH = 1
DEC_SEQ = 512
PAST_LEN = 128

GRID_W = 64
HEAD_DIM = 64
NA_HEADS = 4
NA_WIN_ROWS = 8
NA_WIN_COLS = 16
NA_QCOLS = 16
NA_KCOLS = 32
POOL_GROUPS = 4
POOL_GW = 64
POOL_WINDOWS = (2, 4, 8, 16)
MLA_HEADS = 4
MLA_Q_RANK = 256
MLA_KV_RANK = 128
MLA_NOPE = 64
MLA_ROPE = 32
MLA_V = 64
SWA_HEADS = 4
SWA_KV_HEADS = 2
SWA_WINDOW = 128
SWA_BLOCK = 128
D_FF = 4 * D_MODEL
Q_BLOCK = 128
ROPE_THETA = 10000.0
EPS = 1e-6
NEG = -1e30
IN_SIZES = (NA_HEADS * HEAD_DIM, NA_HEADS * HEAD_DIM, NA_HEADS * HEAD_DIM,
            POOL_GROUPS * POOL_GW,
            MLA_Q_RANK, MLA_KV_RANK, MLA_ROPE,
            SWA_HEADS * HEAD_DIM, SWA_KV_HEADS * HEAD_DIM, SWA_KV_HEADS * HEAD_DIM)
IN_COLS = sum(IN_SIZES)
MIX_WIDTH = NA_HEADS * HEAD_DIM + POOL_GROUPS * POOL_GW + MLA_HEADS * MLA_V + SWA_HEADS * HEAD_DIM

kernel_name = 'hybrid_dit_parallel_heads_step'

def rms_norm(x, g):
    xf = x.astype(jnp.float32)
    xf = xf * lax.rsqrt(jnp.mean(xf * xf, axis=-1, keepdims=True) + EPS)
    return (xf * g.astype(jnp.float32)).astype(x.dtype)

def adaln(cond, w, b):
    return jnp.split(jax.nn.silu(cond) @ w + b, 6, axis=-1)

def axial_rope(x, rows, cols):
    half = x.shape[-1] // 2
    quarter = half // 2
    freqs = ROPE_THETA ** (-jnp.arange(quarter, dtype=jnp.float32) / quarter)

    def rotate(xa, pos):
        ang = pos.astype(jnp.float32)[:, None] * freqs
        cos = jnp.cos(ang)[:, None, :]
        sin = jnp.sin(ang)[:, None, :]
        x1, x2 = xa[..., :quarter], xa[..., quarter:]
        return jnp.concatenate([x1 * cos - x2 * sin, x1 * sin + x2 * cos], axis=-1)

    xf = x.astype(jnp.float32)
    out = jnp.concatenate([rotate(xf[..., :half], rows), rotate(xf[..., half:], cols)], axis=-1)
    return out.astype(x.dtype)

def rope_tail(x, start, rows, cols):
    return jnp.concatenate([x[..., :start], axial_rope(x[..., start:], rows, cols)], axis=-1)

def dense_attention(q, k, v, sink=None):
    b, nq, h, dk = q.shape
    scale = dk ** -0.5
    qb = q.reshape(b, nq // Q_BLOCK, Q_BLOCK, h, dk).swapaxes(0, 1)

    def block(qi):
        s = jnp.einsum('bqhd,bkhd->bhqk', qi, k).astype(jnp.float32) * scale
        if sink is not None:
            s_sink = jnp.broadcast_to(sink.astype(jnp.float32)[None, :, None, None], s.shape[:-1] + (1,))
            p = jax.nn.softmax(jnp.concatenate([s, s_sink], axis=-1), axis=-1)[..., :-1]
        else:
            p = jax.nn.softmax(s, axis=-1)
        return jnp.einsum('bhqk,bkhd->bqhd', p.astype(v.dtype), v)

    out = lax.map(block, qb)
    return out.swapaxes(0, 1).reshape(b, nq, h, v.shape[-1])

def neighbourhood_attention(q, k, v, ctx_k, ctx_v, rpb):
    b, n, h, d = q.shape
    rows = n // GRID_W
    wr = min(NA_WIN_ROWS, rows)
    ncb = GRID_W // NA_QCOLS
    qr = jnp.arange(rows)
    key_rows = jnp.clip(qr - wr // 2, 0, rows - wr)[:, None] + jnp.arange(wr)[None, :]
    qcol = jnp.arange(GRID_W).reshape(ncb, NA_QCOLS)
    col_start = jnp.clip(qcol - NA_WIN_COLS // 2, 0, GRID_W - NA_WIN_COLS)
    key_cols = jnp.clip(col_start[:, :1], 0, GRID_W - NA_KCOLS) + jnp.arange(NA_KCOLS)[None, :]
    nk = wr * NA_KCOLS

    def gather(x):
        xg = x.reshape(b, rows, GRID_W, h, d)
        blk = xg[:, key_rows[:, None, :, None], key_cols[None, :, None, :]]
        return blk.reshape(b, rows, ncb, nk, h, d)

    kb, vb = gather(k), gather(v)
    qg = q.reshape(b, rows, ncb, NA_QCOLS, h, d)
    inside = (key_cols[:, None, :] >= col_start[:, :, None]) & (key_cols[:, None, :] < col_start[:, :, None] + NA_WIN_COLS)
    mask = jnp.broadcast_to(inside[:, :, None, :], (ncb, NA_QCOLS, wr, NA_KCOLS)).reshape(ncb, NA_QCOLS, nk)
    dr = key_rows - qr[:, None] + NA_WIN_ROWS - 1
    dc = jnp.clip(key_cols[:, None, :] - qcol[:, :, None] + NA_WIN_COLS - 1, 0, 2 * NA_WIN_COLS - 2)
    bias = rpb[:, dr[:, None, None, :, None], dc[None, :, :, None, :]]
    bias = bias.transpose(1, 2, 0, 3, 4, 5).reshape(rows, ncb, h, NA_QCOLS, nk).astype(jnp.float32)
    scale = d ** -0.5
    s_loc = jnp.einsum('brcqhd,brckhd->brchqk', qg, kb).astype(jnp.float32) * scale + bias
    s_loc = jnp.where(mask[None, None, :, None, :, :], s_loc, NEG)
    s_ctx = jnp.einsum('brcqhd,blhd->brchql', qg, ctx_k).astype(jnp.float32) * scale
    p = jax.nn.softmax(jnp.concatenate([s_loc, s_ctx], axis=-1), axis=-1).astype(v.dtype)
    out = (jnp.einsum('brchqk,brckhd->brcqhd', p[..., :nk], vb)
           + jnp.einsum('brchql,blhd->brcqhd', p[..., nk:], ctx_v))
    return out.reshape(b, n, h, d)

def window_attention(q, k, v, ctx_k, ctx_v, sink):
    b, n, hq, d = q.shape
    nb = n // SWA_BLOCK
    g = hq // SWA_KV_HEADS
    qb = q.reshape(b, nb, SWA_BLOCK, SWA_KV_HEADS, g, d)

    def band(x):
        xp = jnp.pad(x, ((0, 0), (SWA_BLOCK, SWA_BLOCK), (0, 0), (0, 0)))
        xp = xp.reshape(b, nb + 2, SWA_BLOCK, SWA_KV_HEADS, d)
        return jnp.concatenate([xp[:, :nb], xp[:, 1:nb + 1], xp[:, 2:]], axis=2)

    kb, vb = band(k), band(v)
    kl = 3 * SWA_BLOCK
    qpos = jnp.arange(n).reshape(nb, SWA_BLOCK)
    kpos = (jnp.arange(nb)[:, None] - 1) * SWA_BLOCK + jnp.arange(kl)[None, :]
    valid = ((kpos[:, None, :] >= 0) & (kpos[:, None, :] < n)
             & (jnp.abs(kpos[:, None, :] - qpos[:, :, None]) <= SWA_WINDOW))
    scale = d ** -0.5
    s_loc = jnp.einsum('bnqhgd,bnjhd->bnhgqj', qb, kb).astype(jnp.float32) * scale
    s_loc = jnp.where(valid[None, :, None, None, :, :], s_loc, NEG)
    s_ctx = jnp.einsum('bnqhgd,blhd->bnhgql', qb, ctx_k).astype(jnp.float32) * scale
    s_sink = jnp.broadcast_to(sink.astype(jnp.float32).reshape(SWA_KV_HEADS, g)[None, None, :, :, None, None],
                              s_loc.shape[:-1] + (1,))
    p = jax.nn.softmax(jnp.concatenate([s_loc, s_ctx, s_sink], axis=-1), axis=-1).astype(v.dtype)
    out = (jnp.einsum('bnhgqj,bnjhd->bnqhgd', p[..., :kl], vb)
           + jnp.einsum('bnhgql,blhd->bnqhgd', p[..., kl:-1], ctx_v))
    return out.reshape(b, n, hq, d)

def multiscale_pool(x, w_pool, scale):
    b, n, _ = x.shape
    xf = x.astype(jnp.float32)
    t = jnp.arange(n)
    outs = []
    for gi, w in enumerate(POOL_WINDOWS):
        xg = xf[..., gi * POOL_GW:(gi + 1) * POOL_GW]
        cs = jnp.pad(jnp.cumsum(xg, axis=1), ((0, 0), (1, 0), (0, 0)))
        lo = jnp.clip(t - w // 2, 0, n)
        hi = jnp.clip(t - w // 2 + w, 0, n)
        mean = (cs[:, hi] - cs[:, lo]) / (hi - lo).astype(jnp.float32)[None, :, None]
        outs.append(mean - xg)
    pooled = jnp.stack(outs, axis=2).astype(x.dtype)
    y = jnp.einsum('bngc,gce->bnge', pooled, w_pool).reshape(b, n, POOL_GROUPS * POOL_GW)
    return y * scale

def project_mixers(h, p):
    b, n, _ = h.shape
    offs = np.cumsum(IN_SIZES)[:-1].tolist()
    (na_q, na_k, na_v, pool_in, mla_cq, mla_ckv, mla_kpe,
     swa_q, swa_k, swa_v) = jnp.split(h @ p['w_in'], offs, axis=-1)
    heads = lambda z, nh: z.reshape(b, n, nh, -1)
    na = (rms_norm(heads(na_q, NA_HEADS), p['na_q_norm']),
          rms_norm(heads(na_k, NA_HEADS), p['na_k_norm']),
          heads(na_v, NA_HEADS))
    mla_q = rms_norm(heads(rms_norm(mla_cq, p['mla_q_a_norm']) @ p['mla_w_uq'], MLA_HEADS), p['mla_q_norm'])
    ckv = rms_norm(mla_ckv, p['mla_kv_norm'])
    swa = (rms_norm(heads(swa_q, SWA_HEADS), p['swa_q_norm']),
           rms_norm(heads(swa_k, SWA_KV_HEADS), p['swa_k_norm']),
           heads(swa_v, SWA_KV_HEADS))
    return na, pool_in, mla_q, ckv, mla_kpe, swa

def mla_expand_kv(ckv, kpe, p):
    b, n, _ = ckv.shape
    kv = (ckv @ p['mla_w_ukv']).reshape(b, n, MLA_HEADS, MLA_NOPE + MLA_V)
    k_pe = jnp.broadcast_to(kpe[:, :, None, :], (b, n, MLA_HEADS, MLA_ROPE))
    k = rms_norm(jnp.concatenate([kv[..., :MLA_NOPE], k_pe], axis=-1), p['mla_k_norm'])
    return k, kv[..., MLA_NOPE:]

def channel_mlp(x, shift, scale, gate, p):
    h = rms_norm(x, p['norm2']) * (1 + scale) + shift
    z = jax.nn.relu(h @ p['mlp_w1'])
    return x + gate * ((z * z) @ p['mlp_w2'])

def context_layer(x, mod, p):
    sh1, sc1, g1, sh2, sc2, g2 = mod
    h = rms_norm(x, p['norm1']) * (1 + sc1) + sh1
    b, n, _ = h.shape
    (na_q, na_k, na_v), pool_in, mla_q, ckv, kpe, (sq, sk, sv) = project_mixers(h, p)
    o_na = dense_attention(na_q, na_k, na_v)
    o_pool = multiscale_pool(pool_in, p['pool_w'], p['pool_scale'])
    mk, mv = mla_expand_kv(ckv, kpe, p)
    o_mla = dense_attention(mla_q, mk, mv)
    rep = SWA_HEADS // SWA_KV_HEADS
    o_swa = dense_attention(sq, jnp.repeat(sk, rep, axis=2), jnp.repeat(sv, rep, axis=2), sink=p['swa_sink'])
    mixed = jnp.concatenate([o_na.reshape(b, n, -1), o_pool, o_mla.reshape(b, n, -1), o_swa.reshape(b, n, -1)], axis=-1)
    x = x + g1 * (mixed @ p['w_out'])
    return channel_mlp(x, sh2, sc2, g2, p), (na_k, na_v, ckv, kpe, sk, sv)

def latent_layer(x, mod, cache, rows, cols, p):
    sh1, sc1, g1, sh2, sc2, g2 = mod
    c_na_k, c_na_v, c_ckv, c_kpe, c_swa_k, c_swa_v = cache
    h = rms_norm(x, p['norm1']) * (1 + sc1) + sh1
    b, n, _ = h.shape
    (na_q, na_k, na_v), pool_in, mla_q, ckv, kpe, (sq, sk, sv) = project_mixers(h, p)
    o_na = neighbourhood_attention(na_q, na_k, na_v, c_na_k, c_na_v, p['na_rpb'])
    o_pool = multiscale_pool(pool_in, p['pool_w'], p['pool_scale'])
    mk, mv = mla_expand_kv(ckv, kpe, p)
    ck, cv = mla_expand_kv(c_ckv, c_kpe, p)
    q = rope_tail(mla_q, MLA_NOPE, rows, cols)
    mk = rope_tail(mk, MLA_NOPE, rows, cols)
    o_mla = dense_attention(q, jnp.concatenate([mk, ck], axis=1), jnp.concatenate([mv, cv], axis=1))
    o_swa = window_attention(axial_rope(sq, rows, cols), axial_rope(sk, rows, cols), sv, c_swa_k, c_swa_v, p['swa_sink'])
    mixed = jnp.concatenate([o_na.reshape(b, n, -1), o_pool, o_mla.reshape(b, n, -1), o_swa.reshape(b, n, -1)], axis=-1)
    x = x + g1 * (mixed @ p['w_out'])
    return channel_mlp(x, sh2, sc2, g2, p)

def setup_inputs(seed: int = 0) -> dict:
    key = jax.random.key(seed)
    keys = jax.random.split(key, 40)
    ki = iter(range(40))

    def normal(shape, scale):
        return jax.random.normal(keys[next(ki)], shape, jnp.float32) * scale

    def gain(shape):
        return 1.0 + normal(shape, 0.05)

    d = D_MODEL
    return {
        'x_prompt': normal((BATCH, SEQ, d), 1.0),
        'x_sample': normal((DEC_BATCH, DEC_SEQ, d), 1.0),
        'cache_na_k': normal((DEC_BATCH, DEPTH, PAST_LEN, NA_HEADS, HEAD_DIM), 1.0),
        'cache_na_v': normal((DEC_BATCH, DEPTH, PAST_LEN, NA_HEADS, HEAD_DIM), 1.0),
        'cache_mla_ckv': normal((DEC_BATCH, DEPTH, PAST_LEN, MLA_KV_RANK), 1.0),
        'cache_mla_kpe': normal((DEC_BATCH, DEPTH, PAST_LEN, MLA_ROPE), 1.0),
        'cache_swa_k': normal((DEC_BATCH, DEPTH, PAST_LEN, SWA_KV_HEADS, HEAD_DIM), 1.0),
        'cache_swa_v': normal((DEC_BATCH, DEPTH, PAST_LEN, SWA_KV_HEADS, HEAD_DIM), 1.0),
        'c': normal((DEC_BATCH, d), 1.0),
        'c_ctx': normal((d,), 1.0),
        'norm1': gain((DEPTH, d)),
        'norm2': gain((DEPTH, d)),
        'w_ada': normal((DEPTH, d, 6 * d), 0.5 * d ** -0.5),
        'b_ada': normal((DEPTH, 6 * d), 0.02),
        'w_in': normal((DEPTH, d, IN_COLS), d ** -0.5),
        'w_out': normal((DEPTH, MIX_WIDTH, d), MIX_WIDTH ** -0.5),
        'na_q_norm': gain((DEPTH, HEAD_DIM)),
        'na_k_norm': gain((DEPTH, HEAD_DIM)),
        'na_rpb': normal((DEPTH, NA_HEADS, 2 * NA_WIN_ROWS - 1, 2 * NA_WIN_COLS - 1), 0.5),
        'pool_w': normal((DEPTH, POOL_GROUPS, POOL_GW, POOL_GW), POOL_GW ** -0.5),
        'pool_scale': gain((DEPTH, POOL_GROUPS * POOL_GW)),
        'mla_q_a_norm': gain((DEPTH, MLA_Q_RANK)),
        'mla_w_uq': normal((DEPTH, MLA_Q_RANK, MLA_HEADS * (MLA_NOPE + MLA_ROPE)), MLA_Q_RANK ** -0.5),
        'mla_kv_norm': gain((DEPTH, MLA_KV_RANK)),
        'mla_w_ukv': normal((DEPTH, MLA_KV_RANK, MLA_HEADS * (MLA_NOPE + MLA_V)), MLA_KV_RANK ** -0.5),
        'mla_q_norm': gain((DEPTH, MLA_NOPE + MLA_ROPE)),
        'mla_k_norm': gain((DEPTH, MLA_NOPE + MLA_ROPE)),
        'swa_q_norm': gain((DEPTH, HEAD_DIM)),
        'swa_k_norm': gain((DEPTH, HEAD_DIM)),
        'swa_sink': normal((DEPTH, SWA_HEADS), 1.0),
        'mlp_w1': normal((DEPTH, d, D_FF), d ** -0.5),
        'mlp_w2': normal((DEPTH, D_FF, d), D_FF ** -0.5),
    }

def reference(x_prompt, x_sample, cache_na_k, cache_na_v, cache_mla_ckv, cache_mla_kpe, cache_swa_k, cache_swa_v,
              c, c_ctx, norm1, norm2, w_ada, b_ada, w_in, w_out, na_q_norm, na_k_norm, na_rpb, pool_w, pool_scale,
              mla_q_a_norm, mla_w_uq, mla_kv_norm, mla_w_ukv, mla_q_norm, mla_k_norm, swa_q_norm, swa_k_norm,
              swa_sink, mlp_w1, mlp_w2):
    n_lat = x_sample.shape[1]
    t = jnp.arange(n_lat, dtype=jnp.int32)
    rows, cols = t // GRID_W, t % GRID_W
    xp, xs = x_prompt, x_sample
    st_na_k, st_na_v, st_ckv, st_kpe, st_swa_k, st_swa_v = [], [], [], [], [], []
    for l in range(DEPTH):
        p = {
            'norm1': norm1[l], 'norm2': norm2[l], 'w_in': w_in[l], 'w_out': w_out[l],
            'na_q_norm': na_q_norm[l], 'na_k_norm': na_k_norm[l], 'na_rpb': na_rpb[l],
            'pool_w': pool_w[l], 'pool_scale': pool_scale[l],
            'mla_q_a_norm': mla_q_a_norm[l], 'mla_w_uq': mla_w_uq[l], 'mla_kv_norm': mla_kv_norm[l],
            'mla_w_ukv': mla_w_ukv[l], 'mla_q_norm': mla_q_norm[l], 'mla_k_norm': mla_k_norm[l],
            'swa_q_norm': swa_q_norm[l], 'swa_k_norm': swa_k_norm[l], 'swa_sink': swa_sink[l],
            'mlp_w1': mlp_w1[l], 'mlp_w2': mlp_w2[l],
        }
        mod_ctx = adaln(c_ctx, w_ada[l], b_ada[l])
        xp, (k_na, v_na, ckv, kpe, k_swa, v_swa) = context_layer(xp, mod_ctx, p)
        st_na_k.append(k_na)
        st_na_v.append(v_na)
        st_ckv.append(ckv)
        st_kpe.append(kpe)
        st_swa_k.append(k_swa)
        st_swa_v.append(v_swa)
        mod_lat = adaln(c[:, None, :], w_ada[l], b_ada[l])
        cache_l = (cache_na_k[:, l], cache_na_v[:, l], cache_mla_ckv[:, l], cache_mla_kpe[:, l],
                   cache_swa_k[:, l], cache_swa_v[:, l])
        xs = latent_layer(xs, mod_lat, cache_l, rows, cols, p)
    na_k_new = jnp.stack(st_na_k, axis=1)
    na_v_new = jnp.stack(st_na_v, axis=1)
    mla_ckv_new = jnp.stack(st_ckv, axis=1)
    mla_kpe_new = jnp.stack(st_kpe, axis=1)
    swa_k_new = jnp.stack(st_swa_k, axis=1)
    swa_v_new = jnp.stack(st_swa_v, axis=1)
    return (xp, xs, na_k_new, na_v_new, mla_ckv_new, mla_kpe_new, swa_k_new, swa_v_new)


_drawn_inputs = setup_inputs


def setup_inputs(seed=0):
    import zlib

    import numpy as np

    out = dict(_drawn_inputs(seed))
    spreads = {}
    factors = {'cache_na_k': 5.052,
     'cache_na_v': 4.02,
     'cache_mla_ckv': 8.0,
     'cache_mla_kpe': 8.0,
     'cache_swa_k': 6.552,
     'cache_swa_v': 5.232,
     'na_q_norm': 8.0,
     'na_rpb': 7.365,
     'pool_scale': 6.432,
     'mla_q_a_norm': 8.0,
     'mla_q_norm': 8.0,
     'mla_k_norm': 8.0,
     'swa_q_norm': 8.0,
     'swa_sink': 64.0}
    for name, (base, spread) in spreads.items():
        noise = np.random.default_rng([zlib.crc32(name.encode()), seed]).standard_normal(out[name].shape)
        drawn = base * np.exp(spread * noise) if base else spread * noise
        out[name] = __import__('jax').numpy.asarray(drawn.astype(out[name].dtype))
    for name, factor in factors.items():
        out[name] = (out[name] * factor).astype(out[name].dtype)
    return out
```

```python
from contextlib import ExitStack

import numpy as np

import concourse.bass as bass
from concourse import mybir

ALU = mybir.AluOpType
ACT = mybir.ActivationFunctionType
AX_X = mybir.AxisListType.X
F32 = mybir.dt.float32
F32R = mybir.dt.float32r

P = 128
D = 1024
KC = D // P
DEPTH = 2
CTX, LAT, PAST = 128, 512, 128
NTOK = CTX + LAT
NT = NTOK // P
HALF = NTOK // 2
GRID_W = 64
ROWS = LAT // GRID_W
HD = 64
D_FF = 4 * D
EPS = 1e-6
NEG = -1e30
THETA = 10000.0
POOL_WINDOWS = (2, 4, 8, 16)
PAD = 8
SEG = CTX + LAT + 4 * PAD
KV_RANK, Q_RANK, NOPE, ROPE, DV = 128, 256, 64, 32, 64
QK = NOPE + ROPE
SCALE = HD ** -0.5
SCALE_C = QK ** -0.5

COLS = {"naq": 0, "nak": 256, "nav": 512, "pool": 768, "cq": 1024, "ckv": 1280, "swq": 1440, "swkv": 1696}
KPE = 1408
UW = 256
WU = KC * UW
GROUPS = 8
GC = D_FF // P // GROUPS

NCB, QC, KCOLS = 4, 16, 32
KEY_START = [min(max(min(max(QC * b - 8, 0), GRID_W - 16), 0), GRID_W - KCOLS) for b in range(NCB)]

R_ADA, R_N1, R_N2, R_PS, R_C, NVEC = 0, 48, 56, 64, 66, 82
SHIFT1, SCALE1, GATE1, SHIFT2, SCALE2, GATE2 = (8 * i for i in range(6))
ADA_GROUPS = 12
EARLY = 4

GAINS = {"na_q_norm": 64, "na_k_norm": 64, "swa_q_norm": 64, "swa_k_norm": 64, "mla_q_a_norm": 256,
         "mla_q_norm": 96, "mla_k_norm": 96, "mla_kv_norm": 128, "swa_sink": 4}
GAIN_AT = dict(zip(GAINS, np.cumsum([0, *GAINS.values()])[:-1].tolist()))
NGAIN = sum(GAINS.values())


def weight_units():
    out = []
    for l in range(DEPTH):
        out += [(l, n) for n in ("cq", "ckv", "up", "naq", "nak", "nav", "swq", "swkv", "pool")]
        out += [(l, "wo", j) for j in range(D // UW)]
        out += [(l, "w1", 0, j) for j in range(2)]
        for g in range(GROUPS):
            if g + 1 < GROUPS:
                out += [(l, "w1", g + 1, j) for j in range(2)]
            out += [(l, "w2", g, j) for j in range(2)]
    return out


def psum_steps():
    proj, trans, acc = [], [], []
    trans += [("x", c, "act") for c in range(KC)] + [("vec", l, "act") for l in range(DEPTH)]
    for l in range(DEPTH):
        acc += [(l, "sum1", "dve")]
        for n in ("cq", "ckv", "uq", "ukv", "naq", "nak", "nav", "swq", "swkv"):
            proj += [(l, n, t) for t in range(NT + (n == "ukv"))]
        trans += [(l, "cq", 0, "dve"), (l, "cq", 1, "dve"), (l, "ckv", 0, "dve")]
        trans += [(l, n, h, "act") for n in ("q", "k") for h in range(4)]
        trans += [(l, n, h, "act") for n in ("naq", "nak", "swq") for h in range(2)] + [(l, "swk", 0, "act")]
        acc += [(l, "pool", c, "act") for c in range(2)] + [(l, "mix", c, "dve") for c in range(2)]
        acc += [(l, "wo", d, "dve") for d in range(KC)] + [(l, "sum2", "dve")]
        acc += [(l, "z", g, c, "act") for g in range(GROUPS) for c in range(GC)]
    trans += [("out", t, "act") for t in range(NT)]
    return proj, trans, acc


def attention_pairs(kind):
    return [(kind, b, hp) for b in (None, 0, 1, 2, 3) for hp in range(2)]


def keys_of(kind, block):
    if block is None:
        return 1
    return {"C": 5, "A": 3, "D": 3 if block in (0, 3) else 4}[kind]


class Index:

    def __init__(self, steps):
        self.steps = steps
        self.at = {s[:-1]: i for i, s in enumerate(steps)}

    def last_reader(self, i):
        who = self.steps[i][-1]
        return who, sum(s[-1] == who for s in self.steps[:i + 1])


class Linked:

    def __init__(self, eng, own):
        self.eng, self.own, self.count = eng, own, {}

    def __call__(self, ins, sem=None):
        sem = self.own if sem is None else sem
        key = sem.name
        self.count[key] = self.count.get(key, 0) + 1
        ins.then_inc(sem, 1)
        self.eng.wait_ge(sem, self.count[key])


def hybrid_kernel(nc, a, o):
    units = weight_units()
    unit_at = {u: i for i, u in enumerate(units)}
    proj, trans, acc = psum_steps()
    proj_at = {s: i for i, s in enumerate(proj)}
    trans_ix, acc_ix = Index(trans), Index(acc)
    pairs = [(l, *p) for l in range(DEPTH) for kind in "CAD" for p in attention_pairs(kind)]
    pair_at = {p: i for i, p in enumerate(pairs)}
    xupd = []
    for l in range(DEPTH):
        xupd += [(l, "wo", d) for d in range(KC)] + [(l, "y", g, d) for g in range(GROUPS) for d in range(KC)]
    xupd_at = {s: i for i, s in enumerate(xupd)}

    base = (nc.sbuf_base + 63) // 32 * 32
    room = (nc.sbuf_usable_end - base) // 4

    def at(name, off, shape, dt=F32):
        size = int(np.prod(shape[1:]))
        assert off + size <= room, (name, off + size, room)
        return nc.alloc_sbuf_tensor_at(name, shape, dt, offset=base + 4 * off)

    top = [0]

    def sb(name, shape, dt=F32):
        size = (int(np.prod(shape[1:])) + 7) // 8 * 8
        top[0] += size
        return at(name, top[0] - size, shape, dt)

    xT = sb("xT", [P, KC, NTOK])
    h_hi = sb("h_hi", [P, KC, NTOK], F32R)
    h_lo = sb("h_lo", [P, KC, NTOK], F32R)
    w_raw = sb("w_raw", [P, 2, WU])
    w_hi = sb("w_hi", [P, 2, WU], F32R)
    w_lo = sb("w_lo", [P, 2, WU], F32R)
    ada_w = sb("ada_w", [P, 2, KC, P])
    mixc_hi = sb("mixc_hi", [P, 2, NTOK], F32R)
    mixc_lo = sb("mixc_lo", [P, 2, NTOK], F32R)
    ident = sb("ident", [P, P])
    ones = sb("ones", [P, P])
    gains = sb("gains", [P, NGAIN])
    rope_d = sb("rope_d", [P, 2, 4, HD])
    rope_c = sb("rope_c", [P, 2, 4, ROPE])
    band = sb("band", [P, 2, P])
    col_mask = sb("col_mask", [P, 3, KCOLS])
    mod = sb("mod", [P, 2, 48, 2])
    vcol = sb("vcol", [P, DEPTH, NVEC])
    cond = sb("cond", [P, KC, 32])
    pool_w = sb("pool_w", [P, 2, P])
    cache_in = sb("cache_in", [P, 128 + 32 + 256 + 128])
    acol = sb("acol", [P, KC, 2])
    cexp = sb("cexp", [P, 16])
    hstat = sb("hstat", [P, 24])
    mx = sb("mx", [P, 2, 2])
    nb = sb("nb", [P, 2, 2])
    lsum = sb("lsum", [P, 2, 2])
    rinv = sb("rinv", [P, 2, 2])
    sink_e = sb("sink_e", [P, 2, 2])
    A0 = top[0]

    x_in = at("x_in", A0, [P, NT, D])
    vec_in = at("vec_in", A0 + NT * D, [P, DEPTH, P])
    z_hi = at("z_hi", A0, [P, 2 * GC, NTOK], F32R)
    z_lo = at("z_lo", A0 + 5120, [P, 2 * GC, NTOK], F32R)
    z_relu = at("z_relu", A0 + 10240, [P, 2, NTOK])
    z_sq = at("z_sq", A0 + 11520, [P, 2, NTOK])
    sq = at("sq", A0 + 12800, [P, 2, NTOK])
    xr = at("xr", A0 + 14080, [P, 2, NTOK])
    hf = at("hf", A0 + 15360, [P, 2, NTOK])
    rstd = at("rstd", A0 + 11520, [P, NTOK])
    c_q = at("c_q", A0, [P, 4, NTOK])
    c_k = at("c_k", A0 + 2560, [P, 4, NTOK + PAST])
    c_v = at("c_v", A0 + 5632, [P, NT + 1, 256])
    T0 = A0 + 7168
    cq_st = at("cq_st", T0, [P, NT, Q_RANK])
    ckv_st = at("ckv_st", T0 + 1280, [P, NT, KV_RANK + ROPE])
    q_st = at("q_st", T0, [P, NT, 4 * QK])
    k_st = at("k_st", T0 + 2080, [P, NT + 1, 4, QK])
    cqT_hi = at("cqT_hi", T0 + 4384, [P, 2, NTOK], F32R)
    cqT_lo = at("cqT_lo", T0 + 5664, [P, 2, NTOK], F32R)
    ckvT_hi = at("ckvT_hi", T0 + 6944, [P, NTOK + PAST], F32R)
    ckvT_lo = at("ckvT_lo", T0 + 7712, [P, NTOK + PAST], F32R)
    sq_cq = at("sq_cq", T0 + 2080, [P, NT, Q_RANK])
    sq_up = at("sq_up", T0 + 4384, [P, (NT + 1) * 4 * QK])
    rope_tmp_c = at("rope_tmp_c", T0 + 8480, [P, 2, 4, ROPE])
    pr_c = at("pr_c", T0, [P, 2, 2, NT * P])
    pt_c = at("pt_c", T0 + 2560, [P, 2, 2, NT * P])
    a_q = at("a_q", A0, [P, 4, NTOK])
    a_k = at("a_k", A0 + 2560, [P, 2, NTOK + PAST])
    a_v = at("a_v", A0 + 4096, [P, NCB, 2, 256])
    a_vx = at("a_vx", A0 + 6144, [P, 2, 256])
    a_bias = at("a_bias", A0 + 6656, [P, 4, 8, 48])
    d_q = at("d_q", A0 + 8192, [P, 4, NTOK])
    d_k = at("d_k", A0 + 10752, [P, NTOK + PAST])
    d_v = at("d_v", A0 + 11520, [P, NT + 1, P])
    T1 = A0 + 12288
    st = at("st", T1, [P, 2, NT, 256])
    sq_st = at("sq_st", T1 + 2560, [P, NT, 256])
    rpb_in = at("rpb_in", T1 + 3840, [60, 64])
    rope_tmp_d = at("rope_tmp_d", T1 + 3904, [P, 2, 4, HD])
    pr_a = at("pr_a", T1, [P, 2, 2, 512])
    pt_a = at("pt_a", T1 + 2048, [P, 2, 2, 512])
    pool_in = at("pool_in", T1, [P, 2, SEG])
    pool_s = at("pool_s", T1 + 1344, [P, 2, SEG])
    pool_rc = at("pool_rc", T1 + 2688, [P, SEG])
    ada_row = at("ada_row", A0 + 16704, [P, 512])
    y_out = at("y_out", A0, [P, 2, D])

    ctx = ExitStack()
    with ctx:
        ps = ctx.enter_context(nc.psum_tensor("ps", [P, 4096], F32))
        rpb_pad = nc.dram_tensor("rpb_pad", (DEPTH, 60, 64), F32).ap()

        def sem(name):
            return ctx.enter_context(nc.semaphore(name))

        x_in_dma, vec_dma, const_dma, gain_dma = sem("x_in_dma"), sem("vec_dma"), sem("const_dma"), sem("gain_dma")
        cache_dma, pool_w_dma = sem("cache_dma"), sem("pool_w_dma")
        w_dma = [sem("w_dma0"), sem("w_dma1")]
        ada_dma = [sem("ada_dma0"), sem("ada_dma1")]
        av_dma, ad_cache_dma, rpb_dma, bias_dma, rc_dma = (
            sem("av_dma"), sem("ad_cache_dma"), sem("rpb_dma"), sem("bias_dma"), sem("rc_dma"))
        cv_dma = sem("cv_dma")
        out_st0, out_st1, out_ckv = sem("out_st0"), sem("out_st1"), sem("out_ckv")
        out_y = [sem("out_y0"), sem("out_y1")]
        consts_set, pads_set, rpb_zeroed = sem("consts_set"), sem("pads_set"), sem("rpb_zeroed")
        pool_chain = sem("pool_chain")
        xr_ready, dv_ready = sem("xr_ready"), sem("dv_ready")
        t_done, p_done, m_done, y_done = sem("t_done"), sem("p_done"), sem("m_done"), sem("y_done")
        ada_used, ada_turned = sem("ada_used"), sem("ada_turned")
        scored, turned, pv_done = sem("scored"), sem("turned"), sem("pv_done")
        act_chain = sem("act_chain")
        w_hi_ready, p_read, t_act, m_act = sem("w_hi_ready"), sem("p_read"), sem("t_act"), sem("m_act")
        cond_exp, ada_rows, sq_ready, sqrt_ready = sem("cond_exp"), sem("ada_rows"), sem("sq_ready"), sem("sqrt_ready")
        h_hi_ready, st_sq, st_sqrt, t_hi = sem("h_hi_ready"), sem("st_sq"), sem("st_sqrt"), sem("t_hi")
        exp_done, pt_ready, mix_hi, mixp_hi, z_hi_ready, z_relu_ready = (
            sem("exp_done"), sem("pt_ready"), sem("mix_hi"), sem("mixp_hi"), sem("z_hi_ready"), sem("z_relu_ready"))
        dve_chain = sem("dve_chain")
        w_lo_ready, t_dve, m_dve, y_read = sem("w_lo_ready"), sem("t_dve"), sem("m_dve"), sem("y_read")
        cond_den, cond_ready, ada_reduced, mean_ready, rstd_ready = (
            sem("cond_den"), sem("cond_ready"), sem("ada_reduced"), sem("mean_ready"), sem("rstd_ready"))
        hf_ready, h_lo_ready, st_mean, st_normed = sem("hf_ready"), sem("h_lo_ready"), sem("st_mean"), sem("st_normed")
        kpe_copied, pool_ready = sem("kpe_copied"), sem("pool_ready")
        max_ready, p_normed, mix_lo, x_updated = sem("max_ready"), sem("p_normed"), sem("mix_lo"), sem("x_updated")
        z_sq_ready, z_lo_ready = sem("z_sq_ready"), sem("z_lo_ready")
        sum_used, pool_zeroed = sem("sum_used"), sem("pool_zeroed")

        def bank(b, n=512):
            return ps[:, 512 * b:512 * b + n]

        def trans_view(i, width):
            b = 2 if i % 2 == 0 else 6
            return ps[:, 512 * b:512 * b + width]

        def acc_banks(i):
            s = acc[i]
            if s[1] in ("pool", "mix"):
                return 4 * s[2]
            if s[1] in ("sum1", "sum2"):
                return 0
            return 2 * (s[-2] % 2)

        def acc_view(i):
            b = acc_banks(i)
            return ps[:, 512 * b:512 * b + 1024].rearrange("p (a n) -> p a n", a=2)[:, :, 0:HALF]

        def unit_width(n):
            return 1280 if units[n][1] == "up" else WU

        def dma_count(n):
            return 16 * (n // 2 + 1 + sum(units[m][1] == "up" for m in range(n % 2, n + 1, 2)))

        def wait_unit_done(eng, n):
            u = units[n]
            l, kind = u[0], u[1]
            if kind in ("w1", "w2"):
                g, j = u[2], u[3]
                if kind == "w1":
                    eng.wait_ge(m_done, acc_ix.at[(l, "z", g, 2 * j + 1)] + 1)
                else:
                    eng.wait_ge(y_done, (l * GROUPS + g) * KC + 4 * j + 4)
            elif kind == "wo":
                eng.wait_ge(m_done, acc_ix.at[(l, "wo", 2 * u[2] + 1)] + 1)
            elif kind == "pool":
                eng.wait_ge(m_done, acc_ix.at[(l, "pool", 1)] + 1)
            elif kind == "up":
                eng.wait_ge(p_done, proj_at[(l, "ukv", NT)] + 1)
            else:
                eng.wait_ge(p_done, proj_at[(l, kind, NT - 1)] + 1)

        NORMS = ("cq", "ckv", "q", "k", "naq", "nak", "swq", "swkv")

        def norm_at(l, n):
            return l * len(NORMS) + NORMS.index(n)

        def st_of(n):
            if n == "cq":
                return cq_st[:, :, :]
            if n == "ckv":
                return ckv_st[:, :, 0:KV_RANK]
            if n == "q":
                return q_st[:, :, :].rearrange("p t (h w) -> p (t h) w", w=QK)
            if n == "k":
                return k_st[:, :, :, :].rearrange("p t h w -> p (t h) w")
            b = {"naq": 0, "nak": 1, "nav": 0, "swq": 1, "swkv": 0}[n]
            if n == "swkv":
                return st[:, b, :, 0:128].rearrange("p t (h w) -> p t h w", w=HD)
            return st[:, b, :, :].rearrange("p t (h w) -> p (t h) w", w=HD)

        def sq_of(n):
            if n == "cq":
                return sq_cq[:, :, :]
            if n == "ckv":
                return sq_cq[:, :, 0:KV_RANK]
            if n == "q":
                return sq_up[:, 0:NT * 4 * QK].rearrange("p (g w) -> p g w", w=QK)
            if n == "k":
                return sq_up[:, :].rearrange("p (g w) -> p g w", w=QK)
            if n == "swkv":
                return sq_st[:, :, 0:128].rearrange("p t (h w) -> p t h w", w=HD)
            return sq_st[:, :, :].rearrange("p t (h w) -> p (t h) w", w=HD)

        def mixed(k, part):
            if k in (4, 5):
                return (mixc_hi, mixc_lo)[part][:, k - 4, :]
            return (h_hi, h_lo)[part][:, k, :]

        def mixed_at(l, pair):
            kind, b, hp = pair
            chunk = {"C": 4, "A": 0, "D": 6}[kind] + hp
            if b is None:
                return [mixed(chunk, p)[:, 0:CTX] for p in (0, 1)], bank(7, P)
            if kind == "A":
                dst = [mixed(chunk, p)[:, CTX:NTOK].rearrange("p (r c) -> p r c", r=ROWS)[:, :, QC * b:QC * b + QC]
                       for p in (0, 1)]
                return dst, bank(7, P).rearrange("p (r c) -> p r c", r=ROWS)
            return [mixed(chunk, p)[:, CTX + P * b:CTX + P * b + P] for p in (0, 1)], bank(7, P)

        def scores(i, pair):
            kind, b, _ = pair
            n = keys_of(kind, b) * P
            if kind == "C":
                return ps[:, 0:2048].rearrange("p (h n) -> p h n", h=2)[:, :, 0:n]
            off = 1024 * (i % 2)
            return ps[:, off:off + 1024].rearrange("p (h n) -> p h n", h=2)[:, :, 0:n]

        def probs(i, pair):
            kind, b, _ = pair
            return (pr_c if kind == "C" else pr_a)[:, i % 2, :, 0:keys_of(kind, b) * P]

        def probs_t(i, pair):
            kind, b, _ = pair
            return (pt_c if kind == "C" else pt_a)[:, i % 2, :, 0:keys_of(kind, b) * P]

        def ada_unit_place(u):
            return u // 48, u % 48

        block = ctx.enter_context(nc.Block())

        @block.sync
        def _(sp):
            def row(ap, n):
                return ap.rearrange("(r c) -> r c", r=n)

            def load_weights(n):
                if n >= len(units):
                    return
                if n >= 2:
                    sp.wait_ge(w_lo_ready, n - 1)
                u = units[n]
                l, kind = u[0], u[1]
                dst = w_raw[:, n % 2, :]
                if kind == "up":
                    sp.dma_start(dst[:, 0:768].rearrange("p (k c) -> p k c", k=2),
                                 a["mla_w_uq"][l].rearrange("(k p) c -> p k c", p=P)).then_inc(w_dma[n % 2], 16)
                    sp.dma_start(dst[:, 768:1280], a["mla_w_ukv"][l]).then_inc(w_dma[n % 2], 16)
                    return
                if kind == "w2":
                    g, j = u[2], u[3]
                    src = a["mlp_w2"][l, 512 * g:512 * g + 512, 512 * j:512 * j + 512]
                    sp.dma_start(dst.rearrange("p (k c) -> p k c", k=GC),
                                 src.rearrange("(k p) c -> p k c", p=P)).then_inc(w_dma[n % 2], 16)
                    return
                if kind == "wo":
                    src = a["w_out"][l, :, UW * u[2]:UW * u[2] + UW]
                elif kind == "w1":
                    c = 512 * u[2] + UW * u[3]
                    src = a["mlp_w1"][l, :, c:c + UW]
                else:
                    src = a["w_in"][l, :, COLS[kind]:COLS[kind] + UW]
                sp.dma_start(dst.rearrange("p (k c) -> p k c", k=KC),
                             src.rearrange("(k p) c -> p k c", p=P)).then_inc(w_dma[n % 2], 16)

            def load_ada(u):
                if u >= 48 * DEPTH:
                    return
                if u >= 2:
                    sp.wait_ge(ada_used, u - 1)
                l, c = ada_unit_place(u)
                sp.dma_start(ada_w[:, u % 2], a["w_ada"][l, :, P * c:P * c + P].rearrange("(k p) c -> p k c", p=P))\
                  .then_inc(ada_dma[u % 2], 16)

            def ada_tick(first, k):
                if k < 16:
                    load_ada(first + k + 2)

            sp.dma_start(x_in[:, 0, :], a["x_prompt"][0]).then_inc(x_in_dma, 16)
            sp.dma_start(x_in[:, 1:NT, :], a["x_sample"][0].rearrange("(t p) d -> p t d", p=P)).then_inc(x_in_dma, 16)
            for l in range(DEPTH):
                for r, src, n in ((R_ADA, a["b_ada"][l], 48), (R_N1, a["norm1"][l], 8), (R_N2, a["norm2"][l], 8),
                                  (R_PS, a["pool_scale"][l], 2), (R_C, a["c_ctx"], 8), (R_C + 8, a["c"][0], 8)):
                    sp.dma_start(vec_in[r:r + n, l, :], row(src, n)).then_inc(vec_dma, 16)
            load_ada(0)
            load_ada(1)
            sp.dma_start(rope_d[:, :, :, :], a["rope_d"]).then_inc(const_dma, 16)
            sp.dma_start(rope_c[:, :, :, :], a["rope_c"]).then_inc(const_dma, 16)
            sp.dma_start(band[:, :, :], a["band"]).then_inc(const_dma, 16)
            sp.dma_start(col_mask[:, :, :], a["col_mask"]).then_inc(const_dma, 16)
            load_weights(0)
            load_weights(1)
            for k in range(18):
                ada_tick(0, k)
            for l in range(DEPTH):
                U = 45 * l
                if l:
                    sp.wait_ge(st_normed, norm_at(l - 1, "swkv") + 1)
                    sp.wait_ge(t_done, trans_ix.at[(l - 1, "swk", 0)] + 1)
                    sp.wait_ge(p_normed, pair_at[(l - 1, "D", 3, 1)] + 1)
                    sp.wait_ge(m_done, acc_ix.at[(l - 1, "mix", 1)] + 1)
                for name, w in GAINS.items():
                    sp.dma_start(gains[:, GAIN_AT[name]:GAIN_AT[name] + w],
                                 a[name][l].unsqueeze(0).broadcast_to([P, w])).then_inc(gain_dma, 16)
                sp.dma_start(cache_in[:, 0:128], a["cache_mla_ckv"][0, l]).then_inc(cache_dma, 16)
                sp.dma_start(cache_in[:, 128:160], a["cache_mla_kpe"][0, l]).then_inc(cache_dma, 16)
                sp.dma_start(cache_in[:, 160:416], a["cache_na_k"][0, l].rearrange("t h d -> t (h d)")).then_inc(cache_dma, 16)
                sp.dma_start(cache_in[:, 416:544], a["cache_swa_k"][0, l].rearrange("t h d -> t (h d)")).then_inc(cache_dma, 16)
                sp.wait_ge(consts_set, 1)
                for g in range(4):
                    q = 64 * (g % 2)
                    sp.dma_start(pool_w[q:q + 64, g // 2, q:q + 64], a["pool_w"][l, g]).then_inc(pool_w_dma, 16)

                tick = iter(range(99))
                first = 48 * l + 16

                def unit(n, name, steps):
                    load_weights(U + n + 2)
                    for _ in range(steps):
                        ada_tick(first, next(tick))

                unit(0, "cq", NT)
                unit(1, "ckv", NT)
                sp.wait_ge(st_normed, norm_at(l, "ckv") + 1)
                sp.dma_start(o["mla_ckv_new"][0, l], ckv_st[:, 0, 0:KV_RANK]).then_inc(out_ckv, 16)
                sp.dma_start(o["mla_kpe_new"][0, l], ckv_st[:, 0, KV_RANK:KV_RANK + ROPE]).then_inc(out_ckv, 16)
                unit(2, "up", 2 * NT + 1)
                sp.wait_ge(pv_done, pair_at[(l, "C", 3, 1)] + 1)
                sp.dma_start(a_vx[:, 1, :], a["cache_na_v"][0, l].rearrange("t h d -> t (h d)")).then_inc(ad_cache_dma, 16)
                sp.dma_start(d_v[:, NT, :], a["cache_swa_v"][0, l].rearrange("t h d -> t (h d)")).then_inc(ad_cache_dma, 16)
                sp.wait_ge(rpb_zeroed, l + 1)
                sp.dma_start(rpb_in[:, 16:47], a["na_rpb"][l].rearrange("h r c -> (h r) c")).then_inc(rpb_dma, 16)
                sp.wait_ge(rpb_dma, 32 * l + 16)
                sp.dma_start(rpb_pad[l], rpb_in[:, :]).then_inc(rpb_dma, 16)
                sp.wait_ge(rpb_dma, 32 * l + 32)
                for h in range(4):
                    for r in range(ROWS):
                        src = bass.AP(rpb_pad.tensor, offset=(l * 60 + 15 * h + r) * 64, ap=[[1, QC], [64, 8], [1, 48]])
                        sp.dma_start(a_bias[QC * r:QC * r + QC, h, :, :], src).then_inc(bias_dma, 16)
                tick = iter(range(99))
                first = 48 * l + 32
                unit(3, "naq", NT)
                unit(4, "nak", NT)
                sp.wait_ge(st_normed, norm_at(l, "nak") + 1)
                sp.dma_start(o["na_k_new"][0, l].rearrange("t h d -> t (h d)"), st[:, 1, 0, :]).then_inc(out_st1, 16)
                unit(5, "nav", NT)
                sp.wait_ge(p_read, proj_at[(l, "nav", NT - 1)] + 1)
                for b in range(NCB):
                    for r in range(ROWS):
                        s = GRID_W * (r % 2) + KEY_START[b]
                        sp.dma_start(a_v[32 * (r % 4):32 * (r % 4) + 32, b, r // 4, :],
                                     st[s:s + 32, 0, 1 + r // 2, :]).then_inc(av_dma, 16)
                sp.dma_start(a_vx[:, 0, :], st[:, 0, 0, :]).then_inc(av_dma, 16)
                sp.dma_start(o["na_v_new"][0, l].rearrange("t h d -> t (h d)"), st[:, 0, 0, :]).then_inc(out_st0, 16)
                unit(6, "swq", NT)
                unit(7, "swkv", NT)
                unit(8, "pool", 0)
                sp.wait_ge(st_normed, norm_at(l, "swkv") + 1)
                sp.dma_start(o["swa_k_new"][0, l].rearrange("t h d -> t (h d)"), st[:, 0, 0, 0:128]).then_inc(out_st0, 16)
                sp.dma_start(o["swa_v_new"][0, l].rearrange("t h d -> t (h d)"), st[:, 0, 0, 128:256]).then_inc(out_st0, 16)
                sp.wait_ge(t_done, trans_ix.at[(l, "swk", 0)] + 1)
                for c in range(2):
                    if c:
                        sp.wait_ge(pool_ready, 2 * l + 1)
                    sp.dma_start(pool_rc[:, :], a["pool_rc"][c]).then_inc(rc_dma, 16)
                tick = iter(range(99))
                first = 48 * (l + 1)
                for j in range(4):
                    load_weights(U + 9 + j + 2)
                    if l + 1 < DEPTH:
                        for _ in range(4):
                            ada_tick(first, next(tick))
                for n in range(13, 45):
                    load_weights(U + n + 2)
            for t in range(NT):
                sp.wait_ge(t_act, trans_ix.last_reader(trans_ix.at[("out", t)])[1])
                dst = o["y_prompt"][0] if t == 0 else o["y_sample"][0, P * (t - 1):P * t]
                sp.dma_start(dst, y_out[:, t % 2, :]).then_inc(out_y[t % 2], 16)
            sp.wait_ge(out_y[0], 16 * 3)
            sp.wait_ge(out_y[1], 16 * 2)
            sp.wait_ge(out_ckv, 32 * DEPTH)
            sp.wait_ge(out_st0, 48 * DEPTH)
            sp.wait_ge(out_st1, 16 * DEPTH)

        @block.gpsimd
        def _(pool):
            do = Linked(pool, pool_chain)
            do(pool.memset(ident[:, :], 0.0))
            do(pool.memset(ones[:, :], 1.0))
            do(pool.memset(cond[:, :, :], 0.0))
            do(pool.memset(pool_w[:, :, :], 0.0))
            do(pool.affine_select(out=ident[:, :], in_=ident[:, :], compare_op=ALU.not_equal, fill=1.0,
                                  base=0, pattern=[[-1, P]], channel_multiplier=1), consts_set)

            def scale_x(nrm):
                pool.wait_ge(rstd_ready, nrm + 1)
                for c in range(KC):
                    if c >= 2:
                        pool.wait_ge(hf_ready, KC * nrm + c - 1)
                    do(pool.tensor_tensor(xr[:, c % 2, :], xT[:, c, :], rstd[:, :], ALU.mult), xr_ready)

            for l in range(DEPTH):
                scale_x(2 * l)
                pool.wait_ge(pv_done, pair_at[(l, "C", 3, 1)] + 1)
                if l:
                    pool.wait_ge(rpb_dma, 32 * l)
                do(pool.memset(rpb_in[:, :], 0.0), rpb_zeroed)
                do(pool.memset(a_q[64:128, 0:4:2, :], 0.0))
                do(pool.memset(a_q[0:64, 1:4:2, :], 0.0))
                do(pool.memset(d_q[64:128, 0:2, :], 0.0))
                do(pool.memset(d_q[0:64, 2:4, :], 0.0), pads_set)
                pool.wait_ge(p_read, proj_at[(l, "swkv", NT - 1)] + 1)
                do(pool.tensor_copy(d_v[:, 0:NT, :], st[:, 0, :, 128:256]), dv_ready)
                pool.wait_ge(t_done, trans_ix.at[(l, "swk", 0)] + 1)
                pool.wait_ge(out_st0, 48 * (l + 1))
                pool.wait_ge(out_st1, 16 * (l + 1))
                do(pool.memset(pool_in[:, :, :], 0.0), pool_zeroed)
                scale_x(2 * l + 1)

        @block.scalar
        def _(act):
            do = Linked(act, act_chain)

            def copy(out, in_, sem=None, scale=None):
                if scale is None:
                    do(nc.scalar.activation(out, in_, ACT.Copy), sem)
                else:
                    do(nc.scalar.activation(out, in_, ACT.Copy, scale=scale), sem)

            def split_hi(n):
                if n >= len(units):
                    return
                act.wait_ge(w_dma[n % 2], dma_count(n))
                if n >= 2:
                    wait_unit_done(act, n - 2)
                w = unit_width(n)
                copy(w_hi[:, n % 2, 0:w], w_raw[:, n % 2, 0:w], w_hi_ready)

            def ada_tick(first, k):
                if k < 16 and k % 4 == 3:
                    u = first + k
                    act.wait_ge(ada_used, u + 1)
                    if u >= 4:
                        act.wait_ge(ada_turned, u // 4)
                    copy(ada_row[:, :], bank(4), ada_rows)

            def norm_in(nrm, x_ready):
                for c in range(KC):
                    x_ready(c)
                    if c >= 2:
                        act.wait_ge(sum_used, (KC - 1) * nrm + c - 1)
                    do(nc.scalar.activation(sq[:, c % 2, :], xT[:, c, :], ACT.Square), sq_ready)
                l, name = nrm // 2, ("sum1", "sum2")[nrm % 2]
                act.wait_ge(m_dve, acc_ix.last_reader(acc_ix.at[(l, name)])[1])
                do(nc.scalar.activation(rstd[:, :], rstd[:, :], ACT.Sqrt), sqrt_ready)
                for c in range(KC):
                    act.wait_ge(hf_ready, KC * nrm + c + 1)
                    copy(h_hi[:, c, :], hf[:, c % 2, :], h_hi_ready)

            def evacuate(l, n, t, dst, src_cols):
                i = proj_at[(l, n, t)]
                act.wait_ge(p_done, i + 1)
                src = bank(i % 2)
                if n == "ukv":
                    v = src.rearrange("p (h c) -> p h c", h=4)
                    copy(k_st[:, t, :, 0:NOPE], v[:, :, 0:NOPE])
                    copy(c_v[:, t, :].rearrange("p (h d) -> p h d", h=4), v[:, :, NOPE:NOPE + DV], p_read)
                else:
                    copy(dst, src[:, 0:src_cols], p_read)

            def square(l, n):
                i = norm_at(l, n)
                if i:
                    act.wait_ge(st_mean, i)
                do(nc.scalar.activation(sq_of(n), st_of(n), ACT.Square), st_sq)

            def root(l, n):
                act.wait_ge(st_mean, norm_at(l, n) + 1)
                do(nc.scalar.activation(hstat[:, :], hstat[:, :], ACT.Sqrt), st_sqrt)

            def turn(l, n, part):
                i = trans_ix.at[(l, n, part)]
                act.wait_ge(t_done, i + 1)
                if n == "cq":
                    copy(cqT_hi[:, part, :], trans_view(i, NTOK), t_hi)
                elif n == "ckv":
                    copy(ckvT_hi[:, :], trans_view(i, NTOK + PAST), t_hi)
                elif n == "q":
                    copy(c_q[0:QK, part, :], trans_view(i, NTOK)[0:QK], t_act)
                elif n == "k":
                    copy(c_k[0:QK, part, :], trans_view(i, NTOK + PAST)[0:QK], t_act)
                elif n == "naq":
                    v = trans_view(i, NTOK)
                    for h in range(2):
                        r = 64 * h
                        copy(a_q[r:r + 64, 2 * part + h, 0:CTX], v[r:r + 64, 0:CTX])
                        copy(a_q[r:r + 64, 2 * part + h, CTX:NTOK].rearrange("p (b r c) -> p r b c", b=NCB, r=ROWS),
                             v[r:r + 64, CTX:NTOK].rearrange("p (r b c) -> p r b c", r=ROWS, b=NCB), t_act if h else None)
                elif n == "swq":
                    v = trans_view(i, NTOK)
                    r = 64 * part
                    copy(d_q[r:r + 64, 2 * part, :], v[0:64])
                    copy(d_q[r:r + 64, 2 * part + 1, :], v[64:128], t_act)
                elif n == "nak":
                    copy(a_k[:, part, :], trans_view(i, NTOK + PAST), t_act)
                else:
                    copy(d_k[:, :], trans_view(i, NTOK + PAST), t_act)

            def attention(l, kind_list):
                todo = [(pair_at[(l, *p)], p) for kind in kind_list for p in attention_pairs(kind)]

                def exps(i, pair):
                    kind = pair[0]
                    act.wait_ge(max_ready, i + 1)
                    if i >= 2:
                        act.wait_ge(turned, i - 1)
                    scale = SCALE_C if kind == "C" else SCALE
                    if kind == "D":
                        do(nc.scalar.activation(sink_e[:, i % 2, :], sink_e[:, i % 2, :], ACT.Exp))
                    for h in range(2):
                        do(nc.scalar.activation(probs(i, pair)[:, h, :], scores(i, pair)[:, h, :], ACT.Exp,
                                                bias=nb[:, i % 2, h:h + 1], scale=scale,
                                                accum_out=lsum[:, i % 2, h:h + 1]),
                           exp_done if h else None)

                def take_turned(i, pair):
                    act.wait_ge(turned, i + 1)
                    if i >= 2:
                        act.wait_ge(pv_done, i - 1)
                    dst, n = probs_t(i, pair), keys_of(pair[0], pair[1])
                    w = min(n, 4) * P
                    src = ps[:, 2048:3072].rearrange("p (h n) -> p h n", h=2)[:, :, 0:w]
                    if n == 5:
                        copy(dst[:, :, 0:w], src)
                        copy(dst[:, :, w:w + P], ps[:, 3072:3072 + 2 * P].rearrange("p (h n) -> p h n", h=2), pt_ready)
                    else:
                        copy(dst[:, :, 0:w], src, pt_ready)

                def take_out(i, pair):
                    act.wait_ge(pv_done, i + 1)
                    dst, src = mixed_at(l, pair)
                    copy(dst[0], src, mix_hi)

                for j, (i, pair) in enumerate(todo):
                    exps(i, pair)
                    if j >= 1:
                        take_turned(*todo[j - 1])
                    if j >= 2:
                        take_out(*todo[j - 2])
                take_turned(*todo[-1])
                take_out(*todo[-2])
                take_out(*todo[-1])

            split_hi(0)
            for c in range(KC):
                act.wait_ge(t_done, c + 1)
                copy(xT[:, c, :], trans_view(c, NTOK), t_act)
            for l in range(DEPTH):
                act.wait_ge(t_done, KC + l + 1)
                copy(vcol[:, l, :], trans_view(KC + l, NVEC), t_act)
            do(nc.scalar.activation(cexp[:, :], vcol[:, 0, R_C:NVEC], ACT.Exp, scale=-1.0), cond_exp)
            for k in range(18):
                ada_tick(0, k)

            for l in range(DEPTH):
                U = 45 * l
                norm_in(2 * l, lambda c: l and act.wait_ge(y_read, (l * GROUPS - 1) * KC + c + 1))
                tick, first = iter(range(99)), 48 * l + 16

                def unit(n, name, dst, cols, root_of=None, tiles=NT, split=True):
                    if split:
                        split_hi(U + n + 1)
                    for t in range(tiles):
                        evacuate(l, name, t, dst(t), cols)
                        ada_tick(first, next(tick))
                        if t == 1 and root_of:
                            root(l, root_of)

                unit(0, "cq", lambda t: cq_st[:, t, :], 256)
                square(l, "cq")
                unit(1, "ckv", lambda t: ckv_st[:, t, :], 160, "cq")
                square(l, "ckv")
                turn(l, "cq", 0)
                turn(l, "cq", 1)
                root(l, "ckv")
                turn(l, "ckv", 0)
                act.wait_ge(out_ckv, 32 * (l + 1))
                act.wait_ge(kpe_copied, l + 1)
                unit(2, "uq", lambda t: q_st[:, t, :], 4 * QK)
                square(l, "q")
                unit(2, "ukv", lambda t: None, 0, "q", NT + 1, split=False)
                for h in range(4):
                    turn(l, "q", h)
                square(l, "k")
                root(l, "k")
                for h in range(4):
                    turn(l, "k", h)
                attention(l, "C")
                tick, first = iter(range(99)), 48 * l + 32
                unit(3, "naq", lambda t: st[:, 0, t, :], 256)
                square(l, "naq")
                unit(4, "nak", lambda t: st[:, 1, t, :], 256, "naq")
                square(l, "nak")
                turn(l, "naq", 0)
                turn(l, "naq", 1)
                unit(5, "nav", lambda t: st[:, 0, t, :], 256, "nak")
                turn(l, "nak", 0)
                turn(l, "nak", 1)
                act.wait_ge(out_st1, 16 * (l + 1))
                unit(6, "swq", lambda t: st[:, 1, t, :], 256)
                square(l, "swq")
                act.wait_ge(av_dma, 16 * 33 * (l + 1))
                act.wait_ge(out_st0, 48 * l + 16)
                unit(7, "swkv", lambda t: st[:, 0, t, :], 256, "swq")
                square(l, "swkv")
                turn(l, "swq", 0)
                turn(l, "swq", 1)
                root(l, "swkv")
                turn(l, "swk", 0)
                split_hi(U + 9)
                act.wait_ge(pool_zeroed, l + 1)
                for c in range(2):
                    i = acc_ix.at[(l, "pool", c)]
                    act.wait_ge(m_done, i + 1)
                    v = acc_view(i)
                    lat = PAD + CTX + 2 * PAD
                    copy(pool_in[:, c, PAD:PAD + CTX], v[:, 0, 0:CTX])
                    copy(pool_in[:, c, lat:lat + HALF - CTX], v[:, 0, CTX:HALF])
                    copy(pool_in[:, c, lat + HALF - CTX:lat + LAT], v[:, 1, :], m_act)
                for c in range(2):
                    i = acc_ix.at[(l, "mix", c)]
                    act.wait_ge(m_done, i + 1)
                    copy(h_hi[:, 2 + c, :].rearrange("p (a n) -> p a n", a=2), acc_view(i), mixp_hi,
                         scale=vcol[:, l, R_PS + c:R_PS + c + 1])
                attention(l, "AD")
                first, tick = 48 * (l + 1), iter(range(99))
                for j in range(4):
                    split_hi(U + 9 + j + 1)
                    if l + 1 < DEPTH:
                        for _ in range(4):
                            ada_tick(first, next(tick))
                norm_in(2 * l + 1, lambda c: act.wait_ge(m_dve, acc_ix.last_reader(acc_ix.at[(l, "wo", c)])[1]))
                for n in range(13, 45):
                    split_hi(U + n + 1)
                    u = units[U + n]
                    if u[1] == "w1":
                        g = u[2]
                        gg = l * GROUPS + g
                        for c in (2 * u[3], 2 * u[3] + 1):
                            zi = gg * GC + c
                            i = acc_ix.at[(l, "z", g, c)]
                            act.wait_ge(m_done, i + 1)
                            if zi >= 2:
                                act.wait_ge(z_sq_ready, zi - 1)
                            do(nc.scalar.activation(z_relu[:, c % 2, :].rearrange("p (a n) -> p a n", a=2),
                                                    acc_view(i), ACT.Relu), m_act)
                            if gg >= 2:
                                act.wait_ge(y_done, (gg - 1) * KC)
                            slot = GC * (g % 2) + c
                            do(nc.scalar.activation(z_hi[:, slot, :], z_relu[:, c % 2, :], ACT.Square), z_hi_ready)
            for t in range(NT):
                i = trans_ix.at[("out", t)]
                act.wait_ge(t_done, i + 1)
                if t >= 2:
                    act.wait_ge(out_y[t % 2], 16 * (t // 2))
                copy(y_out[:, t % 2, :], trans_view(i, D), t_act)

        @block.vector
        def _(dve):
            do = Linked(dve, dve_chain)
            V = nc.vector

            def f32(ap):
                return ap.bitcast(F32)

            def split_lo(n):
                if n >= len(units):
                    return
                dve.wait_ge(w_hi_ready, n + 1)
                w = unit_width(n)
                do(V.tensor_tensor(w_lo[:, n % 2, 0:w], w_raw[:, n % 2, 0:w], f32(w_hi[:, n % 2, 0:w]),
                                   ALU.subtract), w_lo_ready)

            def ada_tick(first, k):
                if 5 <= k < 18 and (k - 5) % 4 == 0:
                    u = first + 4 * ((k - 5) // 4)
                    l, c = ada_unit_place(u)
                    dve.wait_ge(ada_turned, u // 4 + 1)
                    m = mod[:, l % 2, c:c + 4, :]
                    do(V.tensor_reduce(m, bank(5).rearrange("p (c j m) -> p c m j", c=4, j=4)[:, :, 0:2, :],
                                       AX_X, ALU.add), ada_reduced)
                    do(V.tensor_tensor(m, m, vcol[:, l, R_ADA + c:R_ADA + c + 4].unsqueeze(2).broadcast_to([P, 4, 2]),
                                       ALU.add))

            def norm_in(nrm):
                l, which = nrm // 2, nrm % 2
                i = acc_ix.at[(l, ("sum1", "sum2")[which])]
                dve.wait_ge(m_done, i + 1)
                do(V.tensor_scalar(rstd[:, :].rearrange("p (a n) -> p a n", a=2), acc_view(i), 1.0 / D, EPS,
                                   ALU.mult, ALU.add), m_dve)
                sc = (SCALE1, SCALE2)[which]
                sh = (SHIFT1, SHIFT2)[which]
                gain = vcol[:, l, (R_N1, R_N2)[which]:(R_N1, R_N2)[which] + KC].unsqueeze(2).broadcast_to([P, KC, 2])
                do(V.scalar_tensor_tensor(acol[:, :, :], mod[:, l % 2, sc:sc + KC, :], 1.0, gain, ALU.add, ALU.mult))
                dve.wait_ge(sqrt_ready, nrm + 1)
                do(V.reciprocal(rstd[:, :], rstd[:, :]), rstd_ready)

                def lo(c):
                    dve.wait_ge(h_hi_ready, KC * nrm + c + 1)
                    do(V.tensor_tensor(h_lo[:, c, :], hf[:, c % 2, :], f32(h_hi[:, c, :]), ALU.subtract), h_lo_ready)

                for c in range(KC):
                    dve.wait_ge(xr_ready, KC * nrm + c + 1)
                    for m, (s, e) in enumerate(((0, CTX), (CTX, NTOK))):
                        do(V.tensor_scalar(hf[:, c % 2, s:e], xr[:, c % 2, s:e], acol[:, c, m:m + 1],
                                           mod[:, l % 2, sh + c, m:m + 1], ALU.mult, ALU.add), hf_ready if m else None)
                    if c:
                        lo(c - 1)
                lo(KC - 1)

            def rope(x, tab, tmp):
                do(V.tensor_tensor(tmp[:, 0], x, tab[:, 0], ALU.mult))

                def quarters(v, s):
                    return v.rearrange("p t (f s q) -> p t f s q", f=2, s=2)[:, :, :, s, :]

                for s in range(2):
                    do(V.tensor_tensor(quarters(tmp[:, 1], s), quarters(x, 1 - s), quarters(tab[:, 1], s), ALU.mult))
                do(V.tensor_tensor(x, tmp[:, 0], tmp[:, 1], ALU.add))

            def norm(l, n):
                gain, w, g = {"cq": ("mla_q_a_norm", 256, 5), "ckv": ("mla_kv_norm", 128, 5),
                              "q": ("mla_q_norm", QK, 20), "k": ("mla_k_norm", QK, 24),
                              "naq": ("na_q_norm", HD, 20), "nak": ("na_k_norm", HD, 20),
                              "swq": ("swa_q_norm", HD, 20), "swkv": ("swa_k_norm", HD, 10)}[n]
                x = st_of(n)
                dve.wait_ge(st_sq, norm_at(l, n) + 1)
                hs = hstat[:, 0:g]
                if n == "swkv":
                    hs = hs.rearrange("p (t h) -> p t h", h=2)
                do(V.tensor_reduce(hs, sq_of(n), AX_X, ALU.add))
                do(V.tensor_scalar(hstat[:, :], hstat[:, :], 1.0 / w, EPS, ALU.mult, ALU.add), st_mean)
                dve.wait_ge(st_sqrt, norm_at(l, n) + 1)
                do(V.reciprocal(hstat[:, :], hstat[:, :]))
                shape = list(x.shape)
                do(V.tensor_tensor(x, x, hs.unsqueeze(len(shape) - 1).broadcast_to(shape), ALU.mult))
                row = gains[:, GAIN_AT[gain]:GAIN_AT[gain] + w]
                for _ in shape[1:-1]:
                    row = row.unsqueeze(1)
                last = n in ("cq", "ckv", "naq", "nak")
                do(V.tensor_tensor(x, x, row.broadcast_to(shape), ALU.mult), st_normed if last else None)
                if last:
                    return
                if n == "q":
                    parts = [q_st[:, 1:NT, QK * h + NOPE:QK * h + QK] for h in range(4)]
                elif n == "k":
                    parts = [k_st[:, 1:NT, h, NOPE:QK] for h in range(4)]
                else:
                    b, heads = (1, 4) if n == "swq" else (0, 2)
                    parts = [st[:, b, 1:NT, HD * h:HD * h + HD] for h in range(heads)]
                tab, tmp = (rope_c, rope_tmp_c) if n in "qk" else (rope_d, rope_tmp_d)
                for part in parts[:-1]:
                    rope(part, tab, tmp)
                x = parts[-1]
                do(V.tensor_tensor(tmp[:, 0], x, tab[:, 0], ALU.mult))
                for s in range(2):
                    q = [v.rearrange("p t (f s q) -> p t f s q", f=2, s=2) for v in (tmp[:, 1], x, tab[:, 1])]
                    do(V.tensor_tensor(q[0][:, :, :, s, :], q[1][:, :, :, 1 - s, :], q[2][:, :, :, s, :], ALU.mult))
                do(V.tensor_tensor(x, tmp[:, 0], tmp[:, 1], ALU.add), st_normed)

            def turn(l, n, part):
                i = trans_ix.at[(l, n, part)]
                dve.wait_ge(t_hi, 3 * l + {"cq": 0, "ckv": 2}[n] + part + 1)
                if n == "cq":
                    do(V.tensor_tensor(cqT_lo[:, part, :], trans_view(i, NTOK), f32(cqT_hi[:, part, :]),
                                       ALU.subtract), t_dve)
                else:
                    do(V.tensor_tensor(ckvT_lo[:, :], trans_view(i, NTOK + PAST), f32(ckvT_hi[:, :]),
                                       ALU.subtract), t_dve)

            def attention(l, kind_list):
                todo = [(pair_at[(l, *p)], p) for kind in kind_list for p in attention_pairs(kind)]

                def maxima(i, pair):
                    kind, b, hp = pair
                    dve.wait_ge(scored, i + 1)
                    s = scores(i, pair)
                    if kind == "A" and b is not None:
                        for h in range(2):
                            v = s[:, h, 0:256].rearrange("p (r c) -> p r c", r=8)
                            off = KEY_START[b] - QC * b + 16
                            bias = bass.AP(a_bias[:, 0, 0, 0:1].tensor, ap=[[4 * 8 * 48, P], [-48, 8], [-1, KCOLS]],
                                           offset=(2 * hp + h) * 8 * 48 + 7 * 48 + 47 - off)
                            do(V.scalar_tensor_tensor(v, bias, 1.0 / SCALE, v,
                                                      ALU.mult, ALU.add))
                        for h in range(2):
                            v = s[:, h, 0:256].rearrange("p (r c) -> p r c", r=8)
                            mask = col_mask[:, {0: 0, 1: 1, 2: 1, 3: 2}[b], :].unsqueeze(1).broadcast_to([P, 8, KCOLS])
                            do(V.tensor_tensor(v, v, mask, ALU.add))
                    if kind == "D" and b is not None:
                        lo = max(b - 1, 0)
                        for blk, m in ((b - 1, 0), (b + 1, 1)):
                            if 0 <= blk < 4:
                                v = s[:, :, P * (blk - lo):P * (blk - lo) + P]
                                do(V.tensor_tensor(v, v, band[:, m, :].unsqueeze(1).broadcast_to([P, 2, P]), ALU.add))
                    do(V.tensor_reduce(mx[:, i % 2, :], s, AX_X, ALU.max))
                    scale = SCALE_C if kind == "C" else SCALE
                    if kind != "D":
                        do(V.tensor_scalar(nb[:, i % 2, :], mx[:, i % 2, :], -scale, None, ALU.mult), max_ready)
                    else:
                        sink = gains[:, GAIN_AT["swa_sink"] + 2 * hp:GAIN_AT["swa_sink"] + 2 * hp + 2]
                        do(V.scalar_tensor_tensor(mx[:, i % 2, :], mx[:, i % 2, :], scale, sink, ALU.mult, ALU.max))
                        do(V.tensor_scalar(nb[:, i % 2, :], mx[:, i % 2, :], -1.0, None, ALU.mult))
                        do(V.tensor_tensor(sink_e[:, i % 2, :], sink, mx[:, i % 2, :], ALU.subtract), max_ready)

                def normalise(i, pair):
                    dve.wait_ge(exp_done, i + 1)
                    if pair[0] == "D":
                        do(V.tensor_tensor(lsum[:, i % 2, :], lsum[:, i % 2, :], sink_e[:, i % 2, :], ALU.add))
                    do(V.reciprocal(rinv[:, i % 2, :], lsum[:, i % 2, :]))
                    for h in range(2):
                        v = probs(i, pair)[:, h, :]
                        do(V.tensor_scalar(v, v, rinv[:, i % 2, h:h + 1], None, ALU.mult), p_normed if h else None)

                def take_out(i, pair):
                    dve.wait_ge(mix_hi, i + 1)
                    dst, src = mixed_at(l, pair)
                    do(V.tensor_tensor(dst[1], src, f32(dst[0]), ALU.subtract), mix_lo)

                for j, (i, pair) in enumerate(todo):
                    maxima(i, pair)
                    normalise(i, pair)
                    if j >= 2:
                        take_out(*todo[j - 2])
                take_out(*todo[-2])
                take_out(*todo[-1])

            def add_gated(d, gate, v, sem):
                x = xT[:, d, :]
                for m, dst, src in ((0, x[:, 0:CTX], v[:, 0, 0:CTX]), (1, x[:, CTX:HALF], v[:, 0, CTX:HALF]),
                                    (1, x[:, HALF:NTOK], v[:, 1, :])):
                    last = dst.shape[1] == HALF
                    do(V.scalar_tensor_tensor(dst, src, gate[:, m:m + 1], dst, ALU.mult, ALU.add),
                       sem if last else None)

            split_lo(0)
            dve.wait_ge(cond_exp, 1)
            dve.wait_ge(consts_set, 1)
            do(V.tensor_scalar(cexp[:, :], cexp[:, :], 1.0, None, ALU.add))
            do(V.reciprocal(cexp[:, :], cexp[:, :]))
            do(V.tensor_tensor(cond[:, :, 0:2].rearrange("p k m -> p m k"),
                               vcol[:, 0, R_C:NVEC].rearrange("p (m k) -> p m k", m=2),
                               cexp[:, :].rearrange("p (m k) -> p m k", m=2), ALU.mult), cond_ready)
            do(V.memset(hstat[:, :], 1.0))
            for k in range(18):
                ada_tick(0, k)
            dve.wait_ge(const_dma, 64)

            for l in range(DEPTH):
                U = 45 * l
                norm_in(2 * l)
                dve.wait_ge(gain_dma, 16 * len(GAINS) * (l + 1))
                dve.wait_ge(cache_dma, 64 * (l + 1))
                tick, first = iter(range(99)), 48 * l + 16

                def ticks(n):
                    for _ in range(n):
                        ada_tick(first, next(tick))

                split_lo(U + 1)
                ticks(NT)
                split_lo(U + 2)
                norm(l, "cq")
                ticks(NT)
                turn(l, "cq", 0)
                turn(l, "cq", 1)
                norm(l, "ckv")
                turn(l, "ckv", 0)
                do(V.tensor_copy(k_st[:, 0:NT, :, NOPE:QK],
                                 ckv_st[:, :, KV_RANK:KV_RANK + ROPE].unsqueeze(2).broadcast_to([P, NT, 4, ROPE])))
                do(V.tensor_copy(k_st[:, NT, :, NOPE:QK],
                                 cache_in[:, 128:160].unsqueeze(1).broadcast_to([P, 4, ROPE])), kpe_copied)
                split_lo(U + 3)
                ticks(NT)
                norm(l, "q")
                ticks(NT + 1)
                norm(l, "k")
                attention(l, "C")
                tick, first = iter(range(99)), 48 * l + 32
                split_lo(U + 4)
                ticks(NT)
                split_lo(U + 5)
                norm(l, "naq")
                ticks(NT)
                split_lo(U + 6)
                norm(l, "nak")
                ticks(NT)
                split_lo(U + 7)
                ticks(NT)
                split_lo(U + 8)
                norm(l, "swq")
                ticks(NT)
                norm(l, "swkv")
                split_lo(U + 9)
                for c in range(2):
                    dve.wait_ge(m_act, acc_ix.last_reader(acc_ix.at[(l, "pool", c)])[1])
                    x, s0, s1 = pool_in[:, c, :], pool_s[:, 0, :], pool_s[:, 1, :]
                    do(V.tensor_tensor(s0[:, 1:SEG], x[:, 0:SEG - 1], x[:, 1:SEG], ALU.add))
                    do(V.tensor_tensor(s1[:, 2:SEG - 1], s0[:, 1:SEG - 2], s0[:, 3:SEG], ALU.add))
                    if c:
                        do(V.tensor_tensor(s0[:, 4:SEG - 3], s1[:, 2:SEG - 5], s1[:, 6:SEG - 1], ALU.add))
                        do(V.tensor_tensor(s1[:, 8:SEG - 7], s0[:, 4:SEG - 11], s0[:, 12:SEG - 3], ALU.add))
                    dve.wait_ge(rc_dma, 16 * (2 * l + c + 1))
                    e = slice(PAD, SEG - PAD)
                    do(V.tensor_tensor(s0[0:64, e], s0[0:64, e], pool_rc[0:64, e], ALU.mult))
                    do(V.tensor_tensor(s0[64:128, e], s1[64:128, e], pool_rc[64:128, e], ALU.mult))
                    do(V.tensor_tensor(x[:, e], s0[:, e], x[:, e], ALU.subtract), pool_ready)
                for c in range(2):
                    i = acc_ix.at[(l, "mix", c)]
                    dve.wait_ge(mixp_hi, 2 * l + c + 1)
                    do(V.scalar_tensor_tensor(h_lo[:, 2 + c, :].rearrange("p (a n) -> p a n", a=2), acc_view(i),
                                              vcol[:, l, R_PS + c:R_PS + c + 1],
                                              f32(h_hi[:, 2 + c, :]).rearrange("p (a n) -> p a n", a=2),
                                              ALU.mult, ALU.subtract), m_dve)
                dve.wait_ge(bias_dma, 16 * 32 * (l + 1))
                attention(l, "AD")
                first, tick = 48 * (l + 1), iter(range(99))
                for j in range(4):
                    split_lo(U + 9 + j + 1)
                    for d in (2 * j, 2 * j + 1):
                        i = acc_ix.at[(l, "wo", d)]
                        dve.wait_ge(m_done, i + 1)
                        add_gated(d, mod[:, l % 2, GATE1 + d, :], acc_view(i), m_dve)
                    if l + 1 < DEPTH:
                        ticks(4)
                if l + 1 < DEPTH:
                    ticks(2)
                norm_in(2 * l + 1)
                for n in range(13, 45):
                    split_lo(U + n + 1)
                    u = units[U + n]
                    g = u[2]
                    gg = l * GROUPS + g
                    if u[1] == "w1":
                        for c in (2 * u[3], 2 * u[3] + 1):
                            dve.wait_ge(m_act, acc_ix.last_reader(acc_ix.at[(l, "z", g, c)])[1])
                            do(V.tensor_tensor(z_sq[:, c % 2, :], z_relu[:, c % 2, :], z_relu[:, c % 2, :],
                                               ALU.mult), z_sq_ready)
                            dve.wait_ge(z_hi_ready, gg * GC + c + 1)
                            slot = GC * (g % 2) + c
                            do(V.tensor_tensor(z_lo[:, slot, :], z_sq[:, c % 2, :], f32(z_hi[:, slot, :]),
                                               ALU.subtract), z_lo_ready)
                    else:
                        for d in range(4 * u[3], 4 * u[3] + 4):
                            dve.wait_ge(y_done, gg * KC + d + 1)
                            b = 4 + 2 * (d % 2)
                            v = ps[:, 512 * b:512 * b + 1024].rearrange("p (a n) -> p a n", a=2)[:, :, 0:HALF]
                            add_gated(d, mod[:, l % 2, GATE2 + d, :], v, y_read)

        @block.tensor
        def _(pe):
            M = nc.tensor
            did = {"p": 0, "t": 0, "m": 0, "y": 0, "ada": 0, "pair": 0}

            def quiet():
                if did["p"]:
                    pe.wait_ge(p_read, did["p"])
                for n, ix, by_act, by_dve in (("t", trans_ix, t_act, t_dve), ("m", acc_ix, m_act, m_dve)):
                    for who, s in (("act", by_act), ("dve", by_dve)):
                        count = sum(x[-1] == who for x in ix.steps[:did[n]])
                        if count:
                            pe.wait_ge(s, count)
                if did["y"]:
                    pe.wait_ge(y_read, did["y"])
                if did["ada"]:
                    pe.wait_ge(ada_rows, did["ada"] // 4)
                if did["pair"]:
                    pe.wait_ge(pt_ready, did["pair"])
                    pe.wait_ge(mix_lo, did["pair"])

            def wait_read(ix, i, by_act, by_dve):
                who, count = ix.last_reader(i)
                pe.wait_ge(by_act if who == "act" else by_dve, count)

            def transpose_step(key, pieces):
                i = trans_ix.at[key]
                assert i == did["t"], (key, i, did)
                if i >= 2:
                    wait_read(trans_ix, i - 2, t_act, t_dve)
                v = trans_view(i, 1024)
                for src, c in pieces:
                    last = M.transpose(v[0:src.shape[1], c:c + src.shape[0]], src,
                                       ident[0:src.shape[0], 0:src.shape[0]])
                last.then_inc(t_done, 1)
                did["t"] += 1

            def begin_acc(key):
                i = acc_ix.at[key]
                assert i == did["m"], (key, i, did)
                before = [j for j in range(i) if acc_banks(j) == acc_banks(i)]
                if before:
                    wait_read(acc_ix, before[-1], m_act, m_dve)
                did["m"] += 1
                return acc_view(i)

            def three(out, w_pair, x_pair, first, last):
                w, wl = w_pair
                x, xl = x_pair
                for n, (lhs, rhs) in enumerate(((w, x), (w, xl), (wl, x))):
                    for a_ in range(2):
                        ins = M.matmul(out[:, a_, :], lhs, rhs[:, HALF * a_:HALF * a_ + HALF],
                                       start=first and n == 0, stop=last and n == 2)
                return ins

            def ada_tick(first, k):
                if 5 <= k < 18 and (k - 5) % 4 == 0:
                    q = first // 4 + (k - 5) // 4
                    pe.wait_ge(ada_rows, q + 1)
                    if q:
                        pe.wait_ge(ada_reduced, q)
                    for j in range(4):
                        last = M.transpose(bank(5)[:, P * j:P * j + P], ada_row[:, P * j:P * j + P], ident[:, :])
                    last.then_inc(ada_turned, 1)
                if k < 16:
                    u = first + k
                    pe.wait_ge(ada_dma[u % 2], 16 * (u // 2 + 1))
                    if u % 4 == 0 and u:
                        pe.wait_ge(ada_rows, u // 4)
                    c = P * (u % 4)
                    for kc in range(KC):
                        j = kc % 4
                        last = M.matmul(ps[32 * j:32 * j + 32, 2048 + c:2048 + c + P], cond[:, kc, :],
                                        ada_w[:, u % 2, kc, :], start=kc < 4, stop=kc >= 4, skip_group_check=True)
                    last.then_inc(ada_used, 1)
                    did["ada"] += 1

            def sums(l, which):
                nrm = 2 * l + (which == "sum2")
                out = begin_acc((l, which))
                for c in range(KC):
                    pe.wait_ge(sq_ready, KC * nrm + c + 1)
                    for a_ in range(2):
                        last = M.matmul(out[:, a_, :], ones[:, :], sq[:, c % 2, HALF * a_:HALF * a_ + HALF],
                                        start=c == 0, stop=c == KC - 1)
                    last.then_inc(sum_used if c < KC - 1 else m_done, 1)

            def project(l, n, name, tiles=NT, wait_h=None):
                s = n % 2
                pe.wait_ge(w_lo_ready, n + 1)
                for t in range(tiles):
                    i = proj_at[(l, name, t)]
                    assert i == did["p"]
                    if i >= 2:
                        pe.wait_ge(p_read, i - 1)
                    tok = slice(P * t, P * t + P)
                    if name == "uq":
                        w = [x[:, s, 0:768].rearrange("p (k c) -> p k c", k=2) for x in (w_hi, w_lo)]
                        x, cols, kk = (cqT_hi[:, :, tok], cqT_lo[:, :, tok]), 4 * QK, 2
                    elif name == "ukv":
                        w = [x[:, s, 768:1280].rearrange("p (k c) -> p k c", k=1) for x in (w_hi, w_lo)]
                        x = [y[:, tok].unsqueeze(1) for y in (ckvT_hi, ckvT_lo)]
                        cols, kk = 512, 1
                    else:
                        w = [x[:, s, :].rearrange("p (k c) -> p k c", k=KC) for x in (w_hi, w_lo)]
                        x, cols, kk = (h_hi[:, :, tok], h_lo[:, :, tok]), UW, KC
                    for k in range(kk):
                        if wait_h is not None and t == 0:
                            pe.wait_ge(h_lo_ready, wait_h + k + 1)
                        for q, (p, r) in enumerate(((0, 0), (1, 0), (0, 1))):
                            last = M.matmul(bank(i % 2)[:, 0:cols], x[p][:, k, :], w[r][:, k, :],
                                            start=k == 0 and q == 0, stop=k == kk - 1 and q == 2)
                    last.then_inc(p_done, 1)
                    did["p"] += 1
                    ada = next(tick)
                    if ada < 18:
                        ada_tick(first, ada)

            def attention(l, kind_list):
                todo = [(pair_at[(l, *p)], p) for kind in kind_list for p in attention_pairs(kind)]

                def score(i, pair):
                    kind, b, hp = pair
                    if kind == "C":
                        if i > todo[0][0]:
                            pe.wait_ge(exp_done, i)
                    elif i - 2 >= todo[0][0]:
                        pe.wait_ge(exp_done, i - 1)
                    out = scores(i, pair)
                    for h in range(2):
                        head = 2 * hp + h
                        q = slice(0, P) if b is None else slice(CTX + P * b, CTX + P * b + P)
                        if kind == "C":
                            keys = [(0, c_k[0:QK, head, 0:P])] if b is None else \
                                [(0, c_k[0:QK, head, CTX:CTX + 512]), (512, c_k[0:QK, head, CTX + 512:CTX + 640])]
                            lhs = c_q[0:QK, head, q]
                        elif kind == "A":
                            lhs = a_q[:, head, q]
                            keys = [(0, a_k[:, hp, 0:P])]
                            if b is not None:
                                s = KEY_START[b]
                                loc = a_k[:, hp, CTX:NTOK].rearrange("p (r c) -> p r c", r=ROWS)[:, :, s:s + KCOLS]
                                keys = [(0, loc), (256, a_k[:, hp, NTOK:NTOK + PAST])]
                        else:
                            lhs = d_q[:, head, q]
                            keys = [(0, d_k[:, 0:P])]
                            if b is not None:
                                s, e = CTX + P * max(b - 1, 0), CTX + P * min(b + 2, 4)
                                keys = [(0, d_k[:, s:e]), (e - s, d_k[:, NTOK:NTOK + PAST])]
                        for n, (c, rhs) in enumerate(keys):
                            width = int(np.prod(rhs.shape[1:]))
                            dst = out[:, h, c:c + width]
                            if len(rhs.shape) == 3:
                                dst = dst.rearrange("p (r c) -> p r c", r=ROWS)
                            last = M.matmul(dst, lhs, rhs, start=True, stop=True, skip_group_check=True)
                    last.then_inc(scored, 1)

                def turn(i, pair):
                    pe.wait_ge(p_normed, i + 1)
                    if i > todo[0][0]:
                        pe.wait_ge(pt_ready, i)
                    for h in range(2):
                        for j in range(keys_of(pair[0], pair[1])):
                            c = 2048 + 512 * h + P * j if j < 4 else 3072 + P * h
                            last = M.transpose(ps[:, c:c + P], probs(i, pair)[:, h, P * j:P * j + P], ident[:, :])
                    last.then_inc(turned, 1)

                def values(i, pair):
                    kind, b, hp = pair
                    pe.wait_ge(pt_ready, i + 1)
                    if i > todo[0][0]:
                        pe.wait_ge(mix_lo, i)
                    n = keys_of(kind, b)
                    for j in range(n):
                        for h in range(2):
                            head = 2 * hp + h
                            d = slice(HD * head, HD * head + HD)
                            if kind == "C":
                                v = c_v[:, 0 if b is None else 1 + j, d]
                            elif kind == "A":
                                v = a_vx[:, 0, d] if b is None else a_vx[:, 1, d] if j == 2 else a_v[:, b, j, d]
                            else:
                                d = slice(HD * hp, HD * hp + HD)
                                v = d_v[:, 0, d] if b is None else d_v[:, NT, d] if j == n - 1 \
                                    else d_v[:, 1 + max(b - 1, 0) + j, d]
                            last = M.matmul(ps[64 * h:64 * h + 64, 3584:3584 + P], v,
                                            probs_t(i, pair)[:, h, P * j:P * j + P], start=j == 0, stop=j == n - 1)
                    last.then_inc(pv_done, 1)

                for j, (i, pair) in enumerate(todo):
                    score(i, pair)
                    if j >= 1:
                        turn(*todo[j - 1])
                    if j >= 2:
                        values(*todo[j - 2])
                turn(*todo[-1])
                values(*todo[-2])
                values(*todo[-1])
                did["pair"] += len(todo)

            pe.wait_ge(consts_set, 1)
            pe.wait_ge(x_in_dma, 32)
            for c in range(KC):
                transpose_step(("x", c), [(x_in[:, t, P * c:P * c + P], P * t) for t in range(NT)])
            pe.wait_ge(vec_dma, 16 * 6 * DEPTH)
            for l in range(DEPTH):
                transpose_step(("vec", l), [(vec_in[0:NVEC, l, :], 0)])
            pe.wait_ge(cond_ready, 1)
            for k in range(18):
                ada_tick(0, k)

            for l in range(DEPTH):
                U = 45 * l
                quiet()
                sums(l, "sum1")
                quiet()
                tick, first = iter(range(99)), 48 * l + 16
                project(l, U, "cq", wait_h=2 * l * KC)
                project(l, U + 1, "ckv")
                pe.wait_ge(st_normed, norm_at(l, "cq") + 1)
                for c in range(2):
                    transpose_step((l, "cq", c), [(cq_st[:, t, P * c:P * c + P], P * t) for t in range(NT)])
                pe.wait_ge(st_normed, norm_at(l, "ckv") + 1)
                pe.wait_ge(cache_dma, 64 * (l + 1))
                transpose_step((l, "ckv", 0), [(ckv_st[:, t, 0:P], P * t) for t in range(NT)]
                               + [(cache_in[:, 0:P], NTOK)])
                pe.wait_ge(t_dve, 3 * l + 2)
                project(l, U + 2, "uq")
                pe.wait_ge(t_dve, 3 * l + 3)
                project(l, U + 2, "ukv", NT + 1)
                pe.wait_ge(st_normed, norm_at(l, "q") + 1)
                for h in range(4):
                    transpose_step((l, "q", h), [(q_st[:, t, QK * h:QK * h + QK], P * t) for t in range(NT)])
                pe.wait_ge(st_normed, norm_at(l, "k") + 1)
                for h in range(4):
                    transpose_step((l, "k", h), [(k_st[:, t, h, :], P * t) for t in range(NT + 1)])
                quiet()
                attention(l, "C")
                quiet()
                tick, first = iter(range(99)), 48 * l + 32
                project(l, U + 3, "naq")
                project(l, U + 4, "nak")
                pe.wait_ge(st_normed, norm_at(l, "naq") + 1)
                for hp in range(2):
                    transpose_step((l, "naq", hp), [(st[:, 0, t, P * hp:P * hp + P], P * t) for t in range(NT)])
                project(l, U + 5, "nav")
                pe.wait_ge(st_normed, norm_at(l, "nak") + 1)
                for hp in range(2):
                    transpose_step((l, "nak", hp), [(st[:, 1, t, P * hp:P * hp + P], P * t) for t in range(NT)]
                                   + [(cache_in[:, 160 + P * hp:160 + P * hp + P], NTOK)])
                project(l, U + 6, "swq")
                project(l, U + 7, "swkv")
                pe.wait_ge(st_normed, norm_at(l, "swq") + 1)
                for hp in range(2):
                    transpose_step((l, "swq", hp), [(st[:, 1, t, P * hp:P * hp + P], P * t) for t in range(NT)])
                pe.wait_ge(st_normed, norm_at(l, "swkv") + 1)
                transpose_step((l, "swk", 0), [(st[:, 0, t, 0:P], P * t) for t in range(NT)]
                               + [(cache_in[:, 416:544], NTOK)])
                quiet()
                pe.wait_ge(w_lo_ready, U + 9)
                for c in range(2):
                    out = begin_acc((l, "pool", c))
                    w = [x[:, (U + 8) % 2, :].rearrange("p (k c) -> p k c", k=KC)[:, :, P * c:P * c + P] for x in (w_hi, w_lo)]
                    for k in range(KC):
                        last = three(out, (w[0][:, k, :], w[1][:, k, :]), (h_hi[:, k, :], h_lo[:, k, :]), k == 0, k == KC - 1)
                    last.then_inc(m_done, 1)
                pe.wait_ge(pool_w_dma, 64 * (l + 1))
                for c in range(2):
                    pe.wait_ge(pool_ready, 2 * l + c + 1)
                    out = begin_acc((l, "mix", c))
                    lat = PAD + CTX + 2 * PAD
                    cut = lat + HALF - CTX
                    M.matmul(out[:, 0, 0:CTX], pool_w[:, c, :], pool_in[:, c, PAD:PAD + CTX], start=True, stop=True)
                    M.matmul(out[:, 0, CTX:HALF], pool_w[:, c, :], pool_in[:, c, lat:cut], start=True, stop=True)
                    M.matmul(out[:, 1, :], pool_w[:, c, :], pool_in[:, c, cut:lat + LAT], start=True, stop=True)\
                        .then_inc(m_done, 1)
                quiet()
                pe.wait_ge(pads_set, l + 1)
                pe.wait_ge(av_dma, 16 * 33 * (l + 1))
                pe.wait_ge(ad_cache_dma, 32 * (l + 1))
                pe.wait_ge(dv_ready, l + 1)
                attention(l, "AD")
                quiet()
                first, tick = 48 * (l + 1), iter(range(99))
                for j in range(4):
                    n = U + 9 + j
                    pe.wait_ge(w_lo_ready, n + 1)
                    w = [x[:, n % 2, :].rearrange("p (k c) -> p k c", k=KC) for x in (w_hi, w_lo)]
                    for d in (2 * j, 2 * j + 1):
                        out = begin_acc((l, "wo", d))
                        c = P * (d % 2)
                        order = (4, 5, 0, 1, 2, 3, 6, 7)
                        for k in order:
                            last = three(out, (w[0][:, k, c:c + P], w[1][:, k, c:c + P]), (mixed(k, 0), mixed(k, 1)),
                                         k == order[0], k == order[-1])
                        last.then_inc(m_done, 1)
                        if l + 1 < DEPTH:
                            ada_tick(first, next(tick))
                            ada_tick(first, next(tick))
                if l + 1 < DEPTH:
                    ada_tick(first, next(tick))
                    ada_tick(first, next(tick))
                quiet()
                sums(l, "sum2")
                pe.wait_ge(h_lo_ready, (2 * l + 2) * KC)
                for n in range(13, 45):
                    u = units[U + n]
                    s = (U + n) % 2
                    g, j = u[2], u[3]
                    gg = l * GROUPS + g
                    pe.wait_ge(w_lo_ready, U + n + 1)
                    if u[1] == "w1":
                        w = [x[:, s, :].rearrange("p (k c) -> p k c", k=KC) for x in (w_hi, w_lo)]
                        for cc in range(2):
                            out = begin_acc((l, "z", g, 2 * j + cc))
                            c = P * cc
                            for k in range(KC):
                                last = three(out, (w[0][:, k, c:c + P], w[1][:, k, c:c + P]),
                                             (h_hi[:, k, :], h_lo[:, k, :]), k == 0, k == KC - 1)
                            last.then_inc(m_done, 1)
                    else:
                        w = [x[:, s, :].rearrange("p (k c) -> p k c", k=GC) for x in (w_hi, w_lo)]
                        pe.wait_ge(z_lo_ready, (gg + 1) * GC)
                        for dd in range(4):
                            d = 4 * j + dd
                            i = gg * KC + d
                            assert i == did["y"]
                            if i >= 2:
                                pe.wait_ge(y_read, i - 1)
                            b = 4 + 2 * (d % 2)
                            out = ps[:, 512 * b:512 * b + 1024].rearrange("p (a n) -> p a n", a=2)[:, :, 0:HALF]
                            c = P * dd
                            for k in range(GC):
                                slot = GC * (g % 2) + k
                                last = three(out, (w[0][:, k, c:c + P], w[1][:, k, c:c + P]),
                                             (z_hi[:, slot, :], z_lo[:, slot, :]), k == 0, k == GC - 1)
                            last.then_inc(y_done, 1)
                            did["y"] += 1
            quiet()
            for t in range(NT):
                transpose_step(("out", t), [(xT[:, c, P * t:P * t + P], P * c) for c in range(KC)])


def constants():
    t = np.arange(LAT)
    pos = (t // GRID_W, t % GRID_W)
    out = {}
    for name, width in (("rope_d", HD), ("rope_c", ROPE)):
        quarter = width // 4
        freqs = (THETA ** (-np.arange(quarter, dtype=np.float32) / np.float32(quarter))).astype(np.float32)
        tab = np.zeros((2, LAT, 2, 2, quarter), np.float32)
        for half in range(2):
            ang = pos[half].astype(np.float32)[:, None] * freqs
            tab[0, :, half, :, :] = np.cos(ang)[:, None, :]
            tab[1, :, half, 0, :] = -np.sin(ang)
            tab[1, :, half, 1, :] = np.sin(ang)
        out[name] = np.ascontiguousarray(tab.reshape(2, 4, P, width).transpose(2, 0, 1, 3))
    q, k = np.arange(P)[:, None], np.arange(P)[None, :]
    out["band"] = np.ascontiguousarray(np.stack([np.where(k >= q, 0, NEG), np.where(k <= q, 0, NEG)], 1).astype(np.float32))
    cols = np.zeros((P, 3, KCOLS), np.float32)
    for i, b in enumerate((0, 1, 3)):
        qcol = QC * b + np.arange(P) % QC
        start = np.clip(qcol - 8, 0, GRID_W - 16)[:, None]
        kcol = KEY_START[b] + np.arange(KCOLS)[None, :]
        cols[:, i] = np.where((kcol >= start) & (kcol < start + 16), 0, NEG)
    out["col_mask"] = cols
    rc = np.zeros((2, P, SEG), np.float32)
    for gi, w in enumerate(POOL_WINDOWS):
        for n, at in ((CTX, PAD), (LAT, PAD + CTX + 2 * PAD)):
            i = np.arange(n)
            count = np.clip(i - w // 2 + w, 0, n) - np.clip(i - w // 2, 0, n)
            rc[gi // 2, 64 * (gi % 2):64 * (gi % 2) + 64, at:at + n] = 1.0 / count.astype(np.float32)
    out["pool_rc"] = rc
    return out


_INS = ["x_prompt", "x_sample", "cache_na_k", "cache_na_v", "cache_mla_ckv", "cache_mla_kpe", "cache_swa_k",
        "cache_swa_v", "c", "c_ctx", "norm1", "norm2", "w_ada", "b_ada", "w_in", "w_out", "na_q_norm", "na_k_norm",
        "na_rpb", "pool_w", "pool_scale", "mla_q_a_norm", "mla_w_uq", "mla_kv_norm", "mla_w_ukv", "mla_q_norm",
        "mla_k_norm", "swa_q_norm", "swa_k_norm", "swa_sink", "mlp_w1", "mlp_w2"]
_OUTS = {"y_prompt": (1, CTX, D), "y_sample": (1, LAT, D), "na_k_new": (1, DEPTH, CTX, 4, HD),
         "na_v_new": (1, DEPTH, CTX, 4, HD), "mla_ckv_new": (1, DEPTH, CTX, KV_RANK),
         "mla_kpe_new": (1, DEPTH, CTX, ROPE), "swa_k_new": (1, DEPTH, CTX, 2, HD), "swa_v_new": (1, DEPTH, CTX, 2, HD)}


def kernel(**inputs):
    import concourse.bacc as bacc
    from concourse.bass_utils import run_bass_kernel_spmd

    nc = bacc.Bacc("TRN2", target_bir_lowering=False, num_devices=1)
    arrays = {f"in_{n}": np.ascontiguousarray(inputs[n]) for n in _INS}
    arrays["in_na_rpb"] = np.ascontiguousarray(inputs["na_rpb"][:, :, ::-1, ::-1])
    arrays.update({f"in_{n}": v for n, v in constants().items()})
    a = {n[3:]: nc.dram_tensor(n, v.shape, F32, kind="ExternalInput").ap() for n, v in arrays.items()}
    o = {n: nc.dram_tensor(f"out_{n}", s, F32, kind="ExternalOutput").ap() for n, s in _OUTS.items()}
    hybrid_kernel(nc, a, o)
    r = run_bass_kernel_spmd(nc, [arrays], core_ids=[0])
    return tuple(r.results[0][f"out_{n}"] for n in _OUTS)
```

```python
from contextlib import ExitStack

import numpy as np

import concourse.bass as bass
from concourse import mybir

ALU = mybir.AluOpType
ACT = mybir.ActivationFunctionType
AX_X = mybir.AxisListType.X
F32 = mybir.dt.float32
F32R = mybir.dt.float32r

P = 128
D = 1024
KC = D // P
DEPTH = 2
CTX, LAT, PAST = 128, 512, 128
NTOK = CTX + LAT
NT = NTOK // P
HALF = NTOK // 2
GRID_W = 64
ROWS = LAT // GRID_W
HD = 64
D_FF = 4 * D
EPS = 1e-6
NEG = -1e30
THETA = 10000.0
POOL_WINDOWS = (2, 4, 8, 16)
PAD = 8
SEG = CTX + LAT + 4 * PAD
KV_RANK, Q_RANK, NOPE, ROPE, DV = 128, 256, 64, 32, 64
QK = NOPE + ROPE
SCALE = HD ** -0.5
SCALE_C = QK ** -0.5

COLS = {"naq": 0, "nak": 256, "nav": 512, "pool": 768, "cq": 1024, "ckv": 1280, "swq": 1440, "swkv": 1696}
KPE = 1408
UW = 256
WU = KC * UW
GROUPS = 8
GC = D_FF // P // GROUPS
AR, AC = 4, 256
OWN, OVER_MIX, FIRST, ROOM = 2, 2, 6, 11


def ada_place(u):
    seq, k = u // 16 % 3, u % 16
    if u < FIRST:
        return OWN + OVER_MIX + u
    if seq == 0 and u >= 48 and k < ROOM:
        return OWN + OVER_MIX + FIRST + k
    return u % OWN if seq == 2 or (seq == 0 and u >= 48) else u % (OWN + OVER_MIX)


def ada_before(u):
    return [v for v in range(u) if ada_place(v) == ada_place(u)]

NCB, QC, KCOLS = 4, 16, 32
KEY_START = [min(max(min(max(QC * b - 8, 0), GRID_W - 16), 0), GRID_W - KCOLS) for b in range(NCB)]

R_ADA, R_N1, R_N2, R_PS, R_C, NVEC = 0, 48, 56, 64, 66, 82
SHIFT1, SCALE1, GATE1, SHIFT2, SCALE2, GATE2 = (8 * i for i in range(6))
ADA_GROUPS = 12
EARLY = 4

GAINS = {"na_q_norm": 64, "na_k_norm": 64, "swa_q_norm": 64, "swa_k_norm": 64, "mla_q_a_norm": 256,
         "mla_q_norm": 96, "mla_k_norm": 96, "mla_kv_norm": 128, "swa_sink": 4}
GAIN_AT = dict(zip(GAINS, np.cumsum([0, *GAINS.values()])[:-1].tolist()))
NGAIN = sum(GAINS.values())


def weight_units():
    out = []
    for l in range(DEPTH):
        out += [(l, n) for n in ("cq", "ckv", "up", "naq", "nak", "nav", "swq", "swkv", "pool")]
        out += [(l, "wo", j) for j in range(D // UW)]
        out += [(l, "w1", 0, j) for j in range(2)]
        for g in range(GROUPS):
            if g + 1 < GROUPS:
                out += [(l, "w1", g + 1, j) for j in range(2)]
            out += [(l, "w2", g, j) for j in range(2)]
    return out


def psum_steps():
    proj, trans, acc = [], [], []
    trans += [("x", c, "act") for c in range(KC)] + [("vec", l, "act") for l in range(DEPTH)]
    for l in range(DEPTH):
        acc += [(l, "sum1", "dve")]
        for n in ("cq", "ckv", "uq", "ukv", "naq", "nak", "nav", "swq", "swkv"):
            proj += [(l, n, t) for t in range(NT + (n == "ukv"))]
        trans += [(l, "cq", 0, "dve"), (l, "cq", 1, "dve"), (l, "ckv", 0, "dve")]
        trans += [(l, n, h, "act") for n in ("q", "k") for h in range(4)]
        trans += [(l, n, h, "act") for n in ("naq", "nak", "swq") for h in range(2)] + [(l, "swk", 0, "act")]
        acc += [(l, "pool", c, "act") for c in range(2)] + [(l, "mix", c, "dve") for c in range(2)]
        acc += [(l, "wo", d, "dve") for d in range(KC)] + [(l, "sum2", "dve")]
        acc += [(l, "z", g, c, "act") for g in range(GROUPS) for c in range(GC)]
    trans += [("out", t, "act") for t in range(NT)]
    return proj, trans, acc


def attention_pairs(kind):
    return [(kind, b, hp) for b in (None, 0, 1, 2, 3) for hp in range(2)]


def keys_of(kind, block):
    if block is None:
        return 1
    return {"C": 5, "A": 3, "D": 3 if block in (0, 3) else 4}[kind]


class Index:

    def __init__(self, steps):
        self.steps = steps
        self.at = {s[:-1]: i for i, s in enumerate(steps)}

    def last_reader(self, i):
        who = self.steps[i][-1]
        return who, sum(s[-1] == who for s in self.steps[:i + 1])


class Linked:

    def __init__(self, eng, own):
        self.eng, self.own, self.count = eng, own, {}

    def __call__(self, ins, sem=None):
        sem = self.own if sem is None else sem
        key = sem.name
        self.count[key] = self.count.get(key, 0) + 1
        ins.then_inc(sem, 1)
        self.eng.wait_ge(sem, self.count[key])


def hybrid_kernel(nc, a, o):
    units = weight_units()
    unit_at = {u: i for i, u in enumerate(units)}
    proj, trans, acc = psum_steps()
    proj_at = {s: i for i, s in enumerate(proj)}
    trans_ix, acc_ix = Index(trans), Index(acc)
    pairs = [(l, *p) for l in range(DEPTH) for kind in "CAD" for p in attention_pairs(kind)]
    pair_at = {p: i for i, p in enumerate(pairs)}

    def signals(i, h=1):
        before = sum(2 if p[1] == "C" else 1 for p in pairs[:i])
        return before + (h + 1 if pairs[i][1] == "C" else 1)

    xupd = []
    for l in range(DEPTH):
        xupd += [(l, "wo", d) for d in range(KC)] + [(l, "y", g, d) for g in range(GROUPS) for d in range(KC)]
    xupd_at = {s: i for i, s in enumerate(xupd)}

    base = (nc.sbuf_base + 63) // 32 * 32
    room = (nc.sbuf_usable_end - base) // 4

    def at(name, off, shape, dt=F32):
        size = int(np.prod(shape[1:]))
        assert off + size <= room, (name, off + size, room)
        return nc.alloc_sbuf_tensor_at(name, shape, dt, offset=base + 4 * off)

    top = [0]

    def sb(name, shape, dt=F32):
        size = (int(np.prod(shape[1:])) + 7) // 8 * 8
        top[0] += size
        return at(name, top[0] - size, shape, dt)

    xT = sb("xT", [P, KC, NTOK])
    h_hi = sb("h_hi", [P, KC, NTOK], F32R)
    h_lo = sb("h_lo", [P, KC, NTOK], F32R)
    w_raw = sb("w_raw", [P, 2, WU])
    w_hi = sb("w_hi", [P, 2, WU], F32R)
    w_lo = sb("w_lo", [P, 2, WU], F32R)
    ada_own = sb("ada_own", [P, OWN, AR, AC])
    ada_mix = at("ada_mix", top[0], [P, OVER_MIX, AR, AC])
    mixc_hi = sb("mixc_hi", [P, 2, NTOK], F32R)
    mixc_lo = sb("mixc_lo", [P, 2, NTOK], F32R)
    ident = sb("ident", [P, P])
    ones = sb("ones", [P, P])
    gains = sb("gains", [P, NGAIN])
    rope_d = sb("rope_d", [P, 2, 4, HD])
    rope_c = sb("rope_c", [P, 2, 4, ROPE])
    band = sb("band", [P, 2, P])
    col_mask = sb("col_mask", [P, 3, KCOLS])
    mod = sb("mod", [P, 2, 48, 2])
    vcol = sb("vcol", [P, DEPTH, NVEC])
    cond = sb("cond", [P, KC, 32])
    pool_w = sb("pool_w", [P, 2, P])
    cache_in = sb("cache_in", [P, 128 + 32 + 256 + 128])
    acol = sb("acol", [P, KC, 2])
    cexp = sb("cexp", [P, 16])
    hstat = sb("hstat", [P, 24])
    mx = sb("mx", [P, 2, 2])
    nb = sb("nb", [P, 2, 2])
    lsum = sb("lsum", [P, 2, 2])
    rinv = sb("rinv", [P, 2, 2])
    sink_e = sb("sink_e", [P, 2, 2])
    A0 = top[0]

    x_in = at("x_in", A0, [P, NT, D])
    vec_in = at("vec_in", A0 + NT * D, [P, DEPTH, P])
    rpb_in = at("rpb_in", A0 + 5376, [60, DEPTH, 64])
    ada_first = at("ada_first", A0 + 5504, [P, FIRST, AR, AC])
    ada_room = at("ada_room", A0, [P, ROOM, AR, AC])
    z_hi = at("z_hi", A0, [P, 2 * GC, NTOK], F32R)
    z_lo = at("z_lo", A0 + 5120, [P, 2 * GC, NTOK], F32R)
    z_relu = at("z_relu", A0 + 10240, [P, 2, NTOK])
    z_sq = at("z_sq", A0 + 11520, [P, 2, NTOK])
    sq = at("sq", A0 + 12800, [P, 2, NTOK])
    xr = at("xr", A0 + 14080, [P, 2, NTOK])
    hf = at("hf", A0 + 15360, [P, 2, NTOK])
    rstd = at("rstd", A0 + 12160, [P, NTOK])
    c_q = at("c_q", A0, [P, 4, NTOK])
    c_k = at("c_k", A0 + 2560, [P, 4, NTOK + PAST])
    c_v = at("c_v", A0 + 5632, [P, NT + 1, 256])
    T0 = A0 + 7168
    cq_st = at("cq_st", T0, [P, NT, Q_RANK])
    ckv_st = at("ckv_st", T0 + 1280, [P, NT, KV_RANK + ROPE])
    q_st = at("q_st", T0, [P, NT, 4 * QK])
    k_st = at("k_st", T0 + 2080, [P, NT + 1, 4, QK])
    cqT_hi = at("cqT_hi", T0 + 4384, [P, 2, NTOK], F32R)
    cqT_lo = at("cqT_lo", T0 + 5664, [P, 2, NTOK], F32R)
    ckvT_hi = at("ckvT_hi", T0 + 6944, [P, NTOK + PAST], F32R)
    ckvT_lo = at("ckvT_lo", T0 + 7712, [P, NTOK + PAST], F32R)
    sq_cq = at("sq_cq", T0 + 2080, [P, NT, Q_RANK])
    sq_up = at("sq_up", T0 + 4384, [P, (NT + 1) * 4 * QK])
    rope_tmp_c = at("rope_tmp_c", T0 + 8480, [P, 2, 4, 4, ROPE])
    pr_c = at("pr_c", T0, [P, 2, 2, NT * P])
    pt_c = at("pt_c", T0 + 2560, [P, 2, 2, NT * P])
    a_q = at("a_q", A0, [P, 4, NTOK])
    a_k = at("a_k", A0 + 2560, [P, 2, NTOK + PAST])
    a_v = at("a_v", A0 + 4096, [P, NCB, 2, 256])
    a_vx = at("a_vx", A0 + 6144, [P, 2, 256])
    a_bias = at("a_bias", A0 + 6656, [P, 8, 4, 48])
    d_q = at("d_q", A0 + 8192, [P, 4, NTOK])
    d_k = at("d_k", A0 + 10752, [P, NTOK + PAST])
    d_v = at("d_v", A0 + 11520, [P, NT + 1, P])
    T1 = A0 + 12288
    st = at("st", T1, [P, 2, NT, 256])
    sq_st = at("sq_st", T1 + 2560, [P, NT, 256])
    rope_tmp_q = at("rope_tmp_q", A0 + 8192, [P, 2, 4, 4, HD])
    rope_tmp_k = [at("rope_tmp_k0", T1 + 3904, [P, 4, 2, HD]), at("rope_tmp_k1", A0 + 10752, [P, 4, 2, HD])]
    pr_a = at("pr_a", T1, [P, 2, 2, 512])
    pt_a = at("pt_a", T1 + 2048, [P, 2, 2, 512])
    pool_in = at("pool_in", T1, [P, 2, SEG])
    pool_s = at("pool_s", T1 + 1344, [P, 2, SEG])
    pool_rc = at("pool_rc", T1 + 2688, [P, SEG])
    H_HI, H_LO = KC * NTOK, 2 * KC * NTOK
    pool_t0 = at("pool_t0", H_HI + 4 * NTOK, [P, SEG])
    pool_t1 = at("pool_t1", H_LO + 4 * NTOK, [P, SEG])
    pool_rc0 = at("pool_rc0", H_HI + 6 * NTOK, [P, SEG])
    ada_row = at("ada_row", A0 + 16704, [P, 512])
    y_out = at("y_out", A0, [P, 2, D])

    ctx = ExitStack()
    with ctx:
        ps = ctx.enter_context(nc.psum_tensor("ps", [P, 4096], F32))
        rpb_pad = nc.dram_tensor("rpb_pad", (DEPTH, 60, 64), F32).ap()
        nav_rows = nc.dram_tensor("nav_rows", (DEPTH, LAT, 256), F32).ap()

        def sem(name):
            return ctx.enter_context(nc.semaphore(name))

        x_in_dma, vec_dma, const_dma, gain_dma = sem("x_in_dma"), sem("vec_dma"), sem("const_dma"), sem("gain_dma")
        cache_dma, pool_w_dma = sem("cache_dma"), sem("pool_w_dma")
        w_dma = [sem("w_dma0"), sem("w_dma1")]
        ada_dma = [sem(f"ada_dma{i}") for i in range(OWN + OVER_MIX + FIRST + ROOM)]
        av_dma, nav_dma, ad_cache_dma, rpb_dma, bias_dma = (
            sem("av_dma"), sem("nav_dma"), sem("ad_cache_dma"), sem("rpb_dma"), sem("bias_dma"))
        rc_dma = [sem("rc_dma0"), sem("rc_dma1")]
        pool_ready = [sem("pool_ready0"), sem("pool_ready1")]
        rinv_ready = sem("rinv_ready")
        out_st0, out_st1, out_ckv = sem("out_st0"), sem("out_st1"), sem("out_ckv")
        out_y = [sem("out_y0"), sem("out_y1")]
        consts_set, pads_set = sem("consts_set"), sem("pads_set")
        pool_chain = sem("pool_chain")
        xr_ready, dv_ready = sem("xr_ready"), sem("dv_ready")
        t_done, p_done, m_done, y_done = sem("t_done"), sem("p_done"), sem("m_done"), sem("y_done")
        ada_used, ada_turned = sem("ada_used"), sem("ada_turned")
        scored, turned, pv_done = sem("scored"), sem("turned"), sem("pv_done")
        act_chain = sem("act_chain")
        w_hi_ready, p_read, t_act, m_act = sem("w_hi_ready"), sem("p_read"), sem("t_act"), sem("m_act")
        cond_exp, ada_rows, sq_ready, sqrt_ready = sem("cond_exp"), sem("ada_rows"), sem("sq_ready"), sem("sqrt_ready")
        h_hi_ready, st_sq, st_sqrt, t_hi = sem("h_hi_ready"), sem("st_sq"), sem("st_sqrt"), sem("t_hi")
        exp_done, pt_ready, mix_hi, mixp_hi, z_hi_ready, z_relu_ready = (
            sem("exp_done"), sem("pt_ready"), sem("mix_hi"), sem("mixp_hi"), sem("z_hi_ready"), sem("z_relu_ready"))
        dve_chain = sem("dve_chain")
        w_lo_ready, t_dve, m_dve, y_read = sem("w_lo_ready"), sem("t_dve"), sem("m_dve"), sem("y_read")
        cond_den, cond_ready, ada_reduced, mean_ready, rstd_ready = (
            sem("cond_den"), sem("cond_ready"), sem("ada_reduced"), sem("mean_ready"), sem("rstd_ready"))
        hf_ready, h_lo_ready, st_mean, st_normed = sem("hf_ready"), sem("h_lo_ready"), sem("st_mean"), sem("st_normed")
        kpe_copied = sem("kpe_copied")
        max_ready, p_normed, mix_lo, x_updated = sem("max_ready"), sem("p_normed"), sem("mix_lo"), sem("x_updated")
        z_sq_ready, z_lo_ready = sem("z_sq_ready"), sem("z_lo_ready")
        sum_used, pool_zeroed = sem("sum_used"), sem("pool_zeroed")

        def bank(b, n=512):
            return ps[:, 512 * b:512 * b + n]

        def trans_view(i, width):
            b = 2 if i % 2 == 0 else 6
            return ps[:, 512 * b:512 * b + width]

        def acc_banks(i):
            s = acc[i]
            if s[1] in ("pool", "mix"):
                return 4 * s[2]
            if s[1] in ("sum1", "sum2"):
                return 0
            return 2 * (s[-2] % 2)

        def acc_view(i):
            b = acc_banks(i)
            return ps[:, 512 * b:512 * b + 1024].rearrange("p (a n) -> p a n", a=2)[:, :, 0:HALF]

        def nav_tile(l, b, j):
            return bass.AP(nav_rows.tensor, offset=(l * LAT + 4 * j * GRID_W + KEY_START[b]) * 256,
                           ap=[[GRID_W * 256, 4], [256, 32], [1, 256]])

        def unit_width(n):
            return 1280 if units[n][1] == "up" else WU

        def dma_count(n):
            return 16 * (n // 2 + 1 + sum(units[m][1] == "up" for m in range(n % 2, n + 1, 2)))

        def wait_unit_done(eng, n):
            u = units[n]
            l, kind = u[0], u[1]
            if kind in ("w1", "w2"):
                g, j = u[2], u[3]
                if kind == "w1":
                    eng.wait_ge(m_done, acc_ix.at[(l, "z", g, 2 * j + 1)] + 1)
                else:
                    eng.wait_ge(y_done, (l * GROUPS + g) * KC + 4 * j + 4)
            elif kind == "wo":
                eng.wait_ge(m_done, acc_ix.at[(l, "wo", 2 * u[2] + 1)] + 1)
            elif kind == "pool":
                eng.wait_ge(m_done, acc_ix.at[(l, "pool", 1)] + 1)
            elif kind == "up":
                eng.wait_ge(p_done, proj_at[(l, "ukv", NT)] + 1)
            else:
                eng.wait_ge(p_done, proj_at[(l, kind, NT - 1)] + 1)

        NORMS = ("cq", "ckv", "q", "k", "naq", "nak", "swq", "swkv")

        def norm_at(l, n):
            return l * len(NORMS) + NORMS.index(n)

        def st_of(n):
            if n == "cq":
                return cq_st[:, :, :]
            if n == "ckv":
                return ckv_st[:, :, 0:KV_RANK]
            if n == "q":
                return q_st[:, :, :].rearrange("p t (h w) -> p (t h) w", w=QK)
            if n == "k":
                return k_st[:, :, :, :].rearrange("p t h w -> p (t h) w")
            b = {"naq": 0, "nak": 1, "nav": 0, "swq": 1, "swkv": 0}[n]
            if n == "swkv":
                return st[:, b, :, 0:128].rearrange("p t (h w) -> p t h w", w=HD)
            return st[:, b, :, :].rearrange("p t (h w) -> p (t h) w", w=HD)

        def sq_of(n):
            if n == "cq":
                return sq_cq[:, :, :]
            if n == "ckv":
                return sq_cq[:, :, 0:KV_RANK]
            if n == "q":
                return sq_up[:, 0:NT * 4 * QK].rearrange("p (g w) -> p g w", w=QK)
            if n == "k":
                return sq_up[:, :].rearrange("p (g w) -> p g w", w=QK)
            if n == "swkv":
                return sq_st[:, :, 0:128].rearrange("p t (h w) -> p t h w", w=HD)
            return sq_st[:, :, :].rearrange("p t (h w) -> p (t h) w", w=HD)

        def mixed(k, part):
            if k in (4, 5):
                return (mixc_hi, mixc_lo)[part][:, k - 4, :]
            return (h_hi, h_lo)[part][:, k, :]

        def mixed_at(l, pair):
            kind, b, hp = pair
            chunk = {"C": 4, "A": 0, "D": 6}[kind] + hp
            if b is None:
                return [mixed(chunk, p)[:, 0:CTX] for p in (0, 1)], bank(7, P)
            if kind == "A":
                dst = [mixed(chunk, p)[:, CTX:NTOK].rearrange("p (r c) -> p r c", r=ROWS)[:, :, QC * b:QC * b + QC]
                       for p in (0, 1)]
                return dst, bank(7, P).rearrange("p (r c) -> p r c", r=ROWS)
            return [mixed(chunk, p)[:, CTX + P * b:CTX + P * b + P] for p in (0, 1)], bank(7, P)

        def scores(i, pair):
            kind, b, _ = pair
            n = keys_of(kind, b) * P
            if kind == "C":
                return ps[:, 0:2048].rearrange("p (h n) -> p h n", h=2)[:, :, 0:n]
            off = 1024 * (i % 2)
            return ps[:, off:off + 1024].rearrange("p (h n) -> p h n", h=2)[:, :, 0:n]

        def probs(i, pair):
            kind, b, _ = pair
            return (pr_c if kind == "C" else pr_a)[:, i % 2, :, 0:keys_of(kind, b) * P]

        def probs_t(i, pair):
            kind, b, _ = pair
            return (pt_c if kind == "C" else pt_a)[:, i % 2, :, 0:keys_of(kind, b) * P]

        ada_slots = [x[:, i] for x, n in ((ada_own, OWN), (ada_mix, OVER_MIX), (ada_first, FIRST), (ada_room, ROOM))
                     for i in range(n)]

        def wait_ada(eng, u):
            eng.wait_ge(ada_dma[ada_place(u)], 16 * (len(ada_before(u)) + 1))

        def late_ticks(l, stage):
            cuts = ((0, 0, 9, 14, 18), (0, 8, 12, 16, 18))[min(l, 1)]
            return range(cuts[stage], cuts[stage + 1])

        TWO_BANKS = [(("turn", (k - 5) // 4) if k >= 5 and k % 4 == 1 else None, ("unit", k) if k < 16 else None)
                     for k in range(18)]
        ONE_BANK = [(("turn", k // 5), None) if k % 5 == 4 else (None, ("unit", k - k // 5)) for k in range(20)]

        def ada_banks(first):
            return (6, 6) if first % 48 == 32 else (4, 5)

        def ada_ticks_of(first):
            return ONE_BANK if first % 48 == 32 else TWO_BANKS

        def ada_unit_place(u):
            return u // 48, u % 48

        def window_sums(do, eng, l, c, s0, s1, rc):
            x = pool_in[:, c, :]

            do(eng.tensor_tensor(s0[:, 1:SEG], x[:, 0:SEG - 1], x[:, 1:SEG], ALU.add))
            do(eng.tensor_tensor(s1[:, 2:SEG - 1], s0[:, 1:SEG - 2], s0[:, 3:SEG], ALU.add))
            if c:
                do(eng.tensor_tensor(s0[:, 4:SEG - 3], s1[:, 2:SEG - 5], s1[:, 6:SEG - 1], ALU.add))
                do(eng.tensor_tensor(s1[:, 8:SEG - 7], s0[:, 4:SEG - 11], s0[:, 12:SEG - 3], ALU.add))
            eng.wait_ge(rc_dma[c], 16 * (l + 1))
            e = slice(PAD, SEG - PAD)
            do(eng.tensor_tensor(s0[0:64, e], s0[0:64, e], rc[0:64, e], ALU.mult))
            do(eng.tensor_tensor(s0[64:128, e], s1[64:128, e], rc[64:128, e], ALU.mult))
            do(eng.tensor_tensor(x[:, e], s0[:, e], x[:, e], ALU.subtract), pool_ready[c])

        block = ctx.enter_context(nc.Block())

        @block.sync
        def _(sp):
            def row(ap, n):
                return ap.rearrange("(r c) -> r c", r=n)

            def load_weights(n):
                if n >= len(units):
                    return
                if n >= 2:
                    sp.wait_ge(w_lo_ready, n - 1)
                u = units[n]
                l, kind = u[0], u[1]
                dst = w_raw[:, n % 2, :]
                if kind == "up":
                    sp.dma_start(dst[:, 0:768].rearrange("p (k c) -> p k c", k=2),
                                 a["mla_w_uq"][l].rearrange("(k p) c -> p k c", p=P)).then_inc(w_dma[n % 2], 16)
                    sp.dma_start(dst[:, 768:1280], a["mla_w_ukv"][l]).then_inc(w_dma[n % 2], 16)
                    return
                if kind == "w2":
                    g, j = u[2], u[3]
                    src = a["mlp_w2"][l, 512 * g:512 * g + 512, 512 * j:512 * j + 512]
                    sp.dma_start(dst.rearrange("p (k c) -> p k c", k=GC),
                                 src.rearrange("(k p) c -> p k c", p=P)).then_inc(w_dma[n % 2], 16)
                    return
                if kind == "wo":
                    src = a["w_out"][l, :, UW * u[2]:UW * u[2] + UW]
                elif kind == "w1":
                    c = 512 * u[2] + UW * u[3]
                    src = a["mlp_w1"][l, :, c:c + UW]
                else:
                    src = a["w_in"][l, :, COLS[kind]:COLS[kind] + UW]
                sp.dma_start(dst.rearrange("p (k c) -> p k c", k=KC),
                             src.rearrange("(k p) c -> p k c", p=P)).then_inc(w_dma[n % 2], 16)

            def load_ada(u):
                before, place = ada_before(u), ada_place(u)
                if before:
                    sp.wait_ge(ada_used, before[-1] + 1)
                k, c = 512 * (u % 2), AC * (u % 48 // 2)
                sp.dma_start(ada_slots[place], a["w_ada"][u // 48, k:k + 512, c:c + AC].rearrange("(k p) c -> p k c", p=P))\
                  .then_inc(ada_dma[place], 16)

            def load_adas(first, ks):
                for k in ks:
                    load_ada(first + k)

            sp.dma_start(x_in[:, 0, :], a["x_prompt"][0]).then_inc(x_in_dma, 16)
            sp.dma_start(x_in[:, 1:NT, :], a["x_sample"][0].rearrange("(t p) d -> p t d", p=P)).then_inc(x_in_dma, 16)
            for l in range(DEPTH):
                for r, src, n in ((R_ADA, a["b_ada"][l], 48), (R_N1, a["norm1"][l], 8), (R_N2, a["norm2"][l], 8),
                                  (R_PS, a["pool_scale"][l], 2), (R_C, a["c_ctx"], 8), (R_C + 8, a["c"][0], 8)):
                    sp.dma_start(vec_in[r:r + n, l, :], row(src, n)).then_inc(vec_dma, 16)
            load_adas(0, range(FIRST + OWN + OVER_MIX))
            sp.dma_start(rope_d[:, :, :, :], a["rope_d"]).then_inc(const_dma, 16)
            sp.dma_start(rope_c[:, :, :, :], a["rope_c"]).then_inc(const_dma, 16)
            sp.dma_start(band[:, :, :], a["band"]).then_inc(const_dma, 16)
            sp.dma_start(col_mask[:, :, :], a["col_mask"]).then_inc(const_dma, 16)
            load_weights(0)
            load_weights(1)
            load_adas(0, range(FIRST + OWN + OVER_MIX, 16))
            for l in range(DEPTH):
                U = 45 * l
                if l:
                    sp.wait_ge(st_normed, norm_at(l - 1, "swkv") + 1)
                    sp.wait_ge(t_done, trans_ix.at[(l - 1, "swk", 0)] + 1)
                    sp.wait_ge(p_normed, pair_at[(l - 1, "D", 3, 1)] + 1)
                    sp.wait_ge(m_done, acc_ix.at[(l - 1, "mix", 1)] + 1)
                for name, w in GAINS.items():
                    sp.dma_start(gains[:, GAIN_AT[name]:GAIN_AT[name] + w],
                                 a[name][l].unsqueeze(0).broadcast_to([P, w])).then_inc(gain_dma, 16)
                sp.dma_start(cache_in[:, 0:128], a["cache_mla_ckv"][0, l]).then_inc(cache_dma, 16)
                sp.dma_start(cache_in[:, 128:160], a["cache_mla_kpe"][0, l]).then_inc(cache_dma, 16)
                sp.dma_start(cache_in[:, 160:416], a["cache_na_k"][0, l].rearrange("t h d -> t (h d)")).then_inc(cache_dma, 16)
                sp.dma_start(cache_in[:, 416:544], a["cache_swa_k"][0, l].rearrange("t h d -> t (h d)")).then_inc(cache_dma, 16)
                sp.wait_ge(consts_set, 1)
                for g in range(4):
                    q = 64 * (g % 2)
                    sp.dma_start(pool_w[q:q + 64, g // 2, q:q + 64], a["pool_w"][l, g]).then_inc(pool_w_dma, 16)

                load_weights(U + 2)
                if l:
                    sp.wait_ge(m_done, acc_ix.at[(l - 1, "wo", KC - 1)] + 1)
                load_adas(48 * l + 16, range(8))
                load_weights(U + 3)
                load_adas(48 * l + 16, range(8, 16))
                for n in (4, 5, 6):
                    load_weights(U + n)
                sp.wait_ge(pv_done, pair_at[(l, "C", 3, 1)] + 1)
                sp.dma_start(a_vx[:, 1, :], a["cache_na_v"][0, l].rearrange("t h d -> t (h d)")).then_inc(ad_cache_dma, 16)
                sp.dma_start(d_v[:, NT, :], a["cache_swa_v"][0, l].rearrange("t h d -> t (h d)")).then_inc(ad_cache_dma, 16)
                sp.wait_ge(rpb_dma, 32 * DEPTH)
                for r in range(ROWS):
                    src = bass.AP(rpb_pad.tensor, offset=(60 * l + 4 * r) * 64, ap=[[1, QC], [64, 32], [1, 48]])
                    sp.dma_start(a_bias[QC * r:QC * r + QC, :, :, :].rearrange("p r h c -> p (r h) c"), src)\
                      .then_inc(bias_dma, 16)
                for n in (7, 8, 9, 10):
                    load_weights(U + n)
                load_adas(48 * l + 32, range(16))
                for n in (11, 12, 13, 14):
                    load_weights(U + n)
                    if l + 1 < DEPTH:
                        if n == 12:
                            sp.wait_ge(pv_done, pair_at[(l, "D", 3, 1)] + 1)
                            load_adas(48 * (l + 1), range(6))
                        if n == 13:
                            load_adas(48 * (l + 1), range(6, ROOM))
                if l + 1 < DEPTH:
                    load_adas(48 * (l + 1), range(ROOM, 16))
                for n in range(15, 47):
                    load_weights(U + n)
            for t in range(NT):
                sp.wait_ge(t_act, trans_ix.last_reader(trans_ix.at[("out", t)])[1])
                dst = o["y_prompt"][0] if t == 0 else o["y_sample"][0, P * (t - 1):P * t]
                sp.dma_start(dst, y_out[:, t % 2, :]).then_inc(out_y[t % 2], 16)
            sp.wait_ge(out_y[0], 16 * 3)
            sp.wait_ge(out_y[1], 16 * 2)
            sp.wait_ge(out_ckv, 32 * DEPTH)
            sp.wait_ge(out_st0, 48 * DEPTH)
            sp.wait_ge(out_st1, 16 * DEPTH)

        @block.gpsimd
        def _(pool):
            do = Linked(pool, pool_chain)
            do(pool.memset(ident[:, :], 0.0))
            do(pool.memset(ones[:, :], 1.0))
            do(pool.memset(cond[:, :, :], 0.0))
            do(pool.memset(pool_w[:, :, :], 0.0))
            do(pool.affine_select(out=ident[:, :], in_=ident[:, :], compare_op=ALU.not_equal, fill=1.0,
                                  base=0, pattern=[[-1, P]], channel_multiplier=1), consts_set)

            do(pool.memset(rpb_in[:, :, :], 0.0))
            for l in range(DEPTH):
                pool.dma_start(rpb_in[:, l, 16:47], a["na_rpb"][l].rearrange("r h c -> (r h) c")).then_inc(rpb_dma, 16)
            pool.wait_ge(rpb_dma, 16 * DEPTH)
            for l in range(DEPTH):
                pool.dma_start(rpb_pad[l], rpb_in[:, l, :]).then_inc(rpb_dma, 16)
            pool.wait_ge(rpb_dma, 32 * DEPTH)

            def scale_x(nrm):
                pool.wait_ge(rstd_ready, nrm + 1)
                for c in range(KC):
                    if c >= 2:
                        pool.wait_ge(hf_ready, KC * nrm + c - 1)
                    do(pool.tensor_tensor(xr[:, c % 2, :], xT[:, c, :], rstd[:, :], ALU.mult), xr_ready)

            def normalise(l, kinds):
                for pair in [p for kind in kinds for p in attention_pairs(kind)]:
                    i = pair_at[(l, *pair)]
                    pool.wait_ge(rinv_ready, i + 1)
                    v = probs(i, pair)
                    do(pool.tensor_tensor(v, v, rinv[:, i % 2, :].unsqueeze(2).broadcast_to(list(v.shape)), ALU.mult),
                       p_normed)

            for l in range(DEPTH):
                scale_x(2 * l)
                normalise(l, "C")
                pool.wait_ge(pv_done, pair_at[(l, "C", 3, 1)] + 1)
                do(pool.memset(a_q[64:128, 0:4:2, :], 0.0))
                do(pool.memset(a_q[0:64, 1:4:2, :], 0.0))
                pool.wait_ge(st_normed, norm_at(l, "swq") + 1)
                do(pool.memset(d_q[64:128, 0:2, :], 0.0))
                do(pool.memset(d_q[0:64, 2:4, :], 0.0), pads_set)
                pool.wait_ge(p_read, proj_at[(l, "swkv", NT - 1)] + 1)
                do(pool.tensor_copy(d_v[:, 0:NT, :], st[:, 0, :, 128:256]), dv_ready)
                pool.wait_ge(t_done, trans_ix.at[(l, "swk", 0)] + 1)
                pool.wait_ge(out_st0, 48 * (l + 1))
                pool.wait_ge(out_st1, 16 * (l + 1))
                for s, e in ((0, PAD), (PAD + CTX, CTX + 3 * PAD), (SEG - PAD, SEG)):
                    do(pool.memset(pool_in[:, :, s:e], 0.0), pool_zeroed if e == SEG else None)
                pool.wait_ge(m_act, acc_ix.last_reader(acc_ix.at[(l, "pool", 0)])[1])
                pool.wait_ge(m_done, acc_ix.at[(l, "pool", 1)] + 1)
                window_sums(do, pool, l, 0, pool_t0, pool_t1, pool_rc0)
                normalise(l, "AD")
                scale_x(2 * l + 1)

        @block.scalar
        def _(act):
            do = Linked(act, act_chain)

            def copy(out, in_, sem=None, scale=None):
                if scale is None:
                    do(nc.scalar.activation(out, in_, ACT.Copy), sem)
                else:
                    do(nc.scalar.activation(out, in_, ACT.Copy, scale=scale), sem)

            def split_hi(n):
                if n >= len(units):
                    return
                act.wait_ge(w_dma[n % 2], dma_count(n))
                if n >= 2:
                    wait_unit_done(act, n - 2)
                w = unit_width(n)
                copy(w_hi[:, n % 2, 0:w], w_raw[:, n % 2, 0:w], w_hi_ready)

            def ada_tick(first, k):
                unit = ada_ticks_of(first)[k][1]
                if unit and unit[1] % 4 == 3:
                    u = first + unit[1]
                    act.wait_ge(ada_used, u + 1)
                    if u >= 4:
                        act.wait_ge(ada_turned, u // 4)
                    copy(ada_row[:, :], bank(ada_banks(first)[0]), ada_rows)

            def ada_ticks(first, ks):
                for k in ks:
                    ada_tick(first, k)

            def squares(nrm, x_ready):
                for c in range(KC):
                    x_ready(c)
                    if c >= 2:
                        act.wait_ge(sum_used, (KC - 1) * nrm + c - 1)
                    do(nc.scalar.activation(sq[:, c % 2, :], xT[:, c, :], ACT.Square), sq_ready)
                l, name = nrm // 2, ("sum1", "sum2")[nrm % 2]
                act.wait_ge(m_dve, acc_ix.last_reader(acc_ix.at[(l, name)])[1])
                do(nc.scalar.activation(rstd[:, :], rstd[:, :], ACT.Sqrt), sqrt_ready)

            def h_halves(nrm, chunks=range(KC)):
                for c in chunks:
                    act.wait_ge(hf_ready, KC * nrm + c + 1)
                    copy(h_hi[:, c, :], hf[:, c % 2, :], h_hi_ready)

            def evacuate(l, n, t, dst, src_cols):
                i = proj_at[(l, n, t)]
                act.wait_ge(p_done, i + 1)
                src = bank(i % 2)
                if n == "ukv":
                    v = src.rearrange("p (h c) -> p h c", h=4)
                    copy(k_st[:, t, :, 0:NOPE], v[:, :, 0:NOPE])
                    copy(c_v[:, t, :].rearrange("p (h d) -> p h d", h=4), v[:, :, NOPE:NOPE + DV], p_read)
                else:
                    copy(dst, src[:, 0:src_cols], p_read)

            def square(l, n):
                i = norm_at(l, n)
                if i:
                    act.wait_ge(st_mean, i)
                do(nc.scalar.activation(sq_of(n), st_of(n), ACT.Square), st_sq)

            def root(l, n):
                act.wait_ge(st_mean, norm_at(l, n) + 1)
                do(nc.scalar.activation(hstat[:, :], hstat[:, :], ACT.Sqrt), st_sqrt)

            def turn(l, n, part):
                i = trans_ix.at[(l, n, part)]
                act.wait_ge(t_done, i + 1)
                if n == "cq":
                    copy(cqT_hi[:, part, :], trans_view(i, NTOK), t_hi)
                elif n == "ckv":
                    copy(ckvT_hi[:, :], trans_view(i, NTOK + PAST), t_hi)
                elif n == "q":
                    copy(c_q[0:QK, part, :], trans_view(i, NTOK)[0:QK], t_act)
                elif n == "k":
                    copy(c_k[0:QK, part, :], trans_view(i, NTOK + PAST)[0:QK], t_act)
                elif n == "naq":
                    v = trans_view(i, NTOK)
                    for h in range(2):
                        r = 64 * h
                        copy(a_q[r:r + 64, 2 * part + h, 0:CTX], v[r:r + 64, 0:CTX])
                        copy(a_q[r:r + 64, 2 * part + h, CTX:NTOK].rearrange("p (b r c) -> p r b c", b=NCB, r=ROWS),
                             v[r:r + 64, CTX:NTOK].rearrange("p (r b c) -> p r b c", r=ROWS, b=NCB), t_act if h else None)
                elif n == "swq":
                    v = trans_view(i, NTOK)
                    r = 64 * part
                    copy(d_q[r:r + 64, 2 * part, :], v[0:64])
                    copy(d_q[r:r + 64, 2 * part + 1, :], v[64:128], t_act)
                elif n == "nak":
                    copy(a_k[:, part, :], trans_view(i, NTOK + PAST), t_act)
                else:
                    copy(d_k[:, :], trans_view(i, NTOK + PAST), t_act)

            def attention(l, kind_list):
                todo = [(pair_at[(l, *p)], p) for kind in kind_list for p in attention_pairs(kind)]

                def exps(i, pair):
                    kind = pair[0]
                    act.wait_ge(max_ready, signals(i, 0))
                    if i >= 2:
                        act.wait_ge(turned, i - 1)
                    scale = SCALE_C if kind == "C" else SCALE
                    if kind == "D":
                        do(nc.scalar.activation(sink_e[:, i % 2, :], sink_e[:, i % 2, :], ACT.Exp))
                    for h in range(2):
                        act.wait_ge(max_ready, signals(i, h))
                        do(nc.scalar.activation(probs(i, pair)[:, h, :], scores(i, pair)[:, h, :], ACT.Exp,
                                                bias=nb[:, i % 2, h:h + 1], scale=scale,
                                                accum_out=lsum[:, i % 2, h:h + 1]),
                           exp_done if h or kind == "C" else None)

                def take_turned(i, pair):
                    act.wait_ge(turned, i + 1)
                    if i >= 2:
                        act.wait_ge(pv_done, i - 1)
                    dst, n = probs_t(i, pair), keys_of(pair[0], pair[1])
                    w = min(n, 4) * P
                    src = ps[:, 2048:3072].rearrange("p (h n) -> p h n", h=2)[:, :, 0:w]
                    if n == 5:
                        copy(dst[:, :, 0:w], src)
                        copy(dst[:, :, w:w + P], ps[:, 3072:3072 + 2 * P].rearrange("p (h n) -> p h n", h=2), pt_ready)
                    else:
                        copy(dst[:, :, 0:w], src, pt_ready)

                def take_out(i, pair):
                    act.wait_ge(pv_done, i + 1)
                    dst, src = mixed_at(l, pair)
                    copy(dst[0], src, mix_hi)

                for j in range(len(todo) + 3):
                    if kind_list == "AD" and j < 15:
                        ada_tick(48 * l + 32, j + 5)
                    if kind_list == "C" and j < len(todo):
                        exps(*todo[j])
                    if 2 <= j < len(todo) + 2:
                        take_turned(*todo[j - 2])
                    if j >= 3:
                        take_out(*todo[j - 3])
                    if kind_list == "AD" and j < len(todo):
                        exps(*todo[j])

            for c in range(KC):
                act.wait_ge(t_done, c + 1)
                copy(xT[:, c, :], trans_view(c, NTOK), t_act)
            for l in range(DEPTH):
                act.wait_ge(t_done, KC + l + 1)
                copy(vcol[:, l, :], trans_view(KC + l, NVEC), t_act)
            do(nc.scalar.activation(cexp[:, :], vcol[:, 0, R_C:NVEC], ACT.Exp, scale=-1.0), cond_exp)
            squares(0, lambda c: None)
            split_hi(0)
            ada_ticks(0, range(18))

            for l in range(DEPTH):
                U = 45 * l
                if l:
                    squares(2 * l, lambda c: act.wait_ge(y_read, (l * GROUPS - 1) * KC + c + 1))
                late = 48 * l + 16
                ada_ticks(late, late_ticks(l, 0))
                h_halves(2 * l)

                def unit(n, name, dst, cols, root_of=None, tiles=NT, split=True):
                    if split:
                        split_hi(U + n + 1)
                    for t in range(tiles):
                        evacuate(l, name, t, dst(t), cols)
                        if t == 1 and root_of:
                            root(l, root_of)

                unit(0, "cq", lambda t: cq_st[:, t, :], 256)
                square(l, "cq")
                unit(1, "ckv", lambda t: ckv_st[:, t, :], 160, "cq")
                square(l, "ckv")
                turn(l, "cq", 0)
                turn(l, "cq", 1)
                root(l, "ckv")
                ada_ticks(late, late_ticks(l, 1))
                turn(l, "ckv", 0)
                act.dma_start(o["mla_ckv_new"][0, l], ckv_st[:, 0, 0:KV_RANK]).then_inc(out_ckv, 16)
                act.dma_start(o["mla_kpe_new"][0, l], ckv_st[:, 0, KV_RANK:KV_RANK + ROPE]).then_inc(out_ckv, 16)
                act.wait_ge(out_ckv, 32 * (l + 1))
                act.wait_ge(kpe_copied, l + 1)
                unit(2, "uq", lambda t: q_st[:, t, :], 4 * QK)
                square(l, "q")
                unit(2, "ukv", lambda t: None, 0, "q", NT + 1, split=False)
                square(l, "k")
                ada_ticks(late, late_ticks(l, 2))
                for h in range(4):
                    turn(l, "q", h)
                root(l, "k")
                ada_ticks(late, late_ticks(l, 3))
                for h in range(4):
                    turn(l, "k", h)
                attention(l, "C")
                unit(3, "naq", lambda t: st[:, 0, t, :], 256)
                square(l, "naq")
                unit(4, "nak", lambda t: st[:, 1, t, :], 256, "naq")
                square(l, "nak")
                turn(l, "naq", 0)
                turn(l, "naq", 1)
                unit(5, "nav", lambda t: st[:, 0, t, :], 256, "nak")
                act.dma_start(nav_rows[l].rearrange("(t p) d -> p t d", p=P), st[:, 0, 1:NT, :]).then_inc(nav_dma, 16)
                act.dma_start(a_vx[:, 0, :], st[:, 0, 0, :]).then_inc(av_dma, 16)
                act.dma_start(o["na_v_new"][0, l].rearrange("t h d -> t (h d)"), st[:, 0, 0, :]).then_inc(out_st0, 16)
                turn(l, "nak", 0)
                turn(l, "nak", 1)
                act.wait_ge(nav_dma, 16 * (l + 1))
                for b in range(NCB):
                    for j in range(2):
                        act.dma_start(a_v[:, b, j, :], nav_tile(l, b, j)).then_inc(av_dma, 16)
                act.dma_start(o["na_k_new"][0, l].rearrange("t h d -> t (h d)"), st[:, 1, 0, :]).then_inc(out_st1, 16)
                act.wait_ge(out_st1, 16 * (l + 1))
                unit(6, "swq", lambda t: st[:, 1, t, :], 256)
                square(l, "swq")
                act.wait_ge(av_dma, 16 * (2 * NCB + 1) * (l + 1))
                act.wait_ge(out_st0, 48 * l + 16)
                unit(7, "swkv", lambda t: st[:, 0, t, :], 256, "swq")
                square(l, "swkv")
                turn(l, "swq", 0)
                turn(l, "swq", 1)
                root(l, "swkv")
                turn(l, "swk", 0)
                act.dma_start(o["swa_k_new"][0, l].rearrange("t h d -> t (h d)"), st[:, 0, 0, 0:128]).then_inc(out_st0, 16)
                act.dma_start(o["swa_v_new"][0, l].rearrange("t h d -> t (h d)"), st[:, 0, 0, 128:256]).then_inc(out_st0, 16)
                act.wait_ge(st_mean, norm_at(l, "swkv") + 1)
                act.dma_start(pool_rc[:, :], a["pool_rc"][1]).then_inc(rc_dma[1], 16)
                act.wait_ge(m_done, acc_ix.at[(l, "pool", 1)] + 1)
                act.dma_start(pool_rc0[:, :], a["pool_rc"][0]).then_inc(rc_dma[0], 16)
                split_hi(U + 9)
                act.wait_ge(pool_zeroed, l + 1)
                for c in range(2):
                    i = acc_ix.at[(l, "pool", c)]
                    act.wait_ge(m_done, i + 1)
                    v = acc_view(i)
                    lat = PAD + CTX + 2 * PAD
                    copy(pool_in[:, c, PAD:PAD + CTX], v[:, 0, 0:CTX])
                    copy(pool_in[:, c, lat:lat + HALF - CTX], v[:, 0, CTX:HALF])
                    copy(pool_in[:, c, lat + HALF - CTX:lat + LAT], v[:, 1, :], m_act)
                ada_ticks(48 * l + 32, range(5))
                for c in range(2):
                    i = acc_ix.at[(l, "mix", c)]
                    act.wait_ge(m_done, i + 1)
                    copy(h_hi[:, 2 + c, :].rearrange("p (a n) -> p a n", a=2), acc_view(i), mixp_hi,
                         scale=vcol[:, l, R_PS + c:R_PS + c + 1])
                attention(l, "AD")
                for j in range(4):
                    split_hi(U + 9 + j + 1)
                squares(2 * l + 1, lambda c: act.wait_ge(m_dve, acc_ix.last_reader(acc_ix.at[(l, "wo", c)])[1]))
                more = l + 1 < DEPTH
                ada_ticks(48 * (l + 1), range(8 * more))
                h_halves(2 * l + 1, range(4))
                ada_ticks(48 * (l + 1), range(8 * more, 12 * more))
                h_halves(2 * l + 1, range(4, KC))
                ada_ticks(48 * (l + 1), range(12 * more, 18 * more))
                for n in range(13, 45):
                    split_hi(U + n + 1)
                    u = units[U + n]
                    if u[1] == "w1":
                        g = u[2]
                        gg = l * GROUPS + g
                        for c in (2 * u[3], 2 * u[3] + 1):
                            zi = gg * GC + c
                            i = acc_ix.at[(l, "z", g, c)]
                            act.wait_ge(m_done, i + 1)
                            if zi >= 2:
                                act.wait_ge(z_sq_ready, zi - 1)
                            do(nc.scalar.activation(z_relu[:, c % 2, :].rearrange("p (a n) -> p a n", a=2),
                                                    acc_view(i), ACT.Relu), m_act)
                            if gg >= 2:
                                act.wait_ge(y_done, (gg - 1) * KC)
                            slot = GC * (g % 2) + c
                            do(nc.scalar.activation(z_hi[:, slot, :], z_relu[:, c % 2, :], ACT.Square), z_hi_ready)
            for t in range(NT):
                i = trans_ix.at[("out", t)]
                act.wait_ge(t_done, i + 1)
                if t >= 2:
                    act.wait_ge(out_y[t % 2], 16 * (t // 2))
                copy(y_out[:, t % 2, :], trans_view(i, D), t_act)

        @block.vector
        def _(dve):
            do = Linked(dve, dve_chain)
            V = nc.vector

            def f32(ap):
                return ap.bitcast(F32)

            def split_lo(n):
                if n >= len(units):
                    return
                dve.wait_ge(w_hi_ready, n + 1)
                w = unit_width(n)
                do(V.tensor_tensor(w_lo[:, n % 2, 0:w], w_raw[:, n % 2, 0:w], f32(w_hi[:, n % 2, 0:w]),
                                   ALU.subtract), w_lo_ready)

            def ada_tick(first, k):
                turned = ada_ticks_of(first)[k][0]
                if turned:
                    u = first + 4 * turned[1]
                    l, c = ada_unit_place(u)
                    dve.wait_ge(ada_turned, u // 4 + 1)
                    m = mod[:, l % 2, c:c + 4, :]
                    do(V.tensor_reduce(m, bank(ada_banks(first)[1]).rearrange("p (c j m) -> p c m j", c=4, j=4)[:, :, 0:2, :],
                                       AX_X, ALU.add), ada_reduced)
                    do(V.tensor_tensor(m, m, vcol[:, l, R_ADA + c:R_ADA + c + 4].unsqueeze(2).broadcast_to([P, 4, 2]),
                                       ALU.add))

            def ada_ticks(first, ks):
                for k in ks:
                    ada_tick(first, k)

            def mean(nrm):
                l, which = nrm // 2, nrm % 2
                i = acc_ix.at[(l, ("sum1", "sum2")[which])]
                dve.wait_ge(m_done, i + 1)
                do(V.tensor_scalar(rstd[:, :].rearrange("p (a n) -> p a n", a=2), acc_view(i), 1.0 / D, EPS,
                                   ALU.mult, ALU.add), m_dve)
                dve.wait_ge(sqrt_ready, nrm + 1)
                do(V.reciprocal(rstd[:, :], rstd[:, :]), rstd_ready)

            def h_of(nrm, between={}):
                l, which = nrm // 2, nrm % 2
                sc = (SCALE1, SCALE2)[which]
                sh = (SHIFT1, SHIFT2)[which]
                gain = vcol[:, l, (R_N1, R_N2)[which]:(R_N1, R_N2)[which] + KC].unsqueeze(2).broadcast_to([P, KC, 2])
                do(V.scalar_tensor_tensor(acol[:, :, :], mod[:, l % 2, sc:sc + KC, :], 1.0, gain, ALU.add, ALU.mult))

                def lo(c):
                    dve.wait_ge(h_hi_ready, KC * nrm + c + 1)
                    do(V.tensor_tensor(h_lo[:, c, :], hf[:, c % 2, :], f32(h_hi[:, c, :]), ALU.subtract), h_lo_ready)

                for c in range(KC):
                    if c in between:
                        between[c]()
                    dve.wait_ge(xr_ready, KC * nrm + c + 1)
                    for m, (s, e) in enumerate(((0, CTX), (CTX, NTOK))):
                        do(V.tensor_scalar(hf[:, c % 2, s:e], xr[:, c % 2, s:e], acol[:, c, m:m + 1],
                                           mod[:, l % 2, sh + c, m:m + 1], ALU.mult, ALU.add), hf_ready if m else None)
                    if c:
                        lo(c - 1)
                lo(KC - 1)

            def norm(l, n):
                gain, w, g = {"cq": ("mla_q_a_norm", 256, 5), "ckv": ("mla_kv_norm", 128, 5),
                              "q": ("mla_q_norm", QK, 20), "k": ("mla_k_norm", QK, 24),
                              "naq": ("na_q_norm", HD, 20), "nak": ("na_k_norm", HD, 20),
                              "swq": ("swa_q_norm", HD, 20), "swkv": ("swa_k_norm", HD, 10)}[n]
                x = st_of(n)
                dve.wait_ge(st_sq, norm_at(l, n) + 1)
                hs = hstat[:, 0:g]
                if n == "swkv":
                    hs = hs.rearrange("p (t h) -> p t h", h=2)
                do(V.tensor_reduce(hs, sq_of(n), AX_X, ALU.add))
                do(V.tensor_scalar(hstat[:, :], hstat[:, :], 1.0 / w, EPS, ALU.mult, ALU.add), st_mean)
                dve.wait_ge(st_sqrt, norm_at(l, n) + 1)
                do(V.reciprocal(hstat[:, :], hstat[:, :]))
                shape = list(x.shape)
                do(V.tensor_tensor(x, x, hs.unsqueeze(len(shape) - 1).broadcast_to(shape), ALU.mult))
                row = gains[:, GAIN_AT[gain]:GAIN_AT[gain] + w]
                for _ in shape[1:-1]:
                    row = row.unsqueeze(1)
                last = n in ("cq", "ckv", "naq", "nak")
                do(V.tensor_tensor(x, x, row.broadcast_to(shape), ALU.mult), st_normed if last else None)
                if last:
                    return
                if n == "q":
                    x = q_st[:, 1:NT, :].rearrange("p t (h c) -> p t h c", h=4)[:, :, :, NOPE:QK]
                elif n == "k":
                    x = k_st[:, 1:NT, :, NOPE:QK]
                elif n == "swq":
                    x = st[:, 1, 1:NT, :].rearrange("p t (h c) -> p t h c", h=4)
                else:
                    x = st[:, 0, 1:NT, 0:2 * HD].rearrange("p t (h c) -> p t h c", h=2)
                tab = rope_c if n in "qk" else rope_d
                tmp = [t[:, :, :, :] for t in rope_tmp_k] if n == "swkv" else [(rope_tmp_c if n in "qk" else rope_tmp_q)[:, k] for k in range(2)]
                cos, sin = [tab[:, k].unsqueeze(2).broadcast_to(list(x.shape)) for k in range(2)]
                do(V.tensor_tensor(tmp[0], x, cos, ALU.mult))
                for f in range(2):
                    for s in range(2):
                        w = x.shape[3] // 4
                        to, of = (2 * f + s) * w, (2 * f + 1 - s) * w
                        do(V.tensor_tensor(tmp[1][:, :, :, to:to + w], x[:, :, :, of:of + w], sin[:, :, :, to:to + w], ALU.mult))
                do(V.tensor_tensor(x, tmp[0], tmp[1], ALU.add), st_normed)

            def turn(l, n, part):
                i = trans_ix.at[(l, n, part)]
                dve.wait_ge(t_hi, 3 * l + {"cq": 0, "ckv": 2}[n] + part + 1)
                if n == "cq":
                    do(V.tensor_tensor(cqT_lo[:, part, :], trans_view(i, NTOK), f32(cqT_hi[:, part, :]),
                                       ALU.subtract), t_dve)
                else:
                    do(V.tensor_tensor(ckvT_lo[:, :], trans_view(i, NTOK + PAST), f32(ckvT_hi[:, :]),
                                       ALU.subtract), t_dve)

            def attention(l, kind_list):
                todo = [(pair_at[(l, *p)], p) for kind in kind_list for p in attention_pairs(kind)]

                def maxima(i, pair):
                    kind, b, hp = pair
                    s = scores(i, pair)
                    if kind == "C":
                        for h in range(2):
                            dve.wait_ge(scored, signals(i, h))
                            do(V.tensor_reduce(mx[:, i % 2, h:h + 1], s[:, h, :], AX_X, ALU.max))
                            do(V.tensor_scalar(nb[:, i % 2, h:h + 1], mx[:, i % 2, h:h + 1], -SCALE_C, None, ALU.mult),
                               max_ready)
                        return
                    dve.wait_ge(scored, signals(i))
                    if kind == "A" and b is not None:
                        for h in range(2):
                            v = s[:, h, 0:256].rearrange("p (r c) -> p r c", r=8)
                            off = KEY_START[b] - QC * b + 16
                            bias = bass.AP(a_bias[:, 0, 0, 0:1].tensor, ap=[[8 * 4 * 48, P], [-4 * 48, 8], [-1, KCOLS]],
                                           offset=(7 * 4 + 2 * hp + h) * 48 + 47 - off)
                            do(V.scalar_tensor_tensor(v, bias, 1.0 / SCALE, v, ALU.mult, ALU.add))
                        v = s[:, :, 0:256].rearrange("p h (r c) -> p h r c", r=8)
                        mask = col_mask[:, {0: 0, 1: 1, 2: 1, 3: 2}[b], :].unsqueeze(1).unsqueeze(1)
                        do(V.tensor_tensor(v, v, mask.broadcast_to([P, 2, 8, KCOLS]), ALU.add))
                    if kind == "D" and b is not None:
                        lo = max(b - 1, 0)
                        for blk, m in ((b - 1, 0), (b + 1, 1)):
                            if 0 <= blk < 4:
                                v = s[:, :, P * (blk - lo):P * (blk - lo) + P]
                                do(V.tensor_tensor(v, v, band[:, m, :].unsqueeze(1).broadcast_to([P, 2, P]), ALU.add))
                    do(V.tensor_reduce(mx[:, i % 2, :], s, AX_X, ALU.max))
                    if kind == "A":
                        do(V.tensor_scalar(nb[:, i % 2, :], mx[:, i % 2, :], -SCALE, None, ALU.mult), max_ready)
                    else:
                        sink = gains[:, GAIN_AT["swa_sink"] + 2 * hp:GAIN_AT["swa_sink"] + 2 * hp + 2]
                        do(V.scalar_tensor_tensor(mx[:, i % 2, :], mx[:, i % 2, :], SCALE, sink, ALU.mult, ALU.max))
                        do(V.tensor_scalar(nb[:, i % 2, :], mx[:, i % 2, :], -1.0, None, ALU.mult))
                        do(V.tensor_tensor(sink_e[:, i % 2, :], sink, mx[:, i % 2, :], ALU.subtract), max_ready)

                def reciprocals(i, pair):
                    dve.wait_ge(exp_done, signals(i))
                    if pair[0] == "D":
                        do(V.tensor_tensor(lsum[:, i % 2, :], lsum[:, i % 2, :], sink_e[:, i % 2, :], ALU.add))
                    do(V.reciprocal(rinv[:, i % 2, :], lsum[:, i % 2, :]), rinv_ready)

                def take_out(i, pair):
                    dve.wait_ge(mix_hi, i + 1)
                    dst, src = mixed_at(l, pair)
                    do(V.tensor_tensor(dst[1], src, f32(dst[0]), ALU.subtract), mix_lo)

                for j in range(len(todo) + 4):
                    if j >= 4:
                        take_out(*todo[j - 4])
                    if kind_list == "C" and 1 <= j < len(todo) + 1:
                        reciprocals(*todo[j - 1])
                    if j < len(todo):
                        maxima(*todo[j])
                    if kind_list == "AD" and 1 <= j < len(todo) + 1:
                        reciprocals(*todo[j - 1])
                    if kind_list == "AD" and j < 15:
                        ada_tick(48 * l + 32, j + 5)

            def add_gated(d, gate, v, sem):
                x = xT[:, d, :]
                for m, dst, src in ((0, x[:, 0:CTX], v[:, 0, 0:CTX]), (1, x[:, CTX:HALF], v[:, 0, CTX:HALF]),
                                    (1, x[:, HALF:NTOK], v[:, 1, :])):
                    last = dst.shape[1] == HALF
                    do(V.scalar_tensor_tensor(dst, src, gate[:, m:m + 1], dst, ALU.mult, ALU.add),
                       sem if last else None)

            dve.wait_ge(cond_exp, 1)
            dve.wait_ge(consts_set, 1)
            do(V.tensor_scalar(cexp[:, :], cexp[:, :], 1.0, None, ALU.add))
            do(V.reciprocal(cexp[:, :], cexp[:, :]))
            do(V.tensor_tensor(cond[:, :, 0:2].rearrange("p k m -> p m k"),
                               vcol[:, 0, R_C:NVEC].rearrange("p (m k) -> p m k", m=2),
                               cexp[:, :].rearrange("p (m k) -> p m k", m=2), ALU.mult), cond_ready)
            do(V.memset(hstat[:, :], 1.0))
            mean(0)
            split_lo(0)
            ada_ticks(0, range(18))
            dve.wait_ge(const_dma, 64)

            for l in range(DEPTH):
                U = 45 * l
                if l:
                    mean(2 * l)
                late = 48 * l + 16
                ada_ticks(late, late_ticks(l, 0))
                h_of(2 * l)
                dve.wait_ge(gain_dma, 16 * len(GAINS) * (l + 1))
                dve.wait_ge(cache_dma, 64 * (l + 1))
                split_lo(U + 1)
                split_lo(U + 2)
                norm(l, "cq")
                turn(l, "cq", 0)
                turn(l, "cq", 1)
                norm(l, "ckv")
                ada_ticks(late, late_ticks(l, 1))
                turn(l, "ckv", 0)
                do(V.tensor_copy(k_st[:, 0:NT, :, NOPE:QK],
                                 ckv_st[:, :, KV_RANK:KV_RANK + ROPE].unsqueeze(2).broadcast_to([P, NT, 4, ROPE])))
                do(V.tensor_copy(k_st[:, NT, :, NOPE:QK],
                                 cache_in[:, 128:160].unsqueeze(1).broadcast_to([P, 4, ROPE])), kpe_copied)
                split_lo(U + 3)
                norm(l, "q")
                ada_ticks(late, late_ticks(l, 2))
                norm(l, "k")
                ada_ticks(late, late_ticks(l, 3))
                attention(l, "C")
                split_lo(U + 4)
                split_lo(U + 5)
                norm(l, "naq")
                split_lo(U + 6)
                norm(l, "nak")
                split_lo(U + 7)
                split_lo(U + 8)
                norm(l, "swq")
                norm(l, "swkv")
                split_lo(U + 9)
                dve.wait_ge(m_act, acc_ix.last_reader(acc_ix.at[(l, "pool", 1)])[1])
                window_sums(do, dve, l, 1, pool_s[:, 0, :], pool_s[:, 1, :], pool_rc)
                ada_ticks(48 * l + 32, range(5))
                for c in range(2):
                    i = acc_ix.at[(l, "mix", c)]
                    dve.wait_ge(mixp_hi, 2 * l + c + 1)
                    do(V.scalar_tensor_tensor(h_lo[:, 2 + c, :].rearrange("p (a n) -> p a n", a=2), acc_view(i),
                                              vcol[:, l, R_PS + c:R_PS + c + 1],
                                              f32(h_hi[:, 2 + c, :]).rearrange("p (a n) -> p a n", a=2),
                                              ALU.mult, ALU.subtract), m_dve)
                dve.wait_ge(bias_dma, 16 * ROWS * (l + 1))
                attention(l, "AD")
                for j in range(4):
                    split_lo(U + 9 + j + 1)
                    for d in (2 * j, 2 * j + 1):
                        i = acc_ix.at[(l, "wo", d)]
                        dve.wait_ge(m_done, i + 1)
                        add_gated(d, mod[:, l % 2, GATE1 + d, :], acc_view(i), m_dve)
                mean(2 * l + 1)
                more = l + 1 < DEPTH
                h_of(2 * l + 1, {0: lambda: ada_ticks(48 * (l + 1), range(6 * more)),
                                 4: lambda: ada_ticks(48 * (l + 1), range(6 * more, 14 * more))})
                ada_ticks(48 * (l + 1), range(14 * more, 18 * more))
                for n in range(13, 45):
                    split_lo(U + n + 1)
                    u = units[U + n]
                    g = u[2]
                    gg = l * GROUPS + g
                    if u[1] == "w1":
                        for c in (2 * u[3], 2 * u[3] + 1):
                            dve.wait_ge(m_act, acc_ix.last_reader(acc_ix.at[(l, "z", g, c)])[1])
                            do(V.tensor_tensor(z_sq[:, c % 2, :], z_relu[:, c % 2, :], z_relu[:, c % 2, :],
                                               ALU.mult), z_sq_ready)
                            dve.wait_ge(z_hi_ready, gg * GC + c + 1)
                            slot = GC * (g % 2) + c
                            do(V.tensor_tensor(z_lo[:, slot, :], z_sq[:, c % 2, :], f32(z_hi[:, slot, :]),
                                               ALU.subtract), z_lo_ready)
                    else:
                        for d in range(4 * u[3], 4 * u[3] + 4):
                            dve.wait_ge(y_done, gg * KC + d + 1)
                            b = 4 + 2 * (d % 2)
                            v = ps[:, 512 * b:512 * b + 1024].rearrange("p (a n) -> p a n", a=2)[:, :, 0:HALF]
                            add_gated(d, mod[:, l % 2, GATE2 + d, :], v, y_read)

        @block.tensor
        def _(pe):
            M = nc.tensor
            did = {"p": 0, "t": 0, "m": 0, "y": 0, "ada": 0, "pair": 0}

            def quiet():
                if did["p"]:
                    pe.wait_ge(p_read, did["p"])
                for n, ix, by_act, by_dve in (("t", trans_ix, t_act, t_dve), ("m", acc_ix, m_act, m_dve)):
                    for who, s in (("act", by_act), ("dve", by_dve)):
                        count = sum(x[-1] == who for x in ix.steps[:did[n]])
                        if count:
                            pe.wait_ge(s, count)
                if did["y"]:
                    pe.wait_ge(y_read, did["y"])
                if did["ada"]:
                    pe.wait_ge(ada_rows, did["ada"] // 4)
                if did["pair"]:
                    pe.wait_ge(pt_ready, did["pair"])
                    pe.wait_ge(mix_lo, did["pair"])

            def wait_read(ix, i, by_act, by_dve):
                who, count = ix.last_reader(i)
                pe.wait_ge(by_act if who == "act" else by_dve, count)

            def transpose_step(key, pieces):
                i = trans_ix.at[key]
                assert i == did["t"], (key, i, did)
                if i >= 2:
                    wait_read(trans_ix, i - 2, t_act, t_dve)
                v = trans_view(i, 1024)
                for src, c in pieces:
                    last = M.transpose(v[0:src.shape[1], c:c + src.shape[0]], src,
                                       ident[0:src.shape[0], 0:src.shape[0]])
                last.then_inc(t_done, 1)
                did["t"] += 1

            def begin_acc(key):
                i = acc_ix.at[key]
                assert i == did["m"], (key, i, did)
                before = [j for j in range(i) if acc_banks(j) == acc_banks(i)]
                if before:
                    wait_read(acc_ix, before[-1], m_act, m_dve)
                did["m"] += 1
                return acc_view(i)

            def three(out, w_pair, x_pair, first, last):
                w, wl = w_pair
                x, xl = x_pair
                for n, (lhs, rhs) in enumerate(((w, x), (w, xl), (wl, x))):
                    for a_ in range(2):
                        ins = M.matmul(out[:, a_, :], lhs, rhs[:, HALF * a_:HALF * a_ + HALF],
                                       start=first and n == 0, stop=last and n == 2)
                return ins

            def ada_tick(first, k):
                turned, unit = ada_ticks_of(first)[k]
                b_acc, b_turn = ada_banks(first)
                if turned:
                    q = first // 4 + turned[1]
                    pe.wait_ge(ada_rows, q + 1)
                    if q:
                        pe.wait_ge(ada_reduced, q)
                    for j in range(4):
                        last = M.transpose(bank(b_turn)[:, P * j:P * j + P], ada_row[:, P * j:P * j + P], ident[:, :])
                    last.then_inc(ada_turned, 1)
                if unit:
                    u = first + unit[1]
                    wait_ada(pe, u)
                    if u % 4 == 0 and u:
                        pe.wait_ge(ada_rows, u // 4)
                        if b_acc == b_turn and unit[1]:
                            pe.wait_ge(ada_reduced, u // 4)
                    c = 512 * b_acc + AC * (u % 4 // 2)
                    for j in range(AR):
                        last = M.matmul(ps[32 * j:32 * j + 32, c:c + AC], cond[:, AR * (u % 2) + j, :],
                                        ada_slots[ada_place(u)][:, j, :], start=u % 2 == 0, stop=u % 2 == 1,
                                        skip_group_check=True)
                    last.then_inc(ada_used, 1)
                    did["ada"] += 1

            def ada_ticks(first, ks):
                for k in ks:
                    ada_tick(first, k)

            def sums(l, which):
                nrm = 2 * l + (which == "sum2")
                out = begin_acc((l, which))
                for c in range(KC):
                    pe.wait_ge(sq_ready, KC * nrm + c + 1)
                    for a_ in range(2):
                        last = M.matmul(out[:, a_, :], ones[:, :], sq[:, c % 2, HALF * a_:HALF * a_ + HALF],
                                        start=c == 0, stop=c == KC - 1)
                    last.then_inc(sum_used if c < KC - 1 else m_done, 1)

            def project(l, n, name, tiles=NT, wait_h=None):
                s = n % 2
                pe.wait_ge(w_lo_ready, n + 1)
                for t in range(tiles):
                    i = proj_at[(l, name, t)]
                    assert i == did["p"]
                    if i >= 2:
                        pe.wait_ge(p_read, i - 1)
                    tok = slice(P * t, P * t + P)
                    if name == "uq":
                        w = [x[:, s, 0:768].rearrange("p (k c) -> p k c", k=2) for x in (w_hi, w_lo)]
                        x, cols, kk = (cqT_hi[:, :, tok], cqT_lo[:, :, tok]), 4 * QK, 2
                    elif name == "ukv":
                        w = [x[:, s, 768:1280].rearrange("p (k c) -> p k c", k=1) for x in (w_hi, w_lo)]
                        x = [y[:, tok].unsqueeze(1) for y in (ckvT_hi, ckvT_lo)]
                        cols, kk = 512, 1
                    else:
                        w = [x[:, s, :].rearrange("p (k c) -> p k c", k=KC) for x in (w_hi, w_lo)]
                        x, cols, kk = (h_hi[:, :, tok], h_lo[:, :, tok]), UW, KC
                    for k in range(kk):
                        if wait_h is not None and t == 0:
                            pe.wait_ge(h_lo_ready, wait_h + k + 1)
                        for q, (p, r) in enumerate(((0, 0), (1, 0), (0, 1))):
                            last = M.matmul(bank(i % 2)[:, 0:cols], x[p][:, k, :], w[r][:, k, :],
                                            start=k == 0 and q == 0, stop=k == kk - 1 and q == 2)
                    last.then_inc(p_done, 1)
                    did["p"] += 1

            def attention(l, kind_list):
                todo = [(pair_at[(l, *p)], p) for kind in kind_list for p in attention_pairs(kind)]

                def score(i, pair):
                    kind, b, hp = pair
                    if kind != "C" and i - 2 >= todo[0][0]:
                        pe.wait_ge(exp_done, signals(i - 2))
                    out = scores(i, pair)
                    for h in range(2):
                        if kind == "C" and i > todo[0][0]:
                            pe.wait_ge(exp_done, signals(i - 1, h))
                        head = 2 * hp + h
                        q = slice(0, P) if b is None else slice(CTX + P * b, CTX + P * b + P)
                        if kind == "C":
                            keys = [(0, c_k[0:QK, head, 0:P])] if b is None else \
                                [(0, c_k[0:QK, head, CTX:CTX + 512]), (512, c_k[0:QK, head, CTX + 512:CTX + 640])]
                            lhs = c_q[0:QK, head, q]
                        elif kind == "A":
                            lhs = a_q[:, head, q]
                            keys = [(0, a_k[:, hp, 0:P])]
                            if b is not None:
                                s = KEY_START[b]
                                loc = a_k[:, hp, CTX:NTOK].rearrange("p (r c) -> p r c", r=ROWS)[:, :, s:s + KCOLS]
                                keys = [(0, loc), (256, a_k[:, hp, NTOK:NTOK + PAST])]
                        else:
                            lhs = d_q[:, head, q]
                            keys = [(0, d_k[:, 0:P])]
                            if b is not None:
                                s, e = CTX + P * max(b - 1, 0), CTX + P * min(b + 2, 4)
                                keys = [(0, d_k[:, s:e]), (e - s, d_k[:, NTOK:NTOK + PAST])]
                        for n, (c, rhs) in enumerate(keys):
                            width = int(np.prod(rhs.shape[1:]))
                            dst = out[:, h, c:c + width]
                            if len(rhs.shape) == 3:
                                dst = dst.rearrange("p (r c) -> p r c", r=ROWS)
                            last = M.matmul(dst, lhs, rhs, start=True, stop=True, skip_group_check=True)
                        if h or kind == "C":
                            last.then_inc(scored, 1)

                def turn(i, pair):
                    pe.wait_ge(p_normed, i + 1)
                    if i > todo[0][0]:
                        pe.wait_ge(pt_ready, i)
                    for h in range(2):
                        for j in range(keys_of(pair[0], pair[1])):
                            c = 2048 + 512 * h + P * j if j < 4 else 3072 + P * h
                            last = M.transpose(ps[:, c:c + P], probs(i, pair)[:, h, P * j:P * j + P], ident[:, :])
                    last.then_inc(turned, 1)

                def values(i, pair):
                    kind, b, hp = pair
                    pe.wait_ge(pt_ready, i + 1)
                    if i > todo[0][0]:
                        pe.wait_ge(mix_lo, i)
                    n = keys_of(kind, b)
                    for j in range(n):
                        for h in range(2):
                            head = 2 * hp + h
                            d = slice(HD * head, HD * head + HD)
                            if kind == "C":
                                v = c_v[:, 0 if b is None else 1 + j, d]
                            elif kind == "A":
                                v = a_vx[:, 0, d] if b is None else a_vx[:, 1, d] if j == 2 else a_v[:, b, j, d]
                            else:
                                d = slice(HD * hp, HD * hp + HD)
                                v = d_v[:, 0, d] if b is None else d_v[:, NT, d] if j == n - 1 \
                                    else d_v[:, 1 + max(b - 1, 0) + j, d]
                            last = M.matmul(ps[64 * h:64 * h + 64, 3584:3584 + P], v,
                                            probs_t(i, pair)[:, h, P * j:P * j + P], start=j == 0, stop=j == n - 1)
                    last.then_inc(pv_done, 1)

                for j in range(len(todo) + 3):
                    if j < len(todo):
                        score(*todo[j])
                    if kind_list == "AD" and j < 15:
                        ada_tick(48 * l + 32, j + 5)
                    if 2 <= j < len(todo) + 2:
                        turn(*todo[j - 2])
                    if j >= 3:
                        values(*todo[j - 3])
                did["pair"] += len(todo)

            pe.wait_ge(consts_set, 1)
            pe.wait_ge(x_in_dma, 32)
            for c in range(KC):
                transpose_step(("x", c), [(x_in[:, t, P * c:P * c + P], P * t) for t in range(NT)])
            pe.wait_ge(vec_dma, 16 * 6 * DEPTH)
            for l in range(DEPTH):
                transpose_step(("vec", l), [(vec_in[0:NVEC, l, :], 0)])
            sums(0, "sum1")
            pe.wait_ge(cond_ready, 1)
            ada_ticks(0, range(18))

            for l in range(DEPTH):
                U = 45 * l
                quiet()
                if l:
                    sums(l, "sum1")
                    quiet()
                late = 48 * l + 16
                ada_ticks(late, late_ticks(l, 0))
                project(l, U, "cq", wait_h=2 * l * KC)
                project(l, U + 1, "ckv")
                pe.wait_ge(st_normed, norm_at(l, "cq") + 1)
                for c in range(2):
                    transpose_step((l, "cq", c), [(cq_st[:, t, P * c:P * c + P], P * t) for t in range(NT)])
                ada_ticks(late, late_ticks(l, 1))
                pe.wait_ge(st_normed, norm_at(l, "ckv") + 1)
                pe.wait_ge(cache_dma, 64 * (l + 1))
                transpose_step((l, "ckv", 0), [(ckv_st[:, t, 0:P], P * t) for t in range(NT)]
                               + [(cache_in[:, 0:P], NTOK)])
                pe.wait_ge(t_dve, 3 * l + 2)
                project(l, U + 2, "uq")
                pe.wait_ge(t_dve, 3 * l + 3)
                project(l, U + 2, "ukv", NT + 1)
                ada_ticks(late, late_ticks(l, 2))
                pe.wait_ge(st_normed, norm_at(l, "q") + 1)
                for h in range(4):
                    transpose_step((l, "q", h), [(q_st[:, t, QK * h:QK * h + QK], P * t) for t in range(NT)])
                ada_ticks(late, late_ticks(l, 3))
                pe.wait_ge(st_normed, norm_at(l, "k") + 1)
                for h in range(4):
                    transpose_step((l, "k", h), [(k_st[:, t, h, :], P * t) for t in range(NT + 1)])
                quiet()
                attention(l, "C")
                quiet()
                project(l, U + 3, "naq")
                project(l, U + 4, "nak")
                pe.wait_ge(st_normed, norm_at(l, "naq") + 1)
                for hp in range(2):
                    transpose_step((l, "naq", hp), [(st[:, 0, t, P * hp:P * hp + P], P * t) for t in range(NT)])
                project(l, U + 5, "nav")
                pe.wait_ge(st_normed, norm_at(l, "nak") + 1)
                for hp in range(2):
                    transpose_step((l, "nak", hp), [(st[:, 1, t, P * hp:P * hp + P], P * t) for t in range(NT)]
                                   + [(cache_in[:, 160 + P * hp:160 + P * hp + P], NTOK)])
                project(l, U + 6, "swq")
                project(l, U + 7, "swkv")
                pe.wait_ge(st_normed, norm_at(l, "swq") + 1)
                for hp in range(2):
                    transpose_step((l, "swq", hp), [(st[:, 1, t, P * hp:P * hp + P], P * t) for t in range(NT)])
                quiet()
                pe.wait_ge(w_lo_ready, U + 9)
                for c in range(2):
                    out = begin_acc((l, "pool", c))
                    w = [x[:, (U + 8) % 2, :].rearrange("p (k c) -> p k c", k=KC)[:, :, P * c:P * c + P] for x in (w_hi, w_lo)]
                    for k in range(KC):
                        last = three(out, (w[0][:, k, :], w[1][:, k, :]), (h_hi[:, k, :], h_lo[:, k, :]), k == 0, k == KC - 1)
                    last.then_inc(m_done, 1)
                pe.wait_ge(st_normed, norm_at(l, "swkv") + 1)
                transpose_step((l, "swk", 0), [(st[:, 0, t, 0:P], P * t) for t in range(NT)]
                               + [(cache_in[:, 416:544], NTOK)])
                pe.wait_ge(pool_w_dma, 64 * (l + 1))
                wait_read(trans_ix, trans_ix.at[(l, "swk", 0)], t_act, t_dve)
                ada_ticks(48 * l + 32, range(5))
                for c in range(2):
                    pe.wait_ge(pool_ready[c], l + 1)
                    out = begin_acc((l, "mix", c))
                    lat = PAD + CTX + 2 * PAD
                    cut = lat + HALF - CTX
                    M.matmul(out[:, 0, 0:CTX], pool_w[:, c, :], pool_in[:, c, PAD:PAD + CTX], start=True, stop=True)
                    M.matmul(out[:, 0, CTX:HALF], pool_w[:, c, :], pool_in[:, c, lat:cut], start=True, stop=True)
                    M.matmul(out[:, 1, :], pool_w[:, c, :], pool_in[:, c, cut:lat + LAT], start=True, stop=True)\
                        .then_inc(m_done, 1)
                quiet()
                pe.wait_ge(pads_set, l + 1)
                pe.wait_ge(av_dma, 16 * (2 * NCB + 1) * (l + 1))
                pe.wait_ge(ad_cache_dma, 32 * (l + 1))
                pe.wait_ge(dv_ready, l + 1)
                attention(l, "AD")
                quiet()
                for j in range(4):
                    n = U + 9 + j
                    pe.wait_ge(w_lo_ready, n + 1)
                    w = [x[:, n % 2, :].rearrange("p (k c) -> p k c", k=KC) for x in (w_hi, w_lo)]
                    for d in (2 * j, 2 * j + 1):
                        out = begin_acc((l, "wo", d))
                        c = P * (d % 2)
                        order = (4, 5, 0, 1, 2, 3, 6, 7)
                        for k in order:
                            last = three(out, (w[0][:, k, c:c + P], w[1][:, k, c:c + P]), (mixed(k, 0), mixed(k, 1)),
                                         k == order[0], k == order[-1])
                        last.then_inc(m_done, 1)
                quiet()
                sums(l, "sum2")
                if l + 1 < DEPTH:
                    ada_ticks(48 * (l + 1), range(18))
                for n in range(13, 45):
                    u = units[U + n]
                    s = (U + n) % 2
                    g, j = u[2], u[3]
                    gg = l * GROUPS + g
                    pe.wait_ge(w_lo_ready, U + n + 1)
                    if u[1] == "w1":
                        w = [x[:, s, :].rearrange("p (k c) -> p k c", k=KC) for x in (w_hi, w_lo)]
                        for cc in range(2):
                            out = begin_acc((l, "z", g, 2 * j + cc))
                            c = P * cc
                            for k in range(KC):
                                if (g, j, cc) == (0, 0, 0):
                                    pe.wait_ge(h_lo_ready, (2 * l + 1) * KC + k + 1)
                                last = three(out, (w[0][:, k, c:c + P], w[1][:, k, c:c + P]),
                                             (h_hi[:, k, :], h_lo[:, k, :]), k == 0, k == KC - 1)
                            last.then_inc(m_done, 1)
                    else:
                        w = [x[:, s, :].rearrange("p (k c) -> p k c", k=GC) for x in (w_hi, w_lo)]
                        pe.wait_ge(z_lo_ready, (gg + 1) * GC)
                        for dd in range(4):
                            d = 4 * j + dd
                            i = gg * KC + d
                            assert i == did["y"]
                            if i >= 2:
                                pe.wait_ge(y_read, i - 1)
                            b = 4 + 2 * (d % 2)
                            out = ps[:, 512 * b:512 * b + 1024].rearrange("p (a n) -> p a n", a=2)[:, :, 0:HALF]
                            c = P * dd
                            for k in range(GC):
                                slot = GC * (g % 2) + k
                                last = three(out, (w[0][:, k, c:c + P], w[1][:, k, c:c + P]),
                                             (z_hi[:, slot, :], z_lo[:, slot, :]), k == 0, k == GC - 1)
                            last.then_inc(y_done, 1)
                            did["y"] += 1
            quiet()
            for t in range(NT):
                transpose_step(("out", t), [(xT[:, c, P * t:P * t + P], P * c) for c in range(KC)])


def constants():
    t = np.arange(LAT)
    pos = (t // GRID_W, t % GRID_W)
    out = {}
    for name, width in (("rope_d", HD), ("rope_c", ROPE)):
        quarter = width // 4
        freqs = (THETA ** (-np.arange(quarter, dtype=np.float32) / np.float32(quarter))).astype(np.float32)
        tab = np.zeros((2, LAT, 2, 2, quarter), np.float32)
        for half in range(2):
            ang = pos[half].astype(np.float32)[:, None] * freqs
            tab[0, :, half, :, :] = np.cos(ang)[:, None, :]
            tab[1, :, half, 0, :] = -np.sin(ang)
            tab[1, :, half, 1, :] = np.sin(ang)
        out[name] = np.ascontiguousarray(tab.reshape(2, 4, P, width).transpose(2, 0, 1, 3))
    q, k = np.arange(P)[:, None], np.arange(P)[None, :]
    out["band"] = np.ascontiguousarray(np.stack([np.where(k >= q, 0, NEG), np.where(k <= q, 0, NEG)], 1).astype(np.float32))
    cols = np.zeros((P, 3, KCOLS), np.float32)
    for i, b in enumerate((0, 1, 3)):
        qcol = QC * b + np.arange(P) % QC
        start = np.clip(qcol - 8, 0, GRID_W - 16)[:, None]
        kcol = KEY_START[b] + np.arange(KCOLS)[None, :]
        cols[:, i] = np.where((kcol >= start) & (kcol < start + 16), 0, NEG)
    out["col_mask"] = cols
    rc = np.zeros((2, P, SEG), np.float32)
    for gi, w in enumerate(POOL_WINDOWS):
        for n, at in ((CTX, PAD), (LAT, PAD + CTX + 2 * PAD)):
            i = np.arange(n)
            count = np.clip(i - w // 2 + w, 0, n) - np.clip(i - w // 2, 0, n)
            rc[gi // 2, 64 * (gi % 2):64 * (gi % 2) + 64, at:at + n] = 1.0 / count.astype(np.float32)
    out["pool_rc"] = rc
    return out


_INS = ["x_prompt", "x_sample", "cache_na_k", "cache_na_v", "cache_mla_ckv", "cache_mla_kpe", "cache_swa_k",
        "cache_swa_v", "c", "c_ctx", "norm1", "norm2", "w_ada", "b_ada", "w_in", "w_out", "na_q_norm", "na_k_norm",
        "na_rpb", "pool_w", "pool_scale", "mla_q_a_norm", "mla_w_uq", "mla_kv_norm", "mla_w_ukv", "mla_q_norm",
        "mla_k_norm", "swa_q_norm", "swa_k_norm", "swa_sink", "mlp_w1", "mlp_w2"]
_OUTS = {"y_prompt": (1, CTX, D), "y_sample": (1, LAT, D), "na_k_new": (1, DEPTH, CTX, 4, HD),
         "na_v_new": (1, DEPTH, CTX, 4, HD), "mla_ckv_new": (1, DEPTH, CTX, KV_RANK),
         "mla_kpe_new": (1, DEPTH, CTX, ROPE), "swa_k_new": (1, DEPTH, CTX, 2, HD), "swa_v_new": (1, DEPTH, CTX, 2, HD)}


def kernel(**inputs):
    import concourse.bacc as bacc
    from concourse.bass_utils import run_bass_kernel_spmd

    nc = bacc.Bacc("TRN2", target_bir_lowering=False, num_devices=1)
    arrays = {f"in_{n}": np.ascontiguousarray(inputs[n]) for n in _INS}
    arrays["in_na_rpb"] = np.ascontiguousarray(inputs["na_rpb"][:, :, ::-1, ::-1].transpose(0, 2, 1, 3))
    arrays.update({f"in_{n}": v for n, v in constants().items()})
    a = {n[3:]: nc.dram_tensor(n, v.shape, F32, kind="ExternalInput").ap() for n, v in arrays.items()}
    o = {n: nc.dram_tensor(f"out_{n}", s, F32, kind="ExternalOutput").ap() for n, s in _OUTS.items()}
    hybrid_kernel(nc, a, o)
    r = run_bass_kernel_spmd(nc, [arrays], core_ids=[0])
    return tuple(r.results[0][f"out_{n}"] for n in _OUTS)
```

```python
from contextlib import ExitStack

import numpy as np

import concourse.bass as bass
from concourse import mybir

ALU = mybir.AluOpType
ACT = mybir.ActivationFunctionType
AX_X = mybir.AxisListType.X
F32 = mybir.dt.float32
F32R = mybir.dt.float32r

P = 128
D = 1024
KC = D // P
DEPTH = 2
CTX, LAT, PAST = 128, 512, 128
NTOK = CTX + LAT
NT = NTOK // P
HALF = NTOK // 2
GRID_W = 64
ROWS = LAT // GRID_W
HD = 64
D_FF = 4 * D
EPS = 1e-6
NEG = -1e30
THETA = 10000.0
POOL_WINDOWS = (2, 4, 8, 16)
PAD = 8
SEG = CTX + LAT + 4 * PAD
KV_RANK, Q_RANK, NOPE, ROPE, DV = 128, 256, 64, 32, 64
QK = NOPE + ROPE
SCALE = HD ** -0.5
SCALE_C = QK ** -0.5

COLS = {"naq": 0, "nak": 256, "nav": 512, "pool": 768, "cq": 1024, "ckv": 1280, "swq": 1440, "swkv": 1696}
KPE = 1408
UW = 256
WU = KC * UW
GROUPS = 8
GC = D_FF // P // GROUPS
AR, AC = 4, 256
OWN, OVER_MIX, FIRST, ROOM = 2, 2, 6, 11
AFTER_X = OWN + OVER_MIX + FIRST


def ada_place(u):
    seq, k = u // 16 % 3, u % 16
    if u < FIRST:
        return OWN + OVER_MIX + u
    if seq == 0 and u >= 48 and k < ROOM:
        return OWN + OVER_MIX + FIRST + k
    if AFTER_X <= u < AFTER_X + 5:
        return OWN + OVER_MIX + FIRST + u - AFTER_X
    if seq == 0 and u >= 48:
        return (u + 1) % (OWN + OVER_MIX)
    return u % OWN if seq == 2 else u % (OWN + OVER_MIX)


def ada_before(u):
    return [v for v in range(u) if ada_place(v) == ada_place(u)]

NCB, QC, KCOLS = 4, 16, 32
KEY_START = [min(max(min(max(QC * b - 8, 0), GRID_W - 16), 0), GRID_W - KCOLS) for b in range(NCB)]

R_ADA, R_N1, R_N2, R_PS, R_C, NVEC = 0, 48, 56, 64, 66, 82
SHIFT1, SCALE1, GATE1, SHIFT2, SCALE2, GATE2 = (8 * i for i in range(6))
H_DVE = (0, 1, 4, 6)

GAINS = {"na_q_norm": 64, "na_k_norm": 64, "swa_q_norm": 64, "swa_k_norm": 64, "mla_q_a_norm": 256,
         "mla_q_norm": 96, "mla_k_norm": 96, "mla_kv_norm": 128, "swa_sink": 4}
GAIN_AT = dict(zip(GAINS, np.cumsum([0, *GAINS.values()])[:-1].tolist()))
NGAIN = sum(GAINS.values())


def weight_units():
    out = []
    for l in range(DEPTH):
        out += [(l, n) for n in ("cq", "ckv", "up", "naq", "nak", "nav", "swq", "swkv", "pool")]
        out += [(l, "wo", j) for j in range(D // UW)]
        out += [(l, "w1", 0, j) for j in range(2)]
        for g in range(GROUPS):
            if g + 1 < GROUPS:
                out += [(l, "w1", g + 1, j) for j in range(2)]
            out += [(l, "w2", g, j) for j in range(2)]
    return out


def psum_steps():
    proj, trans, acc = [], [], []
    trans += [("x", c, "act") for c in range(KC)] + [("vec", l, "act") for l in range(DEPTH)]
    for l in range(DEPTH):
        acc += [(l, "sum1", "dve")]
        for n in ("cq", "ckv", "uq", "ukv", "naq", "nak", "nav", "swq", "swkv"):
            proj += [(l, n, t) for t in range(NT + (n == "ukv"))]
        trans += [(l, "cq", 0, "dve"), (l, "cq", 1, "dve"), (l, "ckv", 0, "dve")]
        trans += [(l, n, h, "act") for n in ("q", "k") for h in range(4)]
        trans += [(l, n, h, "act") for n in ("naq", "nak", "swq") for h in range(2)] + [(l, "swk", 0, "act")]
        acc += [(l, "pool", c, "act") for c in range(2)] + [(l, "mix", c, "dve") for c in range(2)]
        acc += [(l, "wo", d, "dve") for d in range(KC)] + [(l, "sum2", "dve")]
        acc += [(l, "z", g, c, "act") for g in range(GROUPS) for c in range(GC)]
    trans += [("out", c, "act") for c in range(KC)]
    return proj, trans, acc


def attention_pairs(kind):
    return [(kind, b, hp) for b in (None, 0, 1, 2, 3) for hp in range(2)]


def keys_of(kind, block):
    if block is None:
        return 1
    return {"C": 5, "A": 3, "D": 3 if block in (0, 3) else 4}[kind]


class Index:

    def __init__(self, steps):
        self.steps = steps
        self.at = {s[:-1]: i for i, s in enumerate(steps)}

    def last_reader(self, i):
        who = self.steps[i][-1]
        return who, sum(s[-1] == who for s in self.steps[:i + 1])


class Linked:

    def __init__(self, eng, own):
        self.eng, self.own, self.count = eng, own, {}

    def __call__(self, ins, sem=None):
        sem = self.own if sem is None else sem
        key = sem.name
        self.count[key] = self.count.get(key, 0) + 1
        ins.then_inc(sem, 1)
        self.eng.wait_ge(sem, self.count[key])


def hybrid_kernel(nc, a, o):
    units = weight_units()
    proj, trans, acc = psum_steps()
    proj_at = {s: i for i, s in enumerate(proj)}
    trans_ix, acc_ix = Index(trans), Index(acc)
    pairs = [(l, *p) for l in range(DEPTH) for kind in "CAD" for p in attention_pairs(kind)]
    pair_at = {p: i for i, p in enumerate(pairs)}

    def signals(i, h=1):
        before = sum(2 if p[1] == "C" else 1 for p in pairs[:i])
        return before + (h + 1 if pairs[i][1] == "C" else 1)


    base = (nc.sbuf_base + 63) // 32 * 32
    room = (nc.sbuf_usable_end - base) // 4

    def at(name, off, shape, dt=F32):
        size = int(np.prod(shape[1:]))
        assert off + size <= room, (name, off + size, room)
        return nc.alloc_sbuf_tensor_at(name, shape, dt, offset=base + 4 * off)

    top = [0]

    def sb(name, shape, dt=F32):
        size = (int(np.prod(shape[1:])) + 7) // 8 * 8
        top[0] += size
        return at(name, top[0] - size, shape, dt)

    xT = sb("xT", [P, KC, NTOK])
    h_hi = sb("h_hi", [P, KC, NTOK], F32R)
    h_lo = sb("h_lo", [P, KC, NTOK], F32R)
    w_raw = sb("w_raw", [P, 2, WU])
    w_hi = sb("w_hi", [P, 2, WU], F32R)
    w_lo = sb("w_lo", [P, 2, WU], F32R)
    ada_own = sb("ada_own", [P, OWN, AR, AC])
    ada_mix = at("ada_mix", top[0], [P, OVER_MIX, AR, AC])
    mixc_hi = sb("mixc_hi", [P, 2, NTOK], F32R)
    mixc_lo = sb("mixc_lo", [P, 2, NTOK], F32R)
    ident = sb("ident", [P, P])
    ones = sb("ones", [P, P])
    gains = sb("gains", [P, NGAIN])
    rope_d = sb("rope_d", [P, 2, 4, HD])
    rope_c = sb("rope_c", [P, 2, 4, ROPE])
    band = sb("band", [P, 2, P])
    col_mask = sb("col_mask", [P, 3, KCOLS])
    mod = sb("mod", [P, 2, 48, 2])
    vcol = sb("vcol", [P, DEPTH, NVEC])
    cond = sb("cond", [P, KC, 32])
    pool_w = sb("pool_w", [P, 2, P])
    cache_in = sb("cache_in", [P, 128 + 32 + 256 + 128])
    acol = sb("acol", [P, KC, 2])
    cexp = sb("cexp", [P, 16])
    hstat = sb("hstat", [P, 24])
    few = sb("few", [P, 3])
    gcol, warm = few[:, 0:2], few[:, 2:3]
    extrema = sb("extrema", [P, 2, 2, 2])
    mx, nb = extrema[:, 0], extrema[:, 1]
    totals = sb("totals", [P, 2, 2, 2])
    lsum, rinv = totals[:, 0], totals[:, 1]
    sink_e = sb("sink_e", [P, 2, 2])
    A0 = top[0]

    x_in = at("x_in", A0, [P, NT, D])
    vec_in = at("vec_in", A0 + NT * D, [P, DEPTH, P])
    rpb_in = at("rpb_in", A0 + 5376, [60, DEPTH, 64])
    ada_first = at("ada_first", A0 + 5504, [P, FIRST, AR, AC])
    ada_room = at("ada_room", A0, [P, ROOM, AR, AC])
    z_hi = at("z_hi", A0, [P, 2 * GC, NTOK], F32R)
    z_lo = at("z_lo", A0 + 5120, [P, 2 * GC, NTOK], F32R)
    z_relu = at("z_relu", A0 + 10240, [P, 2, NTOK])
    z_sq = at("z_sq", A0 + 11520, [P, 2, NTOK])
    sq = at("sq", A0 + 12800, [P, 2, NTOK])
    hf = at("hf", A0 + 14080, [P, 4, NTOK])
    rstd = at("rstd", A0 + 12160, [P, NTOK])
    c_q = at("c_q", A0, [P, 4, NTOK])
    c_k = at("c_k", A0 + 2560, [P, 4, NTOK + PAST])
    c_v = at("c_v", A0 + 5632, [P, NT + 1, 256])
    T0 = A0 + 7168
    cq_st = at("cq_st", T0, [P, NT, Q_RANK])
    ckv_st = at("ckv_st", T0 + 8480, [P, NT, KV_RANK + ROPE])
    q_st = at("q_st", T0, [P, NT, 4 * QK])
    k_st = at("k_st", T0 + 2080, [P, NT + 1, 4, QK])
    cqT_hi = at("cqT_hi", T0 + 4384, [P, 2, NTOK], F32R)
    cqT_lo = at("cqT_lo", T0 + 5664, [P, 2, NTOK], F32R)
    ckvT_hi = at("ckvT_hi", T0 + 6944, [P, NTOK + PAST], F32R)
    ckvT_lo = at("ckvT_lo", T0 + 7712, [P, NTOK + PAST], F32R)
    sq_cq = at("sq_cq", T0 + 2080, [P, NT, Q_RANK])
    sq_up = at("sq_up", T0 + 4384, [P, (NT + 1) * 4 * QK])
    rope_tmp_c = at("rope_tmp_c", T0 + 8480, [P, 2, 4, 4, ROPE])
    pr_c = at("pr_c", T0, [P, 2, 2, NT * P])
    pt_c = at("pt_c", T0 + 2560, [P, 2, 2, NT * P])
    a_q = at("a_q", A0, [P, 4, NTOK])
    a_k = at("a_k", A0 + 2560, [P, 2, NTOK + PAST])
    a_v = at("a_v", A0 + 4096, [P, NCB, 2, 256])
    a_vx = at("a_vx", A0 + 6144, [P, 2, 256])
    a_bias = at("a_bias", A0 + 6656, [P, 8, 4, 48])
    d_q = at("d_q", A0 + 8192, [P, 4, NTOK])
    d_k = at("d_k", A0 + 10752, [P, NTOK + PAST])
    d_v = at("d_v", A0 + 11520, [P, NT + 1, P])
    T1 = A0 + 12288
    st = at("st", T1, [P, 2, NT, 256])
    sq_st = at("sq_st", T1 + 2560, [P, NT, 256])
    rope_tmp_q = at("rope_tmp_q", A0 + 8192, [P, 2, 4, 4, HD])
    rope_tmp_k = [at("rope_tmp_k0", T1 + 3904, [P, 4, 2, HD]), at("rope_tmp_k1", A0 + 10752, [P, 4, 2, HD])]
    pr_a = at("pr_a", T1, [P, 2, 2, 512])
    pt_a = at("pt_a", T1 + 2048, [P, 2, 2, 512])
    pool_in = at("pool_in", T1 + 256, [P, 2, SEG])
    pool_s = at("pool_s", T1 + 1600, [P, 2, SEG])
    pool_rc = at("pool_rc", T1 + 2944, [P, SEG])
    H_HI, H_LO = KC * NTOK, 2 * KC * NTOK
    pool_t0 = at("pool_t0", H_HI + 4 * NTOK, [P, SEG])
    pool_t1 = at("pool_t1", H_LO + 4 * NTOK, [P, SEG])
    pool_rc0 = at("pool_rc0", H_HI + 6 * NTOK, [P, SEG])
    a_table = [at(f"a_table{i}", h + 6 * NTOK, [P, 4, 8, KCOLS]) for i, h in enumerate((H_LO, H_HI))]
    ada_row = at("ada_row", A0 + 16704, [P, 512])
    y_out = at("y_out", A0 + 10240, [P, NT, D])

    ctx = ExitStack()
    with ctx:
        ps = ctx.enter_context(nc.psum_tensor("ps", [P, 4096], F32))
        rpb_pad = nc.dram_tensor("rpb_pad", (DEPTH, 60, 64), F32).ap()
        nav_rows = nc.dram_tensor("nav_rows", (DEPTH, LAT, 256), F32).ap()

        def sem(name):
            return ctx.enter_context(nc.semaphore(name))

        x_in_dma, vec_dma, const_dma, gain_dma = sem("x_in_dma"), sem("vec_dma"), sem("const_dma"), sem("gain_dma")
        cache_dma, pool_w_dma = sem("cache_dma"), sem("pool_w_dma")
        w_dma = [sem("w_dma0"), sem("w_dma1")]
        ada_dma = [sem(f"ada_dma{i}") for i in range(OWN + OVER_MIX + FIRST + ROOM)]
        av_dma, nav_dma, ad_cache_dma, rpb_dma, bias_dma = (
            sem("av_dma"), sem("nav_dma"), sem("ad_cache_dma"), sem("rpb_dma"), sem("bias_dma"))
        rc_dma = [sem("rc_dma0"), sem("rc_dma1")]
        pool_ready = [sem("pool_ready0"), sem("pool_ready1")]
        rinv_ready = sem("rinv_ready")
        gcol_dma = sem("gcol_dma")
        out_st0, out_st1, out_ckv = sem("out_st0"), sem("out_st1"), sem("out_ckv")
        out_y = sem("out_y")
        consts_set, pads_set = sem("consts_set"), sem("pads_set")
        pool_chain = sem("pool_chain")
        dv_ready = sem("dv_ready")
        t_done, p_done, m_done, y_done = sem("t_done"), sem("p_done"), sem("m_done"), sem("y_done")
        ada_used, ada_turned = sem("ada_used"), sem("ada_turned")
        scored, turned, pv_done = sem("scored"), sem("turned"), sem("pv_done")
        act_chain = sem("act_chain")
        w_hi_ready, p_read, t_act, m_act = sem("w_hi_ready"), sem("p_read"), sem("t_act"), sem("m_act")
        cond_exp, ada_rows, sq_ready, sqrt_ready = sem("cond_exp"), sem("ada_rows"), sem("sq_ready"), sem("sqrt_ready")
        h_hi_ready, st_sq, st_sqrt, t_hi = sem("h_hi_ready"), sem("st_sq"), sem("st_sqrt"), sem("t_hi")
        exp_done, pt_ready, mix_hi, mixp_hi, z_hi_ready = (
            sem("exp_done"), sem("pt_ready"), sem("mix_hi"), sem("mixp_hi"), sem("z_hi_ready"))
        dve_chain = sem("dve_chain")
        w_lo_ready, t_dve, m_dve, y_read = sem("w_lo_ready"), sem("t_dve"), sem("m_dve"), sem("y_read")
        cond_ready, ada_reduced, rstd_ready = sem("cond_ready"), sem("ada_reduced"), sem("rstd_ready")
        table_ready, bias_scaled = sem("table_ready"), sem("bias_scaled")
        hf_dve, hf_pool, acol_ready = sem("hf_dve"), sem("hf_pool"), sem("acol_ready")
        h_lo_ready, st_mean, st_normed = sem("h_lo_ready"), sem("st_mean"), sem("st_normed")
        max_ready, p_normed, mix_lo = sem("max_ready"), sem("p_normed"), sem("mix_lo")
        z_sq_ready, z_lo_ready = sem("z_sq_ready"), sem("z_lo_ready")
        sum_used, pool_zeroed = sem("sum_used"), sem("pool_zeroed")

        def bank(b, n=512):
            return ps[:, 512 * b:512 * b + n]

        def trans_view(i, width):
            b = 2 if i % 2 == 0 else 6
            if trans[i][0] == "out":
                b = 2 * (i % 2)
            return ps[:, 512 * b:512 * b + width]

        def acc_banks(i):
            s = acc[i]
            if s[1] in ("pool", "mix"):
                return 4 * s[2]
            if s[1] in ("sum1", "sum2"):
                return 0
            return 2 * (s[-2] % 2)

        def acc_view(i):
            b = acc_banks(i)
            return ps[:, 512 * b:512 * b + 1024].rearrange("p (a n) -> p a n", a=2)[:, :, 0:HALF]

        def nav_tile(l, b, j):
            return bass.AP(nav_rows.tensor, offset=(l * LAT + 4 * j * GRID_W + KEY_START[b]) * 256,
                           ap=[[GRID_W * 256, 4], [256, 32], [1, 256]])

        def unit_width(n):
            return 1280 if units[n][1] == "up" else WU

        def dma_count(n):
            return 16 * (n // 2 + 1 + sum(units[m][1] == "up" for m in range(n % 2, n + 1, 2)))

        def wait_unit_done(eng, n):
            u = units[n]
            l, kind = u[0], u[1]
            if kind in ("w1", "w2"):
                g, j = u[2], u[3]
                if kind == "w1":
                    eng.wait_ge(m_done, acc_ix.at[(l, "z", g, 2 * j + 1)] + 1)
                else:
                    eng.wait_ge(y_done, (l * GROUPS + g) * KC + 4 * j + 4)
            elif kind == "wo":
                eng.wait_ge(m_done, acc_ix.at[(l, "wo", 2 * u[2] + 1)] + 1)
            elif kind == "pool":
                eng.wait_ge(m_done, acc_ix.at[(l, "pool", 1)] + 1)
            elif kind == "up":
                eng.wait_ge(p_done, proj_at[(l, "ukv", NT)] + 1)
            else:
                eng.wait_ge(p_done, proj_at[(l, kind, NT - 1)] + 1)

        NORMS = ("cq", "ckv", "q", "k", "naq", "nak", "swq", "swkv")

        def norm_at(l, n):
            return l * len(NORMS) + NORMS.index(n)

        def st_of(n):
            if n == "cq":
                return cq_st[:, :, :]
            if n == "ckv":
                return ckv_st[:, :, 0:KV_RANK]
            if n == "q":
                return q_st[:, :, :].rearrange("p t (h w) -> p (t h) w", w=QK)
            if n == "k":
                return k_st[:, :, :, :].rearrange("p t h w -> p (t h) w")
            b = {"naq": 0, "nak": 1, "nav": 0, "swq": 1, "swkv": 0}[n]
            if n == "swkv":
                return st[:, b, :, 0:128].rearrange("p t (h w) -> p t h w", w=HD)
            return st[:, b, :, :].rearrange("p t (h w) -> p (t h) w", w=HD)

        def sq_of(n):
            if n == "cq":
                return sq_cq[:, :, :]
            if n == "ckv":
                return sq_cq[:, :, 0:KV_RANK]
            if n == "q":
                return sq_up[:, 0:NT * 4 * QK].rearrange("p (g w) -> p g w", w=QK)
            if n == "k":
                return sq_up[:, :].rearrange("p (g w) -> p g w", w=QK)
            if n == "swkv":
                return sq_st[:, :, 0:128].rearrange("p t (h w) -> p t h w", w=HD)
            return sq_st[:, :, :].rearrange("p t (h w) -> p (t h) w", w=HD)

        def mixed(k, part):
            if k in (4, 5):
                return (mixc_hi, mixc_lo)[part][:, k - 4, :]
            return (h_hi, h_lo)[part][:, k, :]

        def mixed_at(l, pair):
            kind, b, hp = pair
            chunk = {"C": 4, "A": 0, "D": 6}[kind] + hp
            if b is None:
                return [mixed(chunk, p)[:, 0:CTX] for p in (0, 1)], bank(7, P)
            if kind == "A":
                dst = [mixed(chunk, p)[:, CTX:NTOK].rearrange("p (r c) -> p r c", r=ROWS)[:, :, QC * b:QC * b + QC]
                       for p in (0, 1)]
                return dst, bank(7, P).rearrange("p (r c) -> p r c", r=ROWS)
            return [mixed(chunk, p)[:, CTX + P * b:CTX + P * b + P] for p in (0, 1)], bank(7, P)

        def scores(i, pair):
            kind, b, _ = pair
            n = keys_of(kind, b) * P
            if kind == "C":
                return ps[:, 0:2048].rearrange("p (h n) -> p h n", h=2)[:, :, 0:n]
            off = 1024 * (i % 2)
            return ps[:, off:off + 1024].rearrange("p (h n) -> p h n", h=2)[:, :, 0:n]

        def probs(i, pair):
            kind, b, _ = pair
            return (pr_c if kind == "C" else pr_a)[:, i % 2, :, 0:keys_of(kind, b) * P]

        def probs_t(i, pair):
            kind, b, _ = pair
            return (pt_c if kind == "C" else pt_a)[:, i % 2, :, 0:keys_of(kind, b) * P]

        ada_slots = [x[:, i] for x, n in ((ada_own, OWN), (ada_mix, OVER_MIX), (ada_first, FIRST), (ada_room, ROOM))
                     for i in range(n)]

        def wait_ada(eng, u):
            eng.wait_ge(ada_dma[ada_place(u)], 16 * (len(ada_before(u)) + 1))

        def in_attention(l):
            return 20 if l + 1 < DEPTH else 17

        def late_ticks(l, stage):
            cuts = ((0, 0, 4, 9, 14, 18), (0, 8, 8, 12, 15, 18))[min(l, 1)]
            return range(cuts[stage], cuts[stage + 1])

        TWO_BANKS = [(("turn", (k - 5) // 4) if k >= 5 and k % 4 == 1 else None, ("unit", k) if k < 16 else None)
                     for k in range(18)]
        ONE_BANK = [(("turn", k // 5), None) if k % 5 == 4 else (None, ("unit", k - k // 5)) for k in range(20)]

        def ada_banks(first):
            return (6, 6) if first % 48 == 32 else (4, 5)

        def ada_ticks_of(first):
            return ONE_BANK if first % 48 == 32 else TWO_BANKS

        def ada_unit_place(u):
            return u // 48, u % 48

        SEGMENTS = ((0, 0, CTX), (1, CTX, NTOK))

        def wait_divided(eng, nrm, c):
            mine = [k for k in range(KC) if k not in H_DVE]
            eng.wait_ge(hf_pool, len(mine) * nrm + mine.index(c) + 1)

        def wait_scaled(eng, nrm, c):
            eng.wait_ge(hf_dve, len(H_DVE) * nrm + H_DVE.index(c) + 1)

        def build_table(do, eng, b, sem):
            off = KEY_START[b] - QC * b + 16
            bias = bass.AP(a_bias[:, 0, 0, 0:1].tensor, ap=[[8 * 4 * 48, P], [48, 4], [-4 * 48, 8], [-1, KCOLS]],
                           offset=7 * 4 * 48 + 47 - off)
            mask = col_mask[:, {0: 0, 1: 1, 2: 1, 3: 2}[b], :].unsqueeze(1).unsqueeze(1)
            do(eng.tensor_tensor(a_table[b % 2][:, :, :, :], bias, mask.broadcast_to([P, 4, 8, KCOLS]), ALU.add), sem)

        def window_sums(do, eng, l, c, s0, s1, rc):
            x = pool_in[:, c, :]

            do(eng.tensor_tensor(s0[:, 1:SEG], x[:, 0:SEG - 1], x[:, 1:SEG], ALU.add))
            do(eng.tensor_tensor(s1[:, 2:SEG - 1], s0[:, 1:SEG - 2], s0[:, 3:SEG], ALU.add))
            if c:
                do(eng.tensor_tensor(s0[:, 4:SEG - 3], s1[:, 2:SEG - 5], s1[:, 6:SEG - 1], ALU.add))
                do(eng.tensor_tensor(s1[:, 8:SEG - 7], s0[:, 4:SEG - 11], s0[:, 12:SEG - 3], ALU.add))
            eng.wait_ge(rc_dma[c], 16 * (l + 1))
            e = slice(PAD, SEG - PAD)
            do(eng.tensor_tensor(s0[0:64, e], s0[0:64, e], rc[0:64, e], ALU.mult))
            do(eng.tensor_tensor(s0[64:128, e], s1[64:128, e], rc[64:128, e], ALU.mult))
            do(eng.tensor_tensor(x[:, e], s0[:, e], x[:, e], ALU.subtract), pool_ready[c])

        block = ctx.enter_context(nc.Block())

        @block.sync
        def _(sp):
            def row(ap, n):
                return ap.rearrange("(r c) -> r c", r=n)

            def load_weights(n):
                if n >= len(units):
                    return
                if n >= 2:
                    sp.wait_ge(w_lo_ready, n - 1)
                u = units[n]
                l, kind = u[0], u[1]
                dst = w_raw[:, n % 2, :]
                if kind == "up":
                    sp.dma_start(dst[:, 0:768].rearrange("p (k c) -> p k c", k=2),
                                 a["mla_w_uq"][l].rearrange("(k p) c -> p k c", p=P)).then_inc(w_dma[n % 2], 16)
                    sp.dma_start(dst[:, 768:1280], a["mla_w_ukv"][l]).then_inc(w_dma[n % 2], 16)
                    return
                if kind == "w2":
                    g, j = u[2], u[3]
                    src = a["mlp_w2"][l, 512 * g:512 * g + 512, 512 * j:512 * j + 512]
                    sp.dma_start(dst.rearrange("p (k c) -> p k c", k=GC),
                                 src.rearrange("(k p) c -> p k c", p=P)).then_inc(w_dma[n % 2], 16)
                    return
                if kind == "wo":
                    src = a["w_out"][l, :, UW * u[2]:UW * u[2] + UW]
                elif kind == "w1":
                    c = 512 * u[2] + UW * u[3]
                    src = a["mlp_w1"][l, :, c:c + UW]
                else:
                    src = a["w_in"][l, :, COLS[kind]:COLS[kind] + UW]
                sp.dma_start(dst.rearrange("p (k c) -> p k c", k=KC),
                             src.rearrange("(k p) c -> p k c", p=P)).then_inc(w_dma[n % 2], 16)

            def load_ada(u):
                before, place = ada_before(u), ada_place(u)
                if before:
                    sp.wait_ge(ada_used, before[-1] + 1)
                k, c = 512 * (u % 2), AC * (u % 48 // 2)
                sp.dma_start(ada_slots[place], a["w_ada"][u // 48, k:k + 512, c:c + AC].rearrange("(k p) c -> p k c", p=P))\
                  .then_inc(ada_dma[place], 16)

            def load_adas(first, ks):
                for k in ks:
                    load_ada(first + k)

            sp.dma_start(x_in[:, 0, :], a["x_prompt"][0]).then_inc(x_in_dma, 16)
            sp.dma_start(x_in[:, 1:NT, :], a["x_sample"][0].rearrange("(t p) d -> p t d", p=P)).then_inc(x_in_dma, 16)
            for l in range(DEPTH):
                for r, src, n in ((R_ADA, a["b_ada"][l], 48), (R_N1, a["norm1"][l], 8), (R_N2, a["norm2"][l], 8),
                                  (R_PS, a["pool_scale"][l], 2), (R_C, a["c_ctx"], 8), (R_C + 8, a["c"][0], 8)):
                    sp.dma_start(vec_in[r:r + n, l, :], row(src, n)).then_inc(vec_dma, 16)
            load_adas(0, range(AFTER_X))
            sp.wait_ge(t_done, KC)
            load_adas(0, range(AFTER_X, 16))
            load_weights(0)
            sp.dma_start(rope_d[:, :, :, :], a["rope_d"]).then_inc(const_dma, 16)
            sp.dma_start(rope_c[:, :, :, :], a["rope_c"]).then_inc(const_dma, 16)
            sp.dma_start(band[:, :, :], a["band"]).then_inc(const_dma, 16)
            sp.dma_start(col_mask[:, :, :], a["col_mask"]).then_inc(const_dma, 16)
            load_weights(1)
            for l in range(DEPTH):
                U = 45 * l
                if l:
                    sp.wait_ge(st_normed, norm_at(l - 1, "swkv") + 1)
                    sp.wait_ge(t_done, trans_ix.at[(l - 1, "swk", 0)] + 1)
                    sp.wait_ge(p_normed, pair_at[(l - 1, "D", 3, 1)] + 1)
                    sp.wait_ge(m_done, acc_ix.at[(l - 1, "mix", 1)] + 1)
                    sp.wait_ge(t_act, trans_ix.last_reader(trans_ix.at[(l - 1, "k", 3)])[1])
                for k, name in enumerate(("mla_q_norm", "mla_k_norm")):
                    sp.dma_start(gcol[0:NOPE, k:k + 1], a[name][l, 0:NOPE].unsqueeze(1)).then_inc(gcol_dma, 16)
                for name, w in GAINS.items():
                    sp.dma_start(gains[:, GAIN_AT[name]:GAIN_AT[name] + w],
                                 a[name][l].unsqueeze(0).broadcast_to([P, w])).then_inc(gain_dma, 16)
                sp.dma_start(cache_in[:, 0:128], a["cache_mla_ckv"][0, l]).then_inc(cache_dma, 16)
                sp.dma_start(cache_in[:, 128:160], a["cache_mla_kpe"][0, l]).then_inc(cache_dma, 16)
                sp.dma_start(cache_in[:, 160:416], a["cache_na_k"][0, l].rearrange("t h d -> t (h d)")).then_inc(cache_dma, 16)
                sp.dma_start(cache_in[:, 416:544], a["cache_swa_k"][0, l].rearrange("t h d -> t (h d)")).then_inc(cache_dma, 16)
                sp.wait_ge(consts_set, 1)
                for g in range(4):
                    q = 64 * (g % 2)
                    sp.dma_start(pool_w[q:q + 64, g // 2, q:q + 64], a["pool_w"][l, g]).then_inc(pool_w_dma, 16)

                load_weights(U + 2)
                load_adas(48 * l + 16, range(8))
                load_weights(U + 3)
                load_adas(48 * l + 16, range(8, 16))
                for n in (4, 5, 6):
                    load_weights(U + n)
                sp.wait_ge(pv_done, pair_at[(l, "C", 3, 1)] + 1)
                sp.dma_start(a_vx[:, 1, :], a["cache_na_v"][0, l].rearrange("t h d -> t (h d)")).then_inc(ad_cache_dma, 16)
                sp.dma_start(d_v[:, NT, :], a["cache_swa_v"][0, l].rearrange("t h d -> t (h d)")).then_inc(ad_cache_dma, 16)
                sp.wait_ge(rpb_dma, 32 * DEPTH)
                for r in range(ROWS):
                    src = bass.AP(rpb_pad.tensor, offset=(60 * l + 4 * r) * 64, ap=[[1, QC], [64, 32], [1, 48]])
                    sp.dma_start(a_bias[QC * r:QC * r + QC, :, :, :].rearrange("p r h c -> p (r h) c"), src)\
                      .then_inc(bias_dma, 16)
                load_weights(U + 7)
                load_weights(U + 8)
                sp.wait_ge(p_read, proj_at[(l, "nav", NT - 1)] + 1)
                sp.dma_start(nav_rows[l].rearrange("(t p) d -> p t d", p=P), st[:, 0, 1:NT, :]).then_inc(nav_dma, 16)
                sp.dma_start(a_vx[:, 0, :], st[:, 0, 0, :]).then_inc(nav_dma, 16)
                sp.dma_start(o["na_v_new"][0, l].rearrange("t h d -> t (h d)"), st[:, 0, 0, :]).then_inc(out_st0, 16)
                sp.wait_ge(st_normed, norm_at(l, "nak") + 1)
                sp.dma_start(o["na_k_new"][0, l].rearrange("t h d -> t (h d)"), st[:, 1, 0, :]).then_inc(out_st1, 16)
                sp.wait_ge(nav_dma, 32 * (l + 1))
                for b in range(NCB):
                    for j in range(2):
                        sp.dma_start(a_v[:, b, j, :], nav_tile(l, b, j)).then_inc(av_dma, 16)
                load_weights(U + 9)
                load_weights(U + 10)
                load_adas(48 * l + 32, range(OWN))
                sp.wait_ge(st_normed, norm_at(l, "swkv") + 1)
                sp.dma_start(o["swa_k_new"][0, l].rearrange("t h d -> t (h d)"), st[:, 0, 0, 0:128]).then_inc(out_st0, 16)
                sp.dma_start(o["swa_v_new"][0, l].rearrange("t h d -> t (h d)"), st[:, 0, 0, 128:256]).then_inc(out_st0, 16)
                sp.dma_start(pool_rc[:, :], a["pool_rc"][1]).then_inc(rc_dma[1], 16)
                sp.wait_ge(m_done, acc_ix.at[(l, "pool", 1)] + 1)
                sp.dma_start(pool_rc0[:, :], a["pool_rc"][0]).then_inc(rc_dma[0], 16)
                load_adas(48 * l + 32, range(OWN, 16))
                for n in (11, 12, 13, 14):
                    load_weights(U + n)
                    if l + 1 < DEPTH:
                        if n == 12:
                            sp.wait_ge(pv_done, pair_at[(l, "D", 3, 1)] + 1)
                            load_adas(48 * (l + 1), range(6))
                        if n == 13:
                            load_adas(48 * (l + 1), range(6, ROOM))
                if l + 1 < DEPTH:
                    load_adas(48 * (l + 1), range(ROOM, ROOM + OWN))
                    sp.wait_ge(m_done, acc_ix.at[(l, "wo", KC - 1)] + 1)
                    load_adas(48 * (l + 1), range(ROOM + OWN, 16))
                for n in range(15, 47):
                    load_weights(U + n)
            for c in range(1, KC, 2):
                sp.wait_ge(t_act, trans_ix.last_reader(trans_ix.at[("out", c)])[1])
                cols = slice(P * (c - 1), P * c + P)
                sp.dma_start(o["y_prompt"][0, :, cols], y_out[:, 0, cols]).then_inc(out_y, 16)
                sp.dma_start(o["y_sample"][0, :, cols].rearrange("(t p) d -> p t d", p=P), y_out[:, 1:NT, cols])\
                  .then_inc(out_y, 16)
            sp.wait_ge(out_y, 16 * KC)
            sp.wait_ge(out_ckv, 32 * DEPTH)
            sp.wait_ge(out_st0, 48 * DEPTH)
            sp.wait_ge(out_st1, 16 * DEPTH)

        @block.gpsimd
        def _(pool):
            do = Linked(pool, pool_chain)
            do(pool.memset(ident[:, :], 0.0))
            do(pool.memset(ones[:, :], 1.0))
            do(pool.memset(cond[:, :, :], 0.0))
            do(pool.memset(pool_w[:, :, :], 0.0))
            do(pool.memset(gcol[64:128, :], 1.0))
            do(pool.affine_select(out=ident[:, :], in_=ident[:, :], compare_op=ALU.not_equal, fill=1.0,
                                  base=0, pattern=[[-1, P]], channel_multiplier=1), consts_set)

            do(pool.memset(rpb_in[:, :, :], 0.0))
            for l in range(DEPTH):
                pool.dma_start(rpb_in[:, l, 16:47], a["na_rpb"][l].rearrange("r h c -> (r h) c")).then_inc(rpb_dma, 16)
            pool.wait_ge(rpb_dma, 16 * DEPTH)
            for l in range(DEPTH):
                pool.dma_start(rpb_pad[l], rpb_in[:, l, :]).then_inc(rpb_dma, 16)
            pool.wait_ge(rpb_dma, 32 * DEPTH)

            def scale_x(nrm):
                pool.wait_ge(rstd_ready, nrm + 1)
                for c in range(KC):
                    if c not in H_DVE:
                        if c >= 4:
                            pool.wait_ge(h_lo_ready, KC * nrm + c - 3)
                        do(pool.tensor_tensor(hf[:, c % 4, :], xT[:, c, :], rstd[:, :], ALU.mult), hf_pool)

            def normalise(l, kinds):
                for pair in [p for kind in kinds for p in attention_pairs(kind)]:
                    i = pair_at[(l, *pair)]
                    pool.wait_ge(rinv_ready, i + 1)
                    v = probs(i, pair)
                    do(pool.tensor_tensor(v, v, rinv[:, i % 2, :].unsqueeze(2).broadcast_to(list(v.shape)), ALU.mult),
                       p_normed)
                    if pair[0] == "A" and pair[1] in (None, 0, 1) and pair[2] == 1:
                        b = 1 if pair[1] is None else pair[1] + 2
                        if b == 1:
                            pool.wait_ge(bias_scaled, l + 1)
                        elif b > 1:
                            pool.wait_ge(max_ready, signals(pair_at[(l, "A", b - 2, 1)]))
                        build_table(do, pool, b, table_ready)

            for l in range(DEPTH):
                scale_x(2 * l)
                normalise(l, "C")
                pool.wait_ge(pv_done, pair_at[(l, "C", 3, 1)] + 1)
                do(pool.memset(a_q[64:128, 0:4:2, :], 0.0))
                do(pool.memset(a_q[0:64, 1:4:2, :], 0.0))
                pool.wait_ge(st_normed, norm_at(l, "swq") + 1)
                do(pool.memset(d_q[64:128, 0:2, :], 0.0))
                do(pool.memset(d_q[0:64, 2:4, :], 0.0), pads_set)
                pool.wait_ge(p_read, proj_at[(l, "swkv", NT - 1)] + 1)
                do(pool.tensor_copy(d_v[:, 0:NT, :], st[:, 0, :, 128:256]), dv_ready)
                pool.wait_ge(t_done, trans_ix.at[(l, "swk", 0)] + 1)
                pool.wait_ge(out_st1, 16 * (l + 1))
                for s, e in ((0, PAD), (PAD + CTX, CTX + 3 * PAD), (SEG - PAD, SEG)):
                    do(pool.memset(pool_in[:, :, s:e], 0.0), pool_zeroed if e == SEG else None)
                pool.wait_ge(m_act, acc_ix.last_reader(acc_ix.at[(l, "pool", 0)])[1])
                pool.wait_ge(m_done, acc_ix.at[(l, "pool", 1)] + 1)
                window_sums(do, pool, l, 0, pool_t0, pool_t1, pool_rc0)
                normalise(l, "AD")
                scale_x(2 * l + 1)

        @block.scalar
        def _(act):
            do = Linked(act, act_chain)

            def copy(out, in_, sem=None, scale=None):
                if scale is None:
                    do(nc.scalar.activation(out, in_, ACT.Copy), sem)
                else:
                    do(nc.scalar.activation(out, in_, ACT.Copy, scale=scale), sem)

            def split_hi(n):
                if n >= len(units):
                    return
                act.wait_ge(w_dma[n % 2], dma_count(n))
                if n >= 2:
                    wait_unit_done(act, n - 2)
                w = unit_width(n)
                copy(w_hi[:, n % 2, 0:w], w_raw[:, n % 2, 0:w], w_hi_ready)

            def ada_tick(first, k):
                unit = ada_ticks_of(first)[k][1]
                if unit and unit[1] % 4 == 3:
                    u = first + unit[1]
                    act.wait_ge(ada_used, u + 1)
                    if u >= 4:
                        act.wait_ge(ada_turned, u // 4)
                    copy(ada_row[:, :], bank(ada_banks(first)[0]), ada_rows)

            def ada_ticks(first, ks):
                for k in ks:
                    ada_tick(first, k)

            def square_x(nrm, c):
                if c >= 2:
                    act.wait_ge(sum_used, (KC - 2) * nrm + max(c - 2, 1))
                do(nc.scalar.activation(sq[:, c % 2, :], xT[:, c, :], ACT.Square), sq_ready)

            def root_x(nrm):
                do(nc.scalar.activation(warm[:, :], ones[:, 0:1], ACT.Sqrt))
                l, name = nrm // 2, ("sum1", "sum2")[nrm % 2]
                act.wait_ge(m_dve, acc_ix.last_reader(acc_ix.at[(l, name)])[1])
                do(nc.scalar.activation(rstd[:, :], rstd[:, :], ACT.Sqrt), sqrt_ready)

            def h_halves(nrm, chunks=range(KC)):
                l, sh = nrm // 2, (SHIFT1, SHIFT2)[nrm % 2]
                act.wait_ge(acol_ready, nrm + 1)
                for c in chunks:
                    if c in H_DVE:
                        wait_scaled(act, nrm, c)
                        for m, s, e in SEGMENTS:
                            do(nc.scalar.activation(h_hi[:, c, s:e], hf[:, c % 4, s:e], ACT.Identity,
                                                    bias=mod[:, l % 2, sh + c, m:m + 1]), h_hi_ready if m else None)
                    else:
                        wait_divided(act, nrm, c)
                        for m, s, e in SEGMENTS:
                            do(nc.scalar.activation(hf[:, c % 4, s:e], hf[:, c % 4, s:e], ACT.Identity,
                                                    scale=acol[:, c, m:m + 1], bias=mod[:, l % 2, sh + c, m:m + 1]))
                        copy(h_hi[:, c, :], hf[:, c % 4, :], h_hi_ready)

            def load_exp():
                do(nc.scalar.activation(warm[:, :], cexp[:, 0:1], ACT.Exp))

            def evacuate(l, n, t, dst, src_cols):
                i = proj_at[(l, n, t)]
                act.wait_ge(p_done, i + 1)
                src = bank(i % 2)
                if n == "ukv":
                    v = src.rearrange("p (h c) -> p h c", h=4)
                    copy(k_st[:, t, :, 0:NOPE], v[:, :, 0:NOPE])
                    copy(c_v[:, t, :].rearrange("p (h d) -> p h d", h=4), v[:, :, NOPE:NOPE + DV], p_read)
                else:
                    copy(dst, src[:, 0:src_cols], p_read)

            def square(l, n):
                i = norm_at(l, n)
                if i:
                    act.wait_ge(st_mean, i)
                do(nc.scalar.activation(sq_of(n), st_of(n), ACT.Square), st_sq)

            def root(l, n):
                act.wait_ge(st_mean, norm_at(l, n) + 1)
                do(nc.scalar.activation(hstat[:, :], hstat[:, :], ACT.Sqrt), st_sqrt)

            def turn(l, n, part):
                i = trans_ix.at[(l, n, part)]
                act.wait_ge(t_done, i + 1)
                if n == "cq":
                    copy(cqT_hi[:, part, :], trans_view(i, NTOK), t_hi)
                elif n == "ckv":
                    copy(ckvT_hi[:, :], trans_view(i, NTOK + PAST), t_hi)
                elif n == "q":
                    copy(c_q[0:QK, part, :], trans_view(i, NTOK)[0:QK], t_act, scale=gcol[0:QK, 0:1])
                elif n == "k":
                    copy(c_k[0:QK, part, :], trans_view(i, NTOK + PAST)[0:QK], t_act, scale=gcol[0:QK, 1:2])
                elif n == "naq":
                    v = trans_view(i, NTOK)
                    for h in range(2):
                        r = 64 * h
                        copy(a_q[r:r + 64, 2 * part + h, 0:CTX], v[r:r + 64, 0:CTX])
                        copy(a_q[r:r + 64, 2 * part + h, CTX:NTOK].rearrange("p (b r c) -> p r b c", b=NCB, r=ROWS),
                             v[r:r + 64, CTX:NTOK].rearrange("p (r b c) -> p r b c", r=ROWS, b=NCB), t_act if h else None)
                elif n == "swq":
                    v = trans_view(i, NTOK)
                    r = 64 * part
                    copy(d_q[r:r + 64, 2 * part, :], v[0:64])
                    copy(d_q[r:r + 64, 2 * part + 1, :], v[64:128], t_act)
                elif n == "nak":
                    copy(a_k[:, part, :], trans_view(i, NTOK + PAST), t_act)
                else:
                    copy(d_k[:, :], trans_view(i, NTOK + PAST), t_act)

            def attention(l, kind_list):
                todo = [(pair_at[(l, *p)], p) for kind in kind_list for p in attention_pairs(kind)]

                def exps(i, pair):
                    kind = pair[0]
                    act.wait_ge(max_ready, signals(i, 0))
                    if i >= 2:
                        act.wait_ge(turned, i - 1)
                    scale = SCALE_C if kind == "C" else SCALE
                    if kind == "D":
                        do(nc.scalar.activation(sink_e[:, i % 2, :], sink_e[:, i % 2, :], ACT.Exp))
                    for h in range(2):
                        act.wait_ge(max_ready, signals(i, h))
                        do(nc.scalar.activation(probs(i, pair)[:, h, :], scores(i, pair)[:, h, :], ACT.Exp,
                                                bias=nb[:, i % 2, h:h + 1], scale=scale,
                                                accum_out=lsum[:, i % 2, h:h + 1]),
                           exp_done if h or kind == "C" else None)

                def take_turned(i, pair):
                    act.wait_ge(turned, i + 1)
                    if i >= 2:
                        act.wait_ge(pv_done, i - 1)
                    dst, n = probs_t(i, pair), keys_of(pair[0], pair[1])
                    w = min(n, 4) * P
                    src = ps[:, 2048:3072].rearrange("p (h n) -> p h n", h=2)[:, :, 0:w]
                    if n == 5:
                        copy(dst[:, :, 0:w], src)
                        copy(dst[:, :, w:w + P], ps[:, 3072:3072 + 2 * P].rearrange("p (h n) -> p h n", h=2), pt_ready)
                    else:
                        copy(dst[:, :, 0:w], src, pt_ready)

                def take_out(i, pair):
                    act.wait_ge(pv_done, i + 1)
                    dst, src = mixed_at(l, pair)
                    copy(dst[0], src, mix_hi)

                for j in range(len(todo) + 3):
                    if kind_list == "AD" and j + 5 < in_attention(l):
                        ada_tick(48 * l + 32, j + 5)
                    if kind_list == "C" and j < len(todo):
                        exps(*todo[j])
                    if 2 <= j < len(todo) + 2:
                        take_turned(*todo[j - 2])
                    if j >= 3:
                        take_out(*todo[j - 3])
                    if kind_list == "AD" and j < len(todo):
                        exps(*todo[j])

            for c in range(KC):
                act.wait_ge(t_done, c + 1)
                copy(xT[:, c, :], trans_view(c, NTOK), t_act)
            for l in range(DEPTH):
                act.wait_ge(t_done, KC + l + 1)
                copy(vcol[:, l, :], trans_view(KC + l, NVEC), t_act)
            do(nc.scalar.activation(cexp[:, :], vcol[:, 0, R_C:NVEC], ACT.Exp, scale=-1.0), cond_exp)
            for c in range(KC):
                square_x(0, c)
            ada_ticks(0, range(8))
            root_x(0)
            ada_ticks(0, range(8, 12))
            split_hi(0)
            ada_ticks(0, range(12, 18))

            for l in range(DEPTH):
                U = 45 * l
                if l:
                    for c in range(KC):
                        act.wait_ge(y_read, (l * GROUPS - 1) * KC + c + 1)
                        square_x(2 * l, c)
                    root_x(2 * l)
                late = 48 * l + 16
                before = late_ticks(l, 0)
                ada_ticks(late, before[:4])
                h_halves(2 * l, range(2))
                ada_ticks(late, before[4:])
                h_halves(2 * l, range(2, KC))

                def unit(n, name, dst, cols, root_of=None, tiles=NT, split=True, first=0):
                    if split:
                        split_hi(U + n + 1)
                    for t in range(first, tiles):
                        evacuate(l, name, t, dst(t), cols)
                        if t == 1 and root_of:
                            root(l, root_of)

                unit(0, "cq", lambda t: cq_st[:, t, :], 256)
                square(l, "cq")
                ada_ticks(late, late_ticks(l, 1))
                unit(1, "ckv", lambda t: ckv_st[:, t, :], 160, "cq")
                square(l, "ckv")
                turn(l, "cq", 0)
                turn(l, "cq", 1)
                root(l, "ckv")
                ada_ticks(late, late_ticks(l, 2))
                turn(l, "ckv", 0)
                act.dma_start(o["mla_ckv_new"][0, l], ckv_st[:, 0, 0:KV_RANK]).then_inc(out_ckv, 16)
                act.dma_start(o["mla_kpe_new"][0, l], ckv_st[:, 0, KV_RANK:KV_RANK + ROPE]).then_inc(out_ckv, 16)
                unit(2, "uq", lambda t: q_st[:, t, :], 4 * QK)
                square(l, "q")
                unit(2, "ukv", lambda t: None, 0, "q", NT + 1, split=False)
                square(l, "k")
                ada_ticks(late, late_ticks(l, 3))
                act.wait_ge(gcol_dma, 32 * (l + 1))
                for h in range(4):
                    turn(l, "q", h)
                root(l, "k")
                ada_ticks(late, late_ticks(l, 4))
                unit(3, "naq", lambda t: st[:, 0, t, :], 256, tiles=2, split=False)
                load_exp()
                for h in range(4):
                    turn(l, "k", h)
                attention(l, "C")
                unit(3, "naq", lambda t: st[:, 0, t, :], 256, first=2, tiles=4, split=False)
                unit(3, "naq", lambda t: st[:, 0, t, :], 256, first=4)
                square(l, "naq")
                unit(4, "nak", lambda t: st[:, 1, t, :], 256, "naq")
                square(l, "nak")
                turn(l, "naq", 0)
                turn(l, "naq", 1)
                unit(5, "nav", lambda t: st[:, 0, t, :], 256, "nak")
                turn(l, "nak", 0)
                turn(l, "nak", 1)
                act.wait_ge(out_st1, 16 * (l + 1))
                unit(6, "swq", lambda t: st[:, 1, t, :], 256)
                square(l, "swq")
                act.wait_ge(nav_dma, 32 * (l + 1))
                act.wait_ge(out_st0, 48 * l + 16)
                unit(7, "swkv", lambda t: st[:, 0, t, :], 256, "swq")
                square(l, "swkv")
                turn(l, "swq", 0)
                turn(l, "swq", 1)
                root(l, "swkv")
                turn(l, "swk", 0)
                act.wait_ge(pool_zeroed, l + 1)
                for c in range(2):
                    i = acc_ix.at[(l, "pool", c)]
                    act.wait_ge(m_done, i + 1)
                    v = acc_view(i)
                    lat = PAD + CTX + 2 * PAD
                    copy(pool_in[:, c, PAD:PAD + CTX], v[:, 0, 0:CTX])
                    copy(pool_in[:, c, lat:lat + HALF - CTX], v[:, 0, CTX:HALF])
                    copy(pool_in[:, c, lat + HALF - CTX:lat + LAT], v[:, 1, :], m_act)
                split_hi(U + 9)
                ada_ticks(48 * l + 32, range(5))
                load_exp()
                for c in range(2):
                    i = acc_ix.at[(l, "mix", c)]
                    act.wait_ge(m_done, i + 1)
                    copy(h_hi[:, 2 + c, :].rearrange("p (a n) -> p a n", a=2), acc_view(i), mixp_hi,
                         scale=vcol[:, l, R_PS + c:R_PS + c + 1])
                act.wait_ge(out_st0, 48 * (l + 1))
                attention(l, "AD")
                for j in range(5):
                    if j < 4:
                        split_hi(U + 9 + j + 1)
                    for c in (2 * j - 1, 2 * j):
                        if 0 <= c < KC:
                            act.wait_ge(m_dve, acc_ix.last_reader(acc_ix.at[(l, "wo", c)])[1])
                            square_x(2 * l + 1, c)
                root_x(2 * l + 1)
                more = l + 1 < DEPTH
                ada_ticks(48 * l + 32, range(in_attention(l), 20))
                ada_ticks(48 * (l + 1), range(12 * more))
                h_halves(2 * l + 1, range(4))
                h_halves(2 * l + 1, range(4, KC))
                ada_ticks(48 * (l + 1), range(12 * more, 18 * more))
                for n in range(13, 45):
                    split_hi(U + n + 1)
                    u = units[U + n]
                    if u[1] == "w1":
                        g = u[2]
                        gg = l * GROUPS + g
                        for c in (2 * u[3], 2 * u[3] + 1):
                            zi = gg * GC + c
                            i = acc_ix.at[(l, "z", g, c)]
                            act.wait_ge(m_done, i + 1)
                            if zi >= 2:
                                act.wait_ge(z_sq_ready, zi - 1)
                            do(nc.scalar.activation(z_relu[:, c % 2, :].rearrange("p (a n) -> p a n", a=2),
                                                    acc_view(i), ACT.Relu), m_act)
                            if gg >= 2:
                                act.wait_ge(y_done, (gg - 1) * KC)
                            slot = GC * (g % 2) + c
                            do(nc.scalar.activation(z_hi[:, slot, :], z_relu[:, c % 2, :], ACT.Square), z_hi_ready)
            for c in range(KC):
                i = trans_ix.at[("out", c)]
                act.wait_ge(t_done, i + 1)
                copy(y_out[:, :, P * c:P * c + P], trans_view(i, NTOK).rearrange("p (t n) -> p t n", t=NT), t_act)

        @block.vector
        def _(dve):
            do = Linked(dve, dve_chain)
            V = nc.vector

            def f32(ap):
                return ap.bitcast(F32)

            def split_lo(n):
                if n >= len(units):
                    return
                dve.wait_ge(w_hi_ready, n + 1)
                w = unit_width(n)
                do(V.tensor_tensor(w_lo[:, n % 2, 0:w], w_raw[:, n % 2, 0:w], f32(w_hi[:, n % 2, 0:w]),
                                   ALU.subtract), w_lo_ready)

            def ada_tick(first, k):
                turned = ada_ticks_of(first)[k][0]
                if turned:
                    u = first + 4 * turned[1]
                    l, c = ada_unit_place(u)
                    dve.wait_ge(ada_turned, u // 4 + 1)
                    m = mod[:, l % 2, c:c + 4, :]
                    do(V.tensor_reduce(m, bank(ada_banks(first)[1]).rearrange("p (c j m) -> p c m j", c=4, j=4)[:, :, 0:2, :],
                                       AX_X, ALU.add), ada_reduced)
                    do(V.tensor_tensor(m, m, vcol[:, l, R_ADA + c:R_ADA + c + 4].unsqueeze(2).broadcast_to([P, 4, 2]),
                                       ALU.add))

            def ada_ticks(first, ks):
                for k in ks:
                    ada_tick(first, k)

            def add_square(nrm, c):
                if 0 < c < KC - 1:
                    dve.wait_ge(sq_ready, KC * nrm + c + 1)
                    do(V.tensor_tensor(rstd[:, :], sq[:, 0, :] if c == 1 else rstd[:, :], sq[:, c % 2, :], ALU.add), sum_used)

            def mean(nrm):
                l, which = nrm // 2, nrm % 2
                i = acc_ix.at[(l, ("sum1", "sum2")[which])]
                dve.wait_ge(m_done, i + 1)
                do(V.tensor_scalar(rstd[:, :].rearrange("p (a n) -> p a n", a=2), acc_view(i), 1.0 / D, EPS,
                                   ALU.mult, ALU.add), m_dve)
                dve.wait_ge(sqrt_ready, nrm + 1)
                do(V.reciprocal(rstd[:, :], rstd[:, :]), rstd_ready)

            def h_of(nrm, between={}):
                l, which = nrm // 2, nrm % 2
                sc = (SCALE1, SCALE2)[which]
                sh = (SHIFT1, SHIFT2)[which]
                gain = vcol[:, l, (R_N1, R_N2)[which]:(R_N1, R_N2)[which] + KC].unsqueeze(2).broadcast_to([P, KC, 2])
                do(V.scalar_tensor_tensor(acol[:, :, :], mod[:, l % 2, sc:sc + KC, :], 1.0, gain, ALU.add, ALU.mult),
                   acol_ready)

                def lo(c):
                    dve.wait_ge(h_hi_ready, KC * nrm + c + 1)
                    if c not in H_DVE:
                        do(V.tensor_tensor(h_lo[:, c, :], hf[:, c % 4, :], f32(h_hi[:, c, :]), ALU.subtract), h_lo_ready)
                        return
                    for m, s, e in SEGMENTS:
                        do(V.scalar_tensor_tensor(h_lo[:, c, s:e], hf[:, c % 4, s:e], mod[:, l % 2, sh + c, m:m + 1],
                                                  f32(h_hi[:, c, s:e]), ALU.add, ALU.subtract), h_lo_ready if m else None)

                for c in range(KC):
                    if c in between:
                        between[c]()
                    if c in H_DVE:
                        for m, s, e in SEGMENTS:
                            do(V.scalar_tensor_tensor(hf[:, c % 4, s:e], xT[:, c, s:e], acol[:, c, m:m + 1], rstd[:, s:e],
                                                      ALU.mult, ALU.mult), hf_dve if m else None)
                    if c >= 2:
                        lo(c - 2)
                lo(KC - 2)
                lo(KC - 1)

            def norm(l, n):
                gain, w, g = {"cq": ("mla_q_a_norm", 256, 5), "ckv": ("mla_kv_norm", 128, 5),
                              "q": ("mla_q_norm", QK, 20), "k": ("mla_k_norm", QK, 24),
                              "naq": ("na_q_norm", HD, 20), "nak": ("na_k_norm", HD, 20),
                              "swq": ("swa_q_norm", HD, 20), "swkv": ("swa_k_norm", HD, 10)}[n]
                x = st_of(n)
                dve.wait_ge(st_sq, norm_at(l, n) + 1)
                hs = hstat[:, 0:g]
                if n == "swkv":
                    hs = hs.rearrange("p (t h) -> p t h", h=2)
                do(V.tensor_reduce(hs, sq_of(n), AX_X, ALU.add))
                do(V.tensor_scalar(hstat[:, :], hstat[:, :], 1.0 / w, EPS, ALU.mult, ALU.add), st_mean)
                dve.wait_ge(st_sqrt, norm_at(l, n) + 1)
                do(V.reciprocal(hstat[:, :], hstat[:, :]))
                shape = list(x.shape)
                do(V.tensor_tensor(x, x, hs.unsqueeze(len(shape) - 1).broadcast_to(shape), ALU.mult))
                row = gains[:, GAIN_AT[gain]:GAIN_AT[gain] + w]
                for _ in shape[1:-1]:
                    row = row.unsqueeze(1)
                if n in "qk":
                    x = (q_st[:, :, :].rearrange("p t (h c) -> p t h c", h=4) if n == "q" else k_st)[:, :, :, NOPE:QK]
                    shape = list(x.shape)
                    row = gains[:, GAIN_AT[gain] + NOPE:GAIN_AT[gain] + QK].unsqueeze(1).unsqueeze(1)
                last = n in ("cq", "ckv", "naq", "nak")
                do(V.tensor_tensor(x, x, row.broadcast_to(shape), ALU.mult), st_normed if last else None)
                if last:
                    return
                if n == "q":
                    dve.wait_ge(out_ckv, 32 * (l + 1))
                if n == "q":
                    x = q_st[:, 1:NT, :].rearrange("p t (h c) -> p t h c", h=4)[:, :, :, NOPE:QK]
                elif n == "k":
                    x = k_st[:, 1:NT, :, NOPE:QK]
                elif n == "swq":
                    x = st[:, 1, 1:NT, :].rearrange("p t (h c) -> p t h c", h=4)
                else:
                    x = st[:, 0, 1:NT, 0:2 * HD].rearrange("p t (h c) -> p t h c", h=2)
                tab = rope_c if n in "qk" else rope_d
                tmp = [t[:, :, :, :] for t in rope_tmp_k] if n == "swkv" else [(rope_tmp_c if n in "qk" else rope_tmp_q)[:, k] for k in range(2)]
                cos, sin = [tab[:, k].unsqueeze(2).broadcast_to(list(x.shape)) for k in range(2)]
                do(V.tensor_tensor(tmp[0], x, cos, ALU.mult))
                for f in range(2):
                    for s in range(2):
                        w = x.shape[3] // 4
                        to, of = (2 * f + s) * w, (2 * f + 1 - s) * w
                        do(V.tensor_tensor(tmp[1][:, :, :, to:to + w], x[:, :, :, of:of + w], sin[:, :, :, to:to + w], ALU.mult))
                do(V.tensor_tensor(x, tmp[0], tmp[1], ALU.add), st_normed)

            def turn(l, n, part):
                i = trans_ix.at[(l, n, part)]
                dve.wait_ge(t_hi, 3 * l + {"cq": 0, "ckv": 2}[n] + part + 1)
                if n == "cq":
                    do(V.tensor_tensor(cqT_lo[:, part, :], trans_view(i, NTOK), f32(cqT_hi[:, part, :]),
                                       ALU.subtract), t_dve)
                else:
                    do(V.tensor_tensor(ckvT_lo[:, :], trans_view(i, NTOK + PAST), f32(ckvT_hi[:, :]),
                                       ALU.subtract), t_dve)

            def attention(l, kind_list):
                todo = [(pair_at[(l, *p)], p) for kind in kind_list for p in attention_pairs(kind)]

                def maxima(i, pair):
                    kind, b, hp = pair
                    s = scores(i, pair)
                    if kind == "C":
                        for h in range(2):
                            dve.wait_ge(scored, signals(i, h))
                            do(V.tensor_reduce(mx[:, i % 2, h:h + 1], s[:, h, :], AX_X, ALU.max))
                            do(V.tensor_scalar(nb[:, i % 2, h:h + 1], mx[:, i % 2, h:h + 1], -SCALE_C, None, ALU.mult),
                               max_ready)
                        return
                    dve.wait_ge(scored, signals(i))
                    if kind == "A" and b is not None:
                        if b:
                            dve.wait_ge(table_ready, 3 * l + b)
                        v = s[:, :, 0:256]
                        table = a_table[b % 2][:, 2 * hp:2 * hp + 2, :, :].rearrange("p h r c -> p h (r c)")
                        do(V.tensor_tensor(v, v, table, ALU.add))
                    if kind == "D" and b is not None:
                        lo = max(b - 1, 0)
                        for blk, m in ((b - 1, 0), (b + 1, 1)):
                            if 0 <= blk < 4:
                                v = s[:, :, P * (blk - lo):P * (blk - lo) + P]
                                do(V.tensor_tensor(v, v, band[:, m, :].unsqueeze(1).broadcast_to([P, 2, P]), ALU.add))
                    do(V.tensor_reduce(mx[:, i % 2, :], s, AX_X, ALU.max))
                    if kind == "A":
                        do(V.tensor_scalar(nb[:, i % 2, :], mx[:, i % 2, :], -SCALE, None, ALU.mult), max_ready)
                    else:
                        sink = gains[:, GAIN_AT["swa_sink"] + 2 * hp:GAIN_AT["swa_sink"] + 2 * hp + 2]
                        do(V.scalar_tensor_tensor(mx[:, i % 2, :], mx[:, i % 2, :], SCALE, sink, ALU.mult, ALU.max))
                        do(V.tensor_scalar(nb[:, i % 2, :], mx[:, i % 2, :], -1.0, None, ALU.mult))
                        do(V.tensor_tensor(sink_e[:, i % 2, :], sink, mx[:, i % 2, :], ALU.subtract), max_ready)

                def reciprocals(i, pair):
                    dve.wait_ge(exp_done, signals(i))
                    if pair[0] == "D":
                        do(V.tensor_tensor(lsum[:, i % 2, :], lsum[:, i % 2, :], sink_e[:, i % 2, :], ALU.add))
                    do(V.reciprocal(rinv[:, i % 2, :], lsum[:, i % 2, :]), rinv_ready)

                def take_out(i, pair):
                    dve.wait_ge(mix_hi, i + 1)
                    dst, src = mixed_at(l, pair)
                    do(V.tensor_tensor(dst[1], src, f32(dst[0]), ALU.subtract), mix_lo)

                for j in range(len(todo) + 4):
                    if j >= 4:
                        take_out(*todo[j - 4])
                    if kind_list == "AD" and j == 1:
                        split_lo(45 * l + 9)
                    if kind_list == "C" and 1 <= j < len(todo) + 1:
                        reciprocals(*todo[j - 1])
                    if j < len(todo):
                        maxima(*todo[j])
                    if kind_list == "AD" and 1 <= j < len(todo) + 1:
                        reciprocals(*todo[j - 1])
                    if kind_list == "AD" and j + 5 < in_attention(l):
                        ada_tick(48 * l + 32, j + 5)

            def add_gated(d, gate, v, sem):
                x = xT[:, d, :]
                for m, dst, src in ((0, x[:, 0:CTX], v[:, 0, 0:CTX]), (1, x[:, CTX:HALF], v[:, 0, CTX:HALF]),
                                    (1, x[:, HALF:NTOK], v[:, 1, :])):
                    last = dst.shape[1] == HALF
                    do(V.scalar_tensor_tensor(dst, src, gate[:, m:m + 1], dst, ALU.mult, ALU.add),
                       sem if last else None)

            dve.wait_ge(cond_exp, 1)
            dve.wait_ge(consts_set, 1)
            do(V.tensor_scalar(cexp[:, :], cexp[:, :], 1.0, None, ALU.add))
            do(V.reciprocal(cexp[:, :], cexp[:, :]))
            do(V.tensor_tensor(cond[:, :, 0:2].rearrange("p k m -> p m k"),
                               vcol[:, 0, R_C:NVEC].rearrange("p (m k) -> p m k", m=2),
                               cexp[:, :].rearrange("p (m k) -> p m k", m=2), ALU.mult), cond_ready)
            do(V.memset(hstat[:, :], 1.0))
            for c in range(KC):
                add_square(0, c)
            ada_ticks(0, range(6))
            mean(0)
            ada_ticks(0, range(6, 14))
            split_lo(0)
            ada_ticks(0, range(14, 18))
            dve.wait_ge(const_dma, 64)

            for l in range(DEPTH):
                U = 45 * l
                if l:
                    mean(2 * l)
                late = 48 * l + 16
                ada_ticks(late, late_ticks(l, 0))
                h_of(2 * l)
                dve.wait_ge(gain_dma, 16 * len(GAINS) * (l + 1))
                dve.wait_ge(cache_dma, 64 * (l + 1))
                split_lo(U + 1)
                split_lo(U + 2)
                ada_ticks(late, late_ticks(l, 1))
                norm(l, "cq")
                turn(l, "cq", 0)
                turn(l, "cq", 1)
                norm(l, "ckv")
                ada_ticks(late, late_ticks(l, 2))
                turn(l, "ckv", 0)
                do(V.tensor_copy(k_st[:, 0:NT, :, NOPE:QK],
                                 ckv_st[:, :, KV_RANK:KV_RANK + ROPE].unsqueeze(2).broadcast_to([P, NT, 4, ROPE])))
                do(V.tensor_copy(k_st[:, NT, :, NOPE:QK],
                                 cache_in[:, 128:160].unsqueeze(1).broadcast_to([P, 4, ROPE])))
                split_lo(U + 3)
                norm(l, "q")
                ada_ticks(late, late_ticks(l, 3))
                norm(l, "k")
                ada_ticks(late, late_ticks(l, 4))
                attention(l, "C")
                split_lo(U + 4)
                split_lo(U + 5)
                norm(l, "naq")
                split_lo(U + 6)
                norm(l, "nak")
                split_lo(U + 7)
                split_lo(U + 8)
                norm(l, "swq")
                norm(l, "swkv")
                dve.wait_ge(m_act, acc_ix.last_reader(acc_ix.at[(l, "pool", 1)])[1])
                window_sums(do, dve, l, 1, pool_s[:, 0, :], pool_s[:, 1, :], pool_rc)
                dve.wait_ge(bias_dma, 16 * ROWS * (l + 1))
                do(V.tensor_scalar(a_bias[:, :, :, :], a_bias[:, :, :, :], 1.0 / SCALE, None, ALU.mult), bias_scaled)
                build_table(do, dve, 0, None)
                ada_ticks(48 * l + 32, range(5))
                for c in range(2):
                    i = acc_ix.at[(l, "mix", c)]
                    dve.wait_ge(mixp_hi, 2 * l + c + 1)
                    do(V.scalar_tensor_tensor(h_lo[:, 2 + c, :].rearrange("p (a n) -> p a n", a=2), acc_view(i),
                                              vcol[:, l, R_PS + c:R_PS + c + 1],
                                              f32(h_hi[:, 2 + c, :]).rearrange("p (a n) -> p a n", a=2),
                                              ALU.mult, ALU.subtract), m_dve)
                attention(l, "AD")
                for j in range(4):
                    split_lo(U + 9 + j + 1)
                    for d in (2 * j, 2 * j + 1):
                        i = acc_ix.at[(l, "wo", d)]
                        if d:
                            add_square(2 * l + 1, d - 1)
                        dve.wait_ge(m_done, i + 1)
                        add_gated(d, mod[:, l % 2, GATE1 + d, :], acc_view(i), m_dve)
                mean(2 * l + 1)
                more = l + 1 < DEPTH
                ada_ticks(48 * l + 32, range(in_attention(l), 20))
                h_of(2 * l + 1, {0: lambda: ada_ticks(48 * (l + 1), range(6 * more)),
                                 2: lambda: ada_ticks(48 * (l + 1), range(6 * more, 10 * more)),
                                 5: lambda: ada_ticks(48 * (l + 1), range(10 * more, 14 * more))})
                ada_ticks(48 * (l + 1), range(14 * more, 17 * more))
                for n in range(13, 45):
                    if n == 14 and more:
                        ada_tick(48 * (l + 1), 17)
                    u = units[U + n]
                    g = u[2]
                    gg = l * GROUPS + g
                    if u[1] == "w1":
                        split_lo(U + n + 1)
                        for c in (2 * u[3], 2 * u[3] + 1):
                            dve.wait_ge(m_act, acc_ix.last_reader(acc_ix.at[(l, "z", g, c)])[1])
                            do(V.tensor_tensor(z_sq[:, c % 2, :], z_relu[:, c % 2, :], z_relu[:, c % 2, :],
                                               ALU.mult), z_sq_ready)
                            dve.wait_ge(z_hi_ready, gg * GC + c + 1)
                            slot = GC * (g % 2) + c
                            do(V.tensor_tensor(z_lo[:, slot, :], z_sq[:, c % 2, :], f32(z_hi[:, slot, :]),
                                               ALU.subtract), z_lo_ready)
                    else:
                        for d in range(4 * u[3], 4 * u[3] + 4):
                            if g == GROUPS - 1 and l + 1 < DEPTH:
                                for c in {5: (1, 2), 6: (3, 4), 7: (5, 6)}.get(d, ()):
                                    add_square(2 * (l + 1), c)
                            dve.wait_ge(y_done, gg * KC + d + 1)
                            b = 4 + 2 * (d % 2)
                            v = ps[:, 512 * b:512 * b + 1024].rearrange("p (a n) -> p a n", a=2)[:, :, 0:HALF]
                            add_gated(d, mod[:, l % 2, GATE2 + d, :], v, y_read)
                            if d % 4 == 0:
                                split_lo(U + n + 1)

        @block.tensor
        def _(pe):
            M = nc.tensor
            did = {"p": 0, "t": 0, "m": 0, "y": 0, "ada": 0, "pair": 0}

            def quiet():
                if did["p"]:
                    pe.wait_ge(p_read, did["p"])
                for n, ix, by_act, by_dve in (("t", trans_ix, t_act, t_dve), ("m", acc_ix, m_act, m_dve)):
                    for who, s in (("act", by_act), ("dve", by_dve)):
                        count = sum(x[-1] == who for x in ix.steps[:did[n]])
                        if count:
                            pe.wait_ge(s, count)
                if did["y"]:
                    pe.wait_ge(y_read, did["y"])
                if did["ada"]:
                    pe.wait_ge(ada_rows, did["ada"] // 4)
                if did["pair"]:
                    pe.wait_ge(pt_ready, did["pair"])
                    pe.wait_ge(mix_lo, did["pair"])

            def wait_read(ix, i, by_act, by_dve):
                who, count = ix.last_reader(i)
                pe.wait_ge(by_act if who == "act" else by_dve, count)

            def transpose_step(key, pieces):
                i = trans_ix.at[key]
                assert i == did["t"], (key, i, did)
                if i >= 2:
                    wait_read(trans_ix, i - 2, t_act, t_dve)
                v = trans_view(i, 1024)
                for src, c in pieces:
                    last = M.transpose(v[0:src.shape[1], c:c + src.shape[0]], src,
                                       ident[0:src.shape[0], 0:src.shape[0]])
                last.then_inc(t_done, 1)
                did["t"] += 1

            def begin_acc(key):
                i = acc_ix.at[key]
                assert i == did["m"], (key, i, did)
                before = [j for j in range(i) if acc_banks(j) == acc_banks(i)]
                if before:
                    wait_read(acc_ix, before[-1], m_act, m_dve)
                did["m"] += 1
                return acc_view(i)

            def three(out, w_pair, x_pair, first, last):
                w, wl = w_pair
                x, xl = x_pair
                for n, (lhs, rhs) in enumerate(((w, x), (w, xl), (wl, x))):
                    for a_ in range(2):
                        ins = M.matmul(out[:, a_, :], lhs, rhs[:, HALF * a_:HALF * a_ + HALF],
                                       start=first and n == 0, stop=last and n == 2)
                return ins

            def ada_tick(first, k):
                turned, unit = ada_ticks_of(first)[k]
                b_acc, b_turn = ada_banks(first)
                if turned:
                    q = first // 4 + turned[1]
                    pe.wait_ge(ada_rows, q + 1)
                    if q:
                        pe.wait_ge(ada_reduced, q)
                    for j in range(4):
                        last = M.transpose(bank(b_turn)[:, P * j:P * j + P], ada_row[:, P * j:P * j + P], ident[:, :])
                    last.then_inc(ada_turned, 1)
                if unit:
                    u = first + unit[1]
                    wait_ada(pe, u)
                    if u % 4 == 0 and u:
                        pe.wait_ge(ada_rows, u // 4)
                        if b_acc == b_turn and unit[1]:
                            pe.wait_ge(ada_reduced, u // 4)
                    c = 512 * b_acc + AC * (u % 4 // 2)
                    for j in range(AR):
                        last = M.matmul(ps[32 * j:32 * j + 32, c:c + AC], cond[:, AR * (u % 2) + j, :],
                                        ada_slots[ada_place(u)][:, j, :], start=u % 2 == 0, stop=u % 2 == 1,
                                        skip_group_check=True)
                    last.then_inc(ada_used, 1)
                    did["ada"] += 1

            def ada_ticks(first, ks):
                for k in ks:
                    ada_tick(first, k)

            def sums(l, which):
                nrm = 2 * l + (which == "sum2")
                out = begin_acc((l, which))
                for x, ready, count in ((rstd[:, :], sum_used, (KC - 2) * (nrm + 1)),
                                        (sq[:, (KC - 1) % 2, :], sq_ready, KC * (nrm + 1))):
                    pe.wait_ge(ready, count)
                    for a_ in range(2):
                        last = M.matmul(out[:, a_, :], ones[:, :], x[:, HALF * a_:HALF * a_ + HALF],
                                        start=ready is sum_used, stop=ready is sq_ready)
                last.then_inc(m_done, 1)

            def project(l, n, name, tiles=range(NT), wait_h=None):
                s = n % 2
                pe.wait_ge(w_lo_ready, n + 1)
                for t in tiles:
                    i = proj_at[(l, name, t)]
                    assert i == did["p"]
                    if i >= 2:
                        pe.wait_ge(p_read, i - 1)
                    tok = slice(P * t, P * t + P)
                    if name == "uq":
                        w = [x[:, s, 0:768].rearrange("p (k c) -> p k c", k=2) for x in (w_hi, w_lo)]
                        x, cols, kk = (cqT_hi[:, :, tok], cqT_lo[:, :, tok]), 4 * QK, 2
                    elif name == "ukv":
                        w = [x[:, s, 768:1280].rearrange("p (k c) -> p k c", k=1) for x in (w_hi, w_lo)]
                        x = [y[:, tok].unsqueeze(1) for y in (ckvT_hi, ckvT_lo)]
                        cols, kk = 512, 1
                    else:
                        w = [x[:, s, :].rearrange("p (k c) -> p k c", k=KC) for x in (w_hi, w_lo)]
                        x, cols, kk = (h_hi[:, :, tok], h_lo[:, :, tok]), UW, KC
                    for k in range(kk):
                        if wait_h is not None and t == 0:
                            pe.wait_ge(h_lo_ready, wait_h + k + 1)
                        for q, (p, r) in enumerate(((0, 0), (1, 0), (0, 1))):
                            last = M.matmul(bank(i % 2)[:, 0:cols], x[p][:, k, :], w[r][:, k, :],
                                            start=k == 0 and q == 0, stop=k == kk - 1 and q == 2)
                    last.then_inc(p_done, 1)
                    did["p"] += 1

            def attention(l, kind_list, before_turn):
                todo = [(pair_at[(l, *p)], p) for kind in kind_list for p in attention_pairs(kind)]

                def score(i, pair):
                    kind, b, hp = pair
                    if kind != "C" and i - 2 >= todo[0][0]:
                        pe.wait_ge(exp_done, signals(i - 2))
                    out = scores(i, pair)
                    for h in range(2):
                        if kind == "C" and i > todo[0][0]:
                            pe.wait_ge(exp_done, signals(i - 1, h))
                        head = 2 * hp + h
                        q = slice(0, P) if b is None else slice(CTX + P * b, CTX + P * b + P)
                        if kind == "C":
                            keys = [(0, c_k[0:QK, head, 0:P])] if b is None else \
                                [(0, c_k[0:QK, head, CTX:CTX + 512]), (512, c_k[0:QK, head, CTX + 512:CTX + 640])]
                            lhs = c_q[0:QK, head, q]
                        elif kind == "A":
                            lhs = a_q[:, head, q]
                            keys = [(0, a_k[:, hp, 0:P])]
                            if b is not None:
                                s = KEY_START[b]
                                loc = a_k[:, hp, CTX:NTOK].rearrange("p (r c) -> p r c", r=ROWS)[:, :, s:s + KCOLS]
                                keys = [(0, loc), (256, a_k[:, hp, NTOK:NTOK + PAST])]
                        else:
                            lhs = d_q[:, head, q]
                            keys = [(0, d_k[:, 0:P])]
                            if b is not None:
                                s, e = CTX + P * max(b - 1, 0), CTX + P * min(b + 2, 4)
                                keys = [(0, d_k[:, s:e]), (e - s, d_k[:, NTOK:NTOK + PAST])]
                        for n, (c, rhs) in enumerate(keys):
                            width = int(np.prod(rhs.shape[1:]))
                            dst = out[:, h, c:c + width]
                            if len(rhs.shape) == 3:
                                dst = dst.rearrange("p (r c) -> p r c", r=ROWS)
                            last = M.matmul(dst, lhs, rhs, start=True, stop=True, skip_group_check=True)
                        if h or kind == "C":
                            last.then_inc(scored, 1)

                def turn(i, pair):
                    pe.wait_ge(p_normed, i + 1)
                    if i > todo[0][0]:
                        pe.wait_ge(pt_ready, i)
                    for h in range(2):
                        for j in range(keys_of(pair[0], pair[1])):
                            c = 2048 + 512 * h + P * j if j < 4 else 3072 + P * h
                            last = M.transpose(ps[:, c:c + P], probs(i, pair)[:, h, P * j:P * j + P], ident[:, :])
                    last.then_inc(turned, 1)

                def values(i, pair):
                    kind, b, hp = pair
                    pe.wait_ge(pt_ready, i + 1)
                    if i > todo[0][0]:
                        pe.wait_ge(mix_lo, i)
                    n = keys_of(kind, b)
                    for j in range(n):
                        for h in range(2):
                            head = 2 * hp + h
                            d = slice(HD * head, HD * head + HD)
                            if kind == "C":
                                v = c_v[:, 0 if b is None else 1 + j, d]
                            elif kind == "A":
                                v = a_vx[:, 0, d] if b is None else a_vx[:, 1, d] if j == 2 else a_v[:, b, j, d]
                            else:
                                d = slice(HD * hp, HD * hp + HD)
                                v = d_v[:, 0, d] if b is None else d_v[:, NT, d] if j == n - 1 \
                                    else d_v[:, 1 + max(b - 1, 0) + j, d]
                            last = M.matmul(ps[64 * h:64 * h + 64, 3584:3584 + P], v,
                                            probs_t(i, pair)[:, h, P * j:P * j + P], start=j == 0, stop=j == n - 1)
                    last.then_inc(pv_done, 1)

                for j in range(len(todo) + 3):
                    if j < len(todo):
                        score(*todo[j])
                    if kind_list == "AD" and j + 5 < in_attention(l):
                        ada_tick(48 * l + 32, j + 5)
                    if j in before_turn:
                        before_turn[j]()
                    if 2 <= j < len(todo) + 2:
                        turn(*todo[j - 2])
                    if j >= 3:
                        values(*todo[j - 3])
                did["pair"] += len(todo)

            def turn_result(c):
                pe.wait_ge(y_read, KC * (DEPTH * GROUPS - 1) + c + 1)
                transpose_step(("out", c), [(xT[:, c, P * t:P * t + P], P * t) for t in range(NT)])

            pe.wait_ge(consts_set, 1)
            pe.wait_ge(x_in_dma, 32)
            for c in range(KC):
                transpose_step(("x", c), [(x_in[:, t, P * c:P * c + P], P * t) for t in range(NT)])
            pe.wait_ge(vec_dma, 16 * 6 * DEPTH)
            for l in range(DEPTH):
                transpose_step(("vec", l), [(vec_in[0:NVEC, l, :], 0)])
            pe.wait_ge(cond_ready, 1)
            ada_ticks(0, range(8))
            sums(0, "sum1")
            ada_ticks(0, range(8, 18))

            for l in range(DEPTH):
                U = 45 * l
                if l:
                    sums(l, "sum1")
                    pe.wait_ge(y_read, did["y"])
                late = 48 * l + 16
                ada_ticks(late, late_ticks(l, 0))
                project(l, U, "cq", wait_h=2 * l * KC)
                ada_ticks(late, late_ticks(l, 1))
                project(l, U + 1, "ckv")
                pe.wait_ge(st_normed, norm_at(l, "cq") + 1)
                for c in range(2):
                    transpose_step((l, "cq", c), [(cq_st[:, t, P * c:P * c + P], P * t) for t in range(NT)])
                ada_ticks(late, late_ticks(l, 2))
                pe.wait_ge(st_normed, norm_at(l, "ckv") + 1)
                pe.wait_ge(cache_dma, 64 * (l + 1))
                transpose_step((l, "ckv", 0), [(ckv_st[:, t, 0:P], P * t) for t in range(NT)]
                               + [(cache_in[:, 0:P], NTOK)])
                pe.wait_ge(t_dve, 3 * l + 2)
                project(l, U + 2, "uq")
                pe.wait_ge(t_dve, 3 * l + 3)
                project(l, U + 2, "ukv", range(NT + 1))
                ada_ticks(late, late_ticks(l, 3))
                pe.wait_ge(st_normed, norm_at(l, "q") + 1)
                for h in range(4):
                    transpose_step((l, "q", h), [(q_st[:, t, QK * h:QK * h + QK], P * t) for t in range(NT)])
                ada_ticks(late, late_ticks(l, 4))
                project(l, U + 3, "naq", range(2))
                pe.wait_ge(st_normed, norm_at(l, "k") + 1)
                for h in range(4):
                    transpose_step((l, "k", h), [(k_st[:, t, h, :], P * t) for t in range(NT + 1)])
                quiet()
                def more_naq(t):
                    pe.wait_ge(exp_done, signals(pair_at[(l, "C", 3, 1)], 0))
                    project(l, U + 3, "naq", range(t, t + 1))

                attention(l, "C", {10: lambda: more_naq(2), 11: lambda: more_naq(3)})
                project(l, U + 3, "naq", range(4, NT))
                project(l, U + 4, "nak")
                pe.wait_ge(pt_ready, did["pair"])
                pe.wait_ge(mix_lo, did["pair"])
                pe.wait_ge(st_normed, norm_at(l, "naq") + 1)
                for hp in range(2):
                    transpose_step((l, "naq", hp), [(st[:, 0, t, P * hp:P * hp + P], P * t) for t in range(NT)])
                project(l, U + 5, "nav")
                pe.wait_ge(st_normed, norm_at(l, "nak") + 1)
                for hp in range(2):
                    transpose_step((l, "nak", hp), [(st[:, 1, t, P * hp:P * hp + P], P * t) for t in range(NT)]
                                   + [(cache_in[:, 160 + P * hp:160 + P * hp + P], NTOK)])
                project(l, U + 6, "swq")
                project(l, U + 7, "swkv")
                pe.wait_ge(p_read, did["p"])
                pe.wait_ge(w_lo_ready, U + 9)
                for c in range(2):
                    out = begin_acc((l, "pool", c))
                    w = [x[:, (U + 8) % 2, :].rearrange("p (k c) -> p k c", k=KC)[:, :, P * c:P * c + P] for x in (w_hi, w_lo)]
                    for k in range(KC):
                        last = three(out, (w[0][:, k, :], w[1][:, k, :]), (h_hi[:, k, :], h_lo[:, k, :]), k == 0, k == KC - 1)
                    last.then_inc(m_done, 1)
                    if c == 0:
                        pe.wait_ge(st_normed, norm_at(l, "swq") + 1)
                        for hp in range(2):
                            transpose_step((l, "swq", hp), [(st[:, 1, t, P * hp:P * hp + P], P * t) for t in range(NT)])
                pe.wait_ge(st_normed, norm_at(l, "swkv") + 1)
                transpose_step((l, "swk", 0), [(st[:, 0, t, 0:P], P * t) for t in range(NT)]
                               + [(cache_in[:, 416:544], NTOK)])
                pe.wait_ge(pool_w_dma, 64 * (l + 1))
                wait_read(trans_ix, trans_ix.at[(l, "swk", 0)], t_act, t_dve)
                ada_ticks(48 * l + 32, range(5))
                for c in range(2):
                    pe.wait_ge(pool_ready[c], l + 1)
                    out = begin_acc((l, "mix", c))
                    lat = PAD + CTX + 2 * PAD
                    cut = lat + HALF - CTX
                    M.matmul(out[:, 0, 0:CTX], pool_w[:, c, :], pool_in[:, c, PAD:PAD + CTX], start=True, stop=True)
                    M.matmul(out[:, 0, CTX:HALF], pool_w[:, c, :], pool_in[:, c, lat:cut], start=True, stop=True)
                    M.matmul(out[:, 1, :], pool_w[:, c, :], pool_in[:, c, cut:lat + LAT], start=True, stop=True)\
                        .then_inc(m_done, 1)
                pe.wait_ge(pads_set, l + 1)
                pe.wait_ge(av_dma, 16 * 2 * NCB * (l + 1))
                pe.wait_ge(nav_dma, 32 * (l + 1))
                pe.wait_ge(ad_cache_dma, 32 * (l + 1))
                pe.wait_ge(dv_ready, l + 1)
                wait_read(acc_ix, acc_ix.at[(l, "mix", 0)], m_act, m_dve)

                def w_out(d, ks, order=(4, 5, 0, 1, 2, 3, 6, 7)):
                    n = U + 9 + d // 2
                    pe.wait_ge(w_lo_ready, n + 1)
                    w = [x[:, n % 2, :].rearrange("p (k c) -> p k c", k=KC) for x in (w_hi, w_lo)]
                    out = begin_acc((l, "wo", d)) if ks[0] == 0 else acc_view(acc_ix.at[(l, "wo", d)])
                    c = P * (d % 2)
                    for q in ks:
                        k = order[q]
                        last = three(out, (w[0][:, k, c:c + P], w[1][:, k, c:c + P]), (mixed(k, 0), mixed(k, 1)),
                                     q == 0, q == KC - 1)
                    if ks[-1] == KC - 1:
                        last.then_inc(m_done, 1)

                def first_w_out():
                    pe.wait_ge(mix_lo, pair_at[(l, "A", 3, 1)] + 1)
                    pe.wait_ge(exp_done, signals(pair_at[(l, "D", 3, 0)]))
                    w_out(0, range(6))

                attention(l, "AD", {2: lambda: wait_read(acc_ix, acc_ix.at[(l, "mix", 1)], m_act, m_dve),
                                    20: first_w_out})
                pe.wait_ge(exp_done, signals(pair_at[(l, "D", 3, 1)]))
                pe.wait_ge(mix_lo, did["pair"])
                w_out(0, (6, 7))
                for d in range(1, KC):
                    w_out(d, range(KC))
                sums(l, "sum2")
                ada_ticks(48 * l + 32, range(in_attention(l), 20))
                if l + 1 < DEPTH:
                    ada_ticks(48 * (l + 1), range(17))
                for n in range(13, 45):
                    if n == 14 and l + 1 < DEPTH:
                        ada_tick(48 * (l + 1), 17)
                    u = units[U + n]
                    s = (U + n) % 2
                    g, j = u[2], u[3]
                    gg = l * GROUPS + g
                    pe.wait_ge(w_lo_ready, U + n + 1)
                    if u[1] == "w1":
                        w = [x[:, s, :].rearrange("p (k c) -> p k c", k=KC) for x in (w_hi, w_lo)]
                        for cc in range(2):
                            out = begin_acc((l, "z", g, 2 * j + cc))
                            c = P * cc
                            for k in range(KC):
                                if (g, j, cc) == (0, 0, 0):
                                    pe.wait_ge(h_lo_ready, (2 * l + 1) * KC + k + 1)
                                last = three(out, (w[0][:, k, c:c + P], w[1][:, k, c:c + P]),
                                             (h_hi[:, k, :], h_lo[:, k, :]), k == 0, k == KC - 1)
                            last.then_inc(m_done, 1)
                    else:
                        w = [x[:, s, :].rearrange("p (k c) -> p k c", k=GC) for x in (w_hi, w_lo)]
                        pe.wait_ge(z_lo_ready, (gg + 1) * GC)
                        for dd in range(4):
                            d = 4 * j + dd
                            i = gg * KC + d
                            assert i == did["y"]
                            if i >= 2:
                                pe.wait_ge(y_read, i - 1)
                            b = 4 + 2 * (d % 2)
                            out = ps[:, 512 * b:512 * b + 1024].rearrange("p (a n) -> p a n", a=2)[:, :, 0:HALF]
                            c = P * dd
                            for k in range(GC):
                                slot = GC * (g % 2) + k
                                last = three(out, (w[0][:, k, c:c + P], w[1][:, k, c:c + P]),
                                             (z_hi[:, slot, :], z_lo[:, slot, :]), k == 0, k == GC - 1)
                            last.then_inc(y_done, 1)
                            did["y"] += 1
                            if l == DEPTH - 1 and g == GROUPS - 1 and d:
                                turn_result(d - 1)
            turn_result(KC - 1)


def constants():
    t = np.arange(LAT)
    pos = (t // GRID_W, t % GRID_W)
    out = {}
    for name, width in (("rope_d", HD), ("rope_c", ROPE)):
        quarter = width // 4
        freqs = (THETA ** (-np.arange(quarter, dtype=np.float32) / np.float32(quarter))).astype(np.float32)
        tab = np.zeros((2, LAT, 2, 2, quarter), np.float32)
        for half in range(2):
            ang = pos[half].astype(np.float32)[:, None] * freqs
            tab[0, :, half, :, :] = np.cos(ang)[:, None, :]
            tab[1, :, half, 0, :] = -np.sin(ang)
            tab[1, :, half, 1, :] = np.sin(ang)
        out[name] = np.ascontiguousarray(tab.reshape(2, 4, P, width).transpose(2, 0, 1, 3))
    q, k = np.arange(P)[:, None], np.arange(P)[None, :]
    out["band"] = np.ascontiguousarray(np.stack([np.where(k >= q, 0, NEG), np.where(k <= q, 0, NEG)], 1).astype(np.float32))
    cols = np.zeros((P, 3, KCOLS), np.float32)
    for i, b in enumerate((0, 1, 3)):
        qcol = QC * b + np.arange(P) % QC
        start = np.clip(qcol - 8, 0, GRID_W - 16)[:, None]
        kcol = KEY_START[b] + np.arange(KCOLS)[None, :]
        cols[:, i] = np.where((kcol >= start) & (kcol < start + 16), 0, NEG)
    out["col_mask"] = cols
    rc = np.zeros((2, P, SEG), np.float32)
    for gi, w in enumerate(POOL_WINDOWS):
        for n, at in ((CTX, PAD), (LAT, PAD + CTX + 2 * PAD)):
            i = np.arange(n)
            count = np.clip(i - w // 2 + w, 0, n) - np.clip(i - w // 2, 0, n)
            rc[gi // 2, 64 * (gi % 2):64 * (gi % 2) + 64, at:at + n] = 1.0 / count.astype(np.float32)
    out["pool_rc"] = rc
    return out


_INS = ["x_prompt", "x_sample", "cache_na_k", "cache_na_v", "cache_mla_ckv", "cache_mla_kpe", "cache_swa_k",
        "cache_swa_v", "c", "c_ctx", "norm1", "norm2", "w_ada", "b_ada", "w_in", "w_out", "na_q_norm", "na_k_norm",
        "na_rpb", "pool_w", "pool_scale", "mla_q_a_norm", "mla_w_uq", "mla_kv_norm", "mla_w_ukv", "mla_q_norm",
        "mla_k_norm", "swa_q_norm", "swa_k_norm", "swa_sink", "mlp_w1", "mlp_w2"]
_OUTS = {"y_prompt": (1, CTX, D), "y_sample": (1, LAT, D), "na_k_new": (1, DEPTH, CTX, 4, HD),
         "na_v_new": (1, DEPTH, CTX, 4, HD), "mla_ckv_new": (1, DEPTH, CTX, KV_RANK),
         "mla_kpe_new": (1, DEPTH, CTX, ROPE), "swa_k_new": (1, DEPTH, CTX, 2, HD), "swa_v_new": (1, DEPTH, CTX, 2, HD)}


def kernel(**inputs):
    import concourse.bacc as bacc
    from concourse.bass_utils import run_bass_kernel_spmd

    nc = bacc.Bacc("TRN2", target_bir_lowering=False, num_devices=1)
    arrays = {f"in_{n}": np.ascontiguousarray(inputs[n]) for n in _INS}
    arrays["in_na_rpb"] = np.ascontiguousarray(inputs["na_rpb"][:, :, ::-1, ::-1].transpose(0, 2, 1, 3))
    arrays.update({f"in_{n}": v for n, v in constants().items()})
    a = {n[3:]: nc.dram_tensor(n, v.shape, F32, kind="ExternalInput").ap() for n, v in arrays.items()}
    o = {n: nc.dram_tensor(f"out_{n}", s, F32, kind="ExternalOutput").ap() for n, s in _OUTS.items()}
    hybrid_kernel(nc, a, o)
    r = run_bass_kernel_spmd(nc, [arrays], core_ids=[0])
    return tuple(r.results[0][f"out_{n}"] for n in _OUTS)
```
